# Optimizing a Trainium2 kernel written in Bass

```python
import jax, jax.numpy as jnp
from jax import lax
import numpy as np

D_MODEL = 1024
BATCH = 1
SEQ = 1024
DEPTH = 2

N_MIXERS = 2
N_CONV_LAYERS = (DEPTH + N_MIXERS - 1) // N_MIXERS
N_MLA_LAYERS = DEPTH // N_MIXERS
CONV_WIDTH = 3
N_HEADS = 8
Q_LORA_RANK = 384
KV_LORA_RANK = 256
QK_NOPE_DIM = 128
QK_ROPE_DIM = 64
QK_HEAD_DIM = QK_NOPE_DIM + QK_ROPE_DIM
V_HEAD_DIM = 128
LATENT_DIM = Q_LORA_RANK + KV_LORA_RANK + QK_ROPE_DIM
ROPE_THETA = 10000.0
Q_BLOCK = 128
N_GROUPS = 8
EXPERTS_PER_GROUP = 8
N_EXPERTS = N_GROUPS * EXPERTS_PER_GROUP
TOP_K = 2
D_FF_EXPERT = 384
MOE_BLOCK = 128
RMS_EPS = 1e-6
MAX_POS_OFFSET = 1024

kernel_name = 'hybrid_conv_mla_hier_moe_encoder'

def rms_norm(x, w):
    xf = x.astype(jnp.float32)
    y = xf * lax.rsqrt(jnp.mean(xf * xf, axis=-1, keepdims=True) + RMS_EPS)
    return (y * w.astype(jnp.float32)).astype(x.dtype)

def rope(x, cos, sin):
    half = x.shape[-1] // 2
    x1, x2 = x[..., :half], x[..., half:]
    return jnp.concatenate([x1 * cos - x2 * sin, x2 * cos + x1 * sin], axis=-1)

def short_conv_mixer(h, w_in, conv_k, w_out):
    bcu = h @ w_in
    gb, gc, u = jnp.split(bcu, 3, axis=-1)
    z = gc * u
    zp = jnp.pad(z, ((0, 0), (1, 1), (0, 0)))
    conv = zp[:, :-2] * conv_k[0] + zp[:, 1:-1] * conv_k[1] + zp[:, 2:] * conv_k[2]
    return (gb * conv) @ w_out

def mla_mixer(h, cos, sin, w_down, q_lat_norm, kv_lat_norm, w_q_up, w_kv_up,
              q_head_norm, k_head_norm, w_out):
    b, s, _ = h.shape
    lat = h @ w_down
    q_lat = rms_norm(lat[..., :Q_LORA_RANK], q_lat_norm)
    kv_lat = rms_norm(lat[..., Q_LORA_RANK:Q_LORA_RANK + KV_LORA_RANK], kv_lat_norm)
    k_rope = lat[..., Q_LORA_RANK + KV_LORA_RANK:]
    q = (q_lat @ w_q_up).reshape(b, s, N_HEADS, QK_HEAD_DIM)
    kv = (kv_lat @ w_kv_up).reshape(b, s, N_HEADS, QK_NOPE_DIM + V_HEAD_DIM)
    k_nope, v = kv[..., :QK_NOPE_DIM], kv[..., QK_NOPE_DIM:]
    k = jnp.concatenate(
        [k_nope, jnp.broadcast_to(k_rope[:, :, None, :], (b, s, N_HEADS, QK_ROPE_DIM))], axis=-1)
    q = rms_norm(q, q_head_norm)
    k = rms_norm(k, k_head_norm)
    q = jnp.concatenate([q[..., :QK_NOPE_DIM], rope(q[..., QK_NOPE_DIM:], cos, sin)], axis=-1)
    k = jnp.concatenate([k[..., :QK_NOPE_DIM], rope(k[..., QK_NOPE_DIM:], cos, sin)], axis=-1)
    scale = QK_HEAD_DIM ** -0.5
    n_qb = s // Q_BLOCK
    q_blocks = q.reshape(b, n_qb, Q_BLOCK, N_HEADS, QK_HEAD_DIM).transpose(1, 0, 2, 3, 4)

    def attend(qb):
        scores = jnp.einsum('bqhd,bkhd->bhqk', qb, k).astype(jnp.float32) * scale
        probs = jax.nn.softmax(scores, axis=-1).astype(v.dtype)
        return jnp.einsum('bhqk,bkhd->bqhd', probs, v)

    o = lax.map(attend, q_blocks)
    o = o.transpose(1, 0, 2, 3, 4).reshape(b, s, N_HEADS * V_HEAD_DIM)
    return o @ w_out

def hier_moe(h, w_group, b_group, w_expert, b_expert, w_gate, w_up, w_down):
    b, s, d = h.shape
    t = h.reshape(b * s, d)
    n_tok = b * s
    tok_ids = jnp.arange(n_tok)
    g_logits = (t @ w_group).astype(jnp.float32)
    g_prob = jax.nn.softmax(g_logits, axis=-1)
    g_sel = jnp.argmax(g_logits + b_group.astype(jnp.float32), axis=-1)
    g_gate = g_prob[tok_ids, g_sel]
    e_logits = (t @ w_expert).astype(jnp.float32).reshape(n_tok, N_GROUPS, EXPERTS_PER_GROUP)
    e_logits = e_logits[tok_ids, g_sel]
    e_bias = b_expert.astype(jnp.float32).reshape(N_GROUPS, EXPERTS_PER_GROUP)[g_sel]
    _, e_top = lax.top_k(e_logits + e_bias, TOP_K)
    e_prob = jnp.take_along_axis(jax.nn.softmax(e_logits, axis=-1), e_top, axis=-1)
    e_prob = e_prob / jnp.sum(e_prob, axis=-1, keepdims=True)
    gate = g_gate[:, None] * e_prob
    expert_id = g_sel[:, None] * EXPERTS_PER_GROUP + e_top
    n_assign = n_tok * TOP_K
    flat_e = expert_id.reshape(n_assign).astype(jnp.int32)
    flat_tok = jnp.repeat(tok_ids.astype(jnp.int32), TOP_K)
    flat_gate = gate.reshape(n_assign)
    order = jnp.argsort(flat_e)
    se, stok, sgate = flat_e[order], flat_tok[order], flat_gate[order]
    counts = jnp.bincount(flat_e, length=N_EXPERTS)
    starts = jnp.cumsum(counts) - counts
    padded = (counts + MOE_BLOCK - 1) // MOE_BLOCK * MOE_BLOCK
    pends = jnp.cumsum(padded)
    pstarts = pends - padded
    dest = pstarts[se] + (jnp.arange(n_assign) - starts[se])
    n_blocks = -(-n_assign // MOE_BLOCK) + N_EXPERTS
    n_rows = n_blocks * MOE_BLOCK
    buf_tok = jnp.zeros((n_rows,), jnp.int32).at[dest].set(stok)
    buf_gate = jnp.zeros((n_rows,), jnp.float32).at[dest].set(sgate)
    block_expert = jnp.minimum(
        jnp.searchsorted(pends, jnp.arange(n_blocks) * MOE_BLOCK, side='right'), N_EXPERTS - 1)
    xb = t[buf_tok].reshape(n_blocks, MOE_BLOCK, d)

    def run_block(args):
        xblk, e = args
        hid = jax.nn.silu(xblk @ w_gate[e]) * (xblk @ w_up[e])
        return hid @ w_down[e]

    yb = lax.map(run_block, (xb, block_expert)).reshape(n_rows, d)
    out = jnp.zeros((n_tok, d), h.dtype).at[buf_tok].add(yb * buf_gate[:, None].astype(yb.dtype))
    return out.reshape(b, s, d)

def setup_inputs(seed: int = 0) -> dict:
    key = jax.random.key(seed)
    ks = iter(jax.random.split(key, 32))
    f32 = jnp.float32

    def w(shape, fan_in):
        return jax.random.normal(next(ks), shape, f32) * (fan_in ** -0.5)

    def gain(shape):
        return 1.0 + 0.02 * jax.random.normal(next(ks), shape, f32)

    x = jax.random.normal(next(ks), (BATCH, SEQ, D_MODEL), f32)
    offsets = jax.random.randint(next(ks), (BATCH, 1), 0, MAX_POS_OFFSET, dtype=jnp.int32)
    positions = offsets + jnp.arange(SEQ, dtype=jnp.int32)[None, :]
    nc, nm, L = N_CONV_LAYERS, N_MLA_LAYERS, DEPTH
    return {
        'x': x,
        'positions': positions,
        'conv_norm_w': gain((nc, D_MODEL)),
        'conv_w_in': w((nc, D_MODEL, 3 * D_MODEL), D_MODEL),
        'conv_k': w((nc, CONV_WIDTH, D_MODEL), CONV_WIDTH),
        'conv_w_out': w((nc, D_MODEL, D_MODEL), D_MODEL),
        'mla_norm_w': gain((nm, D_MODEL)),
        'mla_w_down': w((nm, D_MODEL, LATENT_DIM), D_MODEL),
        'mla_q_lat_norm': gain((nm, Q_LORA_RANK)),
        'mla_kv_lat_norm': gain((nm, KV_LORA_RANK)),
        'mla_w_q_up': w((nm, Q_LORA_RANK, N_HEADS * QK_HEAD_DIM), Q_LORA_RANK),
        'mla_w_kv_up': w((nm, KV_LORA_RANK, N_HEADS * (QK_NOPE_DIM + V_HEAD_DIM)), KV_LORA_RANK),
        'mla_q_head_norm': gain((nm, QK_HEAD_DIM)),
        'mla_k_head_norm': gain((nm, QK_HEAD_DIM)),
        'mla_w_out': w((nm, N_HEADS * V_HEAD_DIM, D_MODEL), N_HEADS * V_HEAD_DIM),
        'ffn_norm_w': gain((L, D_MODEL)),
        'router_w_group': w((L, D_MODEL, N_GROUPS), D_MODEL),
        'router_b_group': 0.01 * jax.random.normal(next(ks), (L, N_GROUPS), f32),
        'router_w_expert': w((L, D_MODEL, N_EXPERTS), D_MODEL),
        'router_b_expert': 0.01 * jax.random.normal(next(ks), (L, N_EXPERTS), f32),
        'exp_w_gate': w((L, N_EXPERTS, D_MODEL, D_FF_EXPERT), D_MODEL),
        'exp_w_up': w((L, N_EXPERTS, D_MODEL, D_FF_EXPERT), D_MODEL),
        'exp_w_down': w((L, N_EXPERTS, D_FF_EXPERT, D_MODEL), D_FF_EXPERT),
    }

def reference(x, positions, conv_norm_w, conv_w_in, conv_k, conv_w_out,
              mla_norm_w, mla_w_down, mla_q_lat_norm, mla_kv_lat_norm, mla_w_q_up,
              mla_w_kv_up, mla_q_head_norm, mla_k_head_norm, mla_w_out,
              ffn_norm_w, router_w_group, router_b_group, router_w_expert, router_b_expert,
              exp_w_gate, exp_w_up, exp_w_down):
    inv_freq = ROPE_THETA ** (-jnp.arange(0, QK_ROPE_DIM, 2, dtype=jnp.float32) / QK_ROPE_DIM)
    ang = positions.astype(jnp.float32)[..., None] * inv_freq
    cos = jnp.cos(ang)[:, :, None, :].astype(x.dtype)
    sin = jnp.sin(ang)[:, :, None, :].astype(x.dtype)
    for i in range(DEPTH):
        j = i // N_MIXERS
        if i % N_MIXERS == 0:
            h = rms_norm(x, conv_norm_w[j])
            x = x + short_conv_mixer(h, conv_w_in[j], conv_k[j], conv_w_out[j])
        else:
            h = rms_norm(x, mla_norm_w[j])
            x = x + mla_mixer(h, cos, sin, mla_w_down[j], mla_q_lat_norm[j], mla_kv_lat_norm[j],
                              mla_w_q_up[j], mla_w_kv_up[j], mla_q_head_norm[j],
                              mla_k_head_norm[j], mla_w_out[j])
        h = rms_norm(x, ffn_norm_w[i])
        x = x + hier_moe(h, router_w_group[i], router_b_group[i], router_w_expert[i],
                         router_b_expert[i], exp_w_gate[i], exp_w_up[i], exp_w_down[i])
    return x


_drawn_inputs = setup_inputs


def setup_inputs(seed=0):
    import zlib

    import numpy as np

    out = dict(_drawn_inputs(seed))
    spreads = {}
    factors = {'mla_norm_w': 8.0,
     'mla_q_lat_norm': 8.0,
     'mla_kv_lat_norm': 8.0,
     'mla_q_head_norm': 8.0,
     'mla_k_head_norm': 8.0,
     'router_b_group': 5.728,
     'router_b_expert': 4.174}
    for name, (base, spread) in spreads.items():
        noise = np.random.default_rng([zlib.crc32(name.encode()), seed]).standard_normal(out[name].shape)
        drawn = base * np.exp(spread * noise) if base else spread * noise
        out[name] = __import__('jax').numpy.asarray(drawn.astype(out[name].dtype))
    for name, factor in factors.items():
        out[name] = (out[name] * factor).astype(out[name].dtype)
    return out
```

```python
from contextlib import ExitStack

import numpy as np

import concourse.bass as bass
from concourse import mybir

F32 = mybir.dt.float32
I32 = mybir.dt.int32
ALU = mybir.AluOpType
ACT = mybir.ActivationFunctionType
X = mybir.AxisListType.X

P = 128
D, S = 1024, 1024
KD = D // P
NT = S // P
EPS = 1e-6
BANK = 512
NE, NG, EG = 64, 8, 8
NL = NG + NE
FF = 384
KF = FF // P
RANKS = 64
MAXR = 2 * S // RANKS
NH, NOPE, ROPE, VD = 8, 128, 64, 128
QD = NOPE + ROPE
QL, KVL = 384, 256
LAT = QL + KVL + ROPE
KQ, KKV = QL // P, KVL // P
AHEAD = 2


def wait(eng, sem, value):
    if isinstance(value, int) and value <= 0:
        return
    eng.wait_ge(sem, value)


class Chain:

    def __init__(self, eng, sem):
        self.eng, self.sem, self.base, self.n = eng, sem, 0, 0

    def at(self, base):
        self.base, self.n = base, 0

    def mark(self, ins):
        ins.then_inc(self.sem, 1)
        self.n += 1

    def sync(self, ins=None):
        if ins is not None:
            self.mark(ins)
        self.eng.wait_ge(self.sem, self.base + self.n)


class Core:

    def __init__(self, nc, ins, out, ctx):
        self.nc, self.ins, self.out = nc, ins, out

        def sb(name, shape, dt=F32):
            return ctx.enter_context(nc.sbuf_tensor(name, shape, dt))

        self.x = sb("x", [P, NT, D])
        self.hT = sb("hT", [P, KD, S])
        self.rows = sb("rows", [P, 4, D])
        self.turned = sb("turned", [P, 2, KD, P])
        self.logits = sb("logits", [P, NT, NL])
        self.w_router = sb("w_router", [P, KD, NL])
        self.ident = sb("ident", [P, P])
        self.before = sb("before", [P, P])
        self.ones = sb("ones", [P, P])
        self.rank_of_col = sb("rank_of_col", [P, 2, RANKS])
        self.code = sb("code", [P, 2, NT])
        self.from_last = sb("from_last", [P, EG])
        self.round_start = sb("round_start", [P, MAXR])
        self.upper_half = sb("upper_half", [P, 1])
        self.minus_half = sb("minus_half", [P, 2])
        self.sumsq = sb("sumsq", [P, NT])
        self.var = sb("var", [P, NT])
        self.rstd = sb("rstd", [P, NT])
        self.norm_w = sb("norm_w", [P, 4, KD])
        self.xw = sb("xw", [P, 2, 4, 2])
        self.gather_idx = sb("gather_idx", [P, NE], I32)
        self.scatter_idx = sb("scatter_idx", [P, NE], I32)
        self.col_idx = sb("col_idx", [P, 4, 1], I32)
        self.n_rounds = sb("n_rounds", [P, 1], I32)
        self.pos_i = sb("pos_i", [P, NT], I32)
        self.arena_words = 28600
        self.arena = sb("arena", [P, self.arena_words])
        self.ps = ctx.enter_context(nc.psum_tensor("ps", [P, 8, BANK], F32))
        self.h_rows = nc.dram_tensor("h_rows", [S, D], F32, kind="Internal").ap()
        self.y_rows = nc.dram_tensor("y_rows", [2 * S, D], F32, kind="Internal").ap()

    def carve(self, place=None):
        at = [0]
        place = self.arena[:, :] if place is None else place
        words = place.shape[1]

        def piece(*shape):
            n = int(np.prod(shape))
            a = place[:, at[0]:at[0] + n]
            at[0] += n
            assert at[0] <= words, (at[0], words)
            if len(shape) == 2:
                a = a.rearrange("p (a b) -> p a b", b=shape[1])
            elif len(shape) == 3:
                a = a.rearrange("p (a b c) -> p a b c", b=shape[1], c=shape[2])
            elif len(shape) == 4:
                a = a.rearrange("p (a b c d) -> p a b c d", b=shape[1], c=shape[2], d=shape[3])
            return a

        piece.at = at
        return piece


def bc(ap, axis, n):
    a = ap.unsqueeze(axis)
    shape = list(a.shape)
    shape[axis] = n
    return a.broadcast_to(shape)


class Sems:

    def __init__(self, nc, tag):
        self.nc, self.tag, self.all = nc, tag, []

    def __call__(self, name):
        s = self.nc.alloc_semaphore(f"{self.tag}_{name}")
        self.all.append(s)
        return s

    def clear(self):
        self.nc.clear_and_free_semaphores(self.all)
        self.nc.all_engine_barrier()


class Norm:

    def __init__(self, c, sems, which, route, banks, logit_bank=None):
        self.c, self.w, self.route, self.banks, self.logit_bank = c, which, route, banks, logit_bank
        named = sems

        def sems(name):
            return named(f"{name}_{which}")

        self.squares = sems("norm_squares")
        self.var_ready = sems("norm_var_ready")
        self.rstd_ready = sems("norm_rstd_ready")
        self.rows_ready = sems("norm_rows_ready")
        self.turns = sems("norm_turns")
        self.evacuated = sems("norm_evacuated")
        self.scaled = self.evacuated
        if route:
            self.logits_ready = sems("norm_logits_ready")
            self.logits_copied = sems("norm_logits_copied")
            self.rows_stored = [sems(f"norm_rows_stored{i}") for i in range(4)]

    def act_squares(self, act, t):
        c = self.c
        if t >= 4:
            act.wait_ge(self.turns, 2 * (t - 3))
            if self.route:
                act.wait_ge(self.rows_stored[t % 4], 16 * (t // 4))
        act.activation(c.rows[:, t % 4, :], c.x[:, t, :], ACT.Square,
                       accum_out=c.sumsq[:, t:t + 1]).then_inc(self.squares, 1)

    def dve_var(self, dve, t):
        c = self.c
        dve.wait_ge(self.squares, t + 1)
        dve.tensor_scalar(c.var[:, t:t + 1], c.sumsq[:, t:t + 1], 1.0 / D, EPS,
                          ALU.mult, ALU.add).then_inc(self.var_ready, 1)

    def pool_rstd(self, pool, t):
        c = self.c
        pool.wait_ge(self.var_ready, t + 1)
        pool.tensor_tensor(c.rstd[:, t:t + 1], c.var[:, t:t + 1], c.minus_half[:, 0:1],
                           ALU.pow).then_inc(self.rstd_ready, 1)

    def act_rows(self, act, t):
        c = self.c
        act.wait_ge(self.rstd_ready, t + 1)
        act.activation(c.rows[:, t % 4, :], c.x[:, t, :], ACT.Copy,
                       scale=c.rstd[:, t:t + 1]).then_inc(self.rows_ready, 1)

    def sp_store(self, sp, t):
        c = self.c
        sp.wait_ge(self.rows_ready, t + 1)
        sp.dma_start(c.h_rows[t * P:(t + 1) * P, :], c.rows[:, t % 4, :]).then_inc(self.rows_stored[t % 4], 16)

    def pe_turn(self, pe, t):
        c = self.c
        pe.wait_ge(self.rows_ready, t + 1)
        for g in range(2):
            n = 2 * t + g
            wait(pe, self.evacuated, n - 1)
            for j in range(4):
                k = 4 * g + j
                ins = pe.transpose(c.ps[:, self.banks[g], j * P:(j + 1) * P],
                                   c.rows[:, t % 4, k * P:(k + 1) * P], c.ident[:, :])
            ins.then_inc(self.turns, 1)

    def dve_evacuate(self, dve, t):
        c = self.c
        for g in range(2):
            dve.wait_ge(self.turns, 2 * t + g + 1)
            if self.route:
                if g == 0:
                    wait(dve, self.logits_ready, t - 1)
                out = c.turned[:, t % 2, 4 * g:4 * g + 4, :]
            else:
                out = c.hT[:, 4 * g:4 * g + 4, t * P:(t + 1) * P]
            dve.tensor_tensor(out, c.ps[:, self.banks[g], :].rearrange("p (a b) -> p a b", b=P),
                              bc(c.norm_w[:, self.w, 4 * g:4 * g + 4], 2, P),
                              ALU.mult).then_inc(self.evacuated, 1)

    def pe_route(self, pe, t):
        c = self.c
        pe.wait_ge(self.evacuated, 2 * t + 2)
        wait(pe, self.logits_copied, t - 1)
        at = (t % 2) * P
        for k in range(KD):
            ins = pe.matmul(c.ps[:, self.logit_bank, at:at + NL], c.turned[:, t % 2, k, :],
                            c.w_router[:, k, :], start=(k == 0), stop=(k == KD - 1))
        ins.then_inc(self.logits_ready, 1)

    def act_logits(self, act, t):
        c = self.c
        act.wait_ge(self.logits_ready, t + 1)
        at = (t % 2) * P
        act.activation(c.logits[:, t, :], c.ps[:, self.logit_bank, at:at + NL],
                       ACT.Copy).then_inc(self.logits_copied, 1)


def load_router(eng, c, layer, sem):
    eng.dma_start(c.w_router[:, :, 0:NG],
                  c.ins["router_w_group"][layer].rearrange("(k p) g -> p k g", p=P)).then_inc(sem, 16)
    eng.dma_start(c.w_router[:, :, NG:NL],
                  c.ins["router_w_expert"][layer].rearrange("(k p) e -> p k e", p=P)).then_inc(sem, 16)


def conv_phase(c):
    nc, ins = c.nc, c.ins
    sems = Sems(nc, "conv")
    piece = c.carve()
    yT = piece(KD, S)
    w_out = piece(KD, D)
    w_in = piece(2, KD, 3, P)
    z = piece(S + 2)
    acc = piece(S)
    gc = piece(2, BANK)
    gb = piece(S)
    taps = piece(KD, 3)
    HT = S // BANK

    x_loaded = [sems(f"x_loaded{t}") for t in range(NT)]
    w_in_loaded = [sems(f"w_in_loaded{i}") for i in range(2)]
    w_out_loaded = sems("w_out_loaded")
    small_loaded = sems("small_loaded")
    consts = sems("consts")
    z_edges = sems("z_edges")
    products = sems("products")
    g_copied = sems("g_copied")
    z_half = sems("z_half")
    conv_step = sems("conv_step")
    y_ready = sems("y_ready")
    out_products = sems("out_products")
    x_added = sems("x_added")
    norm0 = Norm(c, sems, 0, False, (6, 7))
    norm1 = Norm(c, sems, 1, True, (6, 7), logit_bank=5)
    w_in_dram = ins["conv_w_in"][0].rearrange("(k p) (j c m) -> p k j c m", p=P, j=3, m=P)

    with nc.Block() as block:

        @block.sync
        def _(sp):
            for t in range(NT):
                sp.dma_start(c.x[:, t, :], ins["x"][0, t * P:(t + 1) * P, :]).then_inc(x_loaded[t], 16)
                if t == 1:
                    for i in range(2):
                        for k in range(3):
                            sp.dma_start(w_in[:, i, :, k, :], w_in_dram[:, :, k, i, :]).then_inc(w_in_loaded[i], 16)
            sp.dma_start(w_out, ins["conv_w_out"][0].rearrange("(k p) d -> p k d", p=P)).then_inc(w_out_loaded, 16)
            with sp.Fori(1, KD // 2) as pair:
                ct = pair * 2
                for i in range(2):
                    sp.wait_ge(products, HT * (ct + (i - 1)))
                    for k in range(3):
                        sp.dma_start(w_in[:, i, :, k, :],
                                     w_in_dram[:, :, k, bass.ds(ct + i, 1), :].rearrange("p k a m -> p (k a) m")
                                     ).then_inc(w_in_loaded[i], 16)
            for t in range(NT):
                norm1.sp_store(sp, t)
            for t in range(4):
                sp.wait_ge(norm1.rows_stored[t], 16 * NT // 4)

        @block.gpsimd
        def _(pool):
            step = Chain(pool, consts)
            step.mark(pool.memset(c.ident[:, :], 0.0))
            step.mark(pool.memset(c.ones[:, :], 1.0))
            step.mark(pool.memset(c.before[:, :], 1.0))
            step.mark(pool.memset(c.minus_half[:, :], -0.5))
            step.mark(pool.memset(c.upper_half[:, :], -1.0))
            step.mark(pool.iota(c.rank_of_col[:, :, :], [[0, 2], [1, RANKS]], base=0, channel_multiplier=0,
                                allow_small_or_imprecise_dtypes=True))
            step.mark(pool.iota(c.code[:, :, :], [[S, 2], [P, NT]], base=1, channel_multiplier=1,
                                allow_small_or_imprecise_dtypes=True))
            step.mark(pool.iota(c.from_last[:, :], [[-1, EG]], base=EG, channel_multiplier=0,
                                allow_small_or_imprecise_dtypes=True))
            step.mark(pool.iota(c.round_start[:, :], [[RANKS, MAXR]], base=0, channel_multiplier=0,
                                allow_small_or_imprecise_dtypes=True))
            step.sync()
            step.mark(pool.affine_select(out=c.ident[:, :], in_=c.ident[:, :], compare_op=ALU.not_equal, fill=1.0,
                                         base=0, pattern=[[-1, P]], channel_multiplier=1))
            step.mark(pool.affine_select(out=c.before[:, :], in_=c.before[:, :], compare_op=ALU.is_gt, fill=0.0,
                                         base=0, pattern=[[1, P]], channel_multiplier=-1))
            step.mark(pool.affine_select(out=c.upper_half[:, :], in_=c.upper_half[:, :], compare_op=ALU.is_ge,
                                         fill=-2.0, base=-RANKS, pattern=[[0, 1]], channel_multiplier=1))
            for t in range(NT):
                norm0.pool_rstd(pool, t)
            for t in range(NT):
                norm1.pool_rstd(pool, t)

        N_CONST = 12

        @block.scalar
        def _(act):
            for i, name in enumerate(("conv_norm_w", "ffn_norm_w", "mla_norm_w", "ffn_norm_w")):
                act.dma_start(c.norm_w[:, i, :], ins[name][i // 2 if name[0] == "f" else 0]
                              .rearrange("(k p) -> p k", p=P)).then_inc(small_loaded, 16)
            for layer in range(2):
                for half in range(2):
                    act.dma_start(c.xw[:, layer, :, half],
                                  ins["ffn_norm_w"][layer, half * BANK:(half + 1) * BANK]
                                  .rearrange("(p j) -> p j", j=4)).then_inc(small_loaded, 16)
            for j in range(3):
                act.dma_start(taps[:, :, j], ins["conv_k"][0, j].rearrange("(k p) -> p k", p=P)).then_inc(small_loaded, 16)
            load_router(act, c, 0, small_loaded)
            for t in range(NT + 2):
                if t < NT:
                    act.wait_ge(x_loaded[t], 16)
                    norm0.act_squares(act, t)
                if t >= 2:
                    norm0.act_rows(act, t - 2)

            def copies(ct, i):
                for h in range(HT):
                    n = HT * (ct + i) + h
                    act.wait_ge(products, n + 1)
                    wait(act, z_half, n - 1)
                    act.activation(gc[:, h, :], c.ps[:, 3 * h + 1, :], ACT.Copy).then_inc(g_copied, 1)
                    wait(act, y_ready, ct + i)
                    act.activation(gb[:, h * BANK:(h + 1) * BANK], c.ps[:, 3 * h, :], ACT.Copy).then_inc(g_copied, 1)

            copies(0, 0)
            copies(0, 1)
            with act.Fori(1, KD // 2) as pair:
                ct = pair * 2
                for i in range(2):
                    copies(ct, i)
            for t in range(NT):
                act.wait_ge(x_added, 2 * t + 2)
                norm1.act_squares(act, t)
                norm1.act_rows(act, t)
                norm1.act_logits(act, t)

        @block.vector
        def _(dve):
            dve.memset(z[:, 0:1], 0.0).then_inc(z_edges, 1)
            dve.memset(z[:, S + 1:S + 2], 0.0).then_inc(z_edges, 1)
            dve.wait_ge(small_loaded, 16 * 13)
            for t in range(NT + 3):
                if t < NT:
                    norm0.dve_var(dve, t)
                if t >= 3:
                    norm0.dve_evacuate(dve, t - 3)
            dve.wait_ge(z_edges, 2)
            step = Chain(dve, conv_step)

            def conv_tile(ct, i):
                step.at((ct + i) * 3)
                for h in range(HT):
                    n = HT * (ct + i) + h
                    dve.wait_ge(g_copied, 2 * n + 1)
                    dve.tensor_tensor(z[:, 1 + h * BANK:1 + (h + 1) * BANK], gc[:, h, :],
                                      c.ps[:, 3 * h + 2, :], ALU.mult).then_inc(z_half, 1)
                dve.wait_ge(z_half, HT * (ct + i) + HT)
                tap = taps[:, bass.ds(ct + i, 1), :].rearrange("p a j -> p (a j)")
                step.sync(dve.tensor_scalar(acc, z[:, 0:S], tap[:, 0:1], None, ALU.mult))
                step.sync(dve.scalar_tensor_tensor(out=acc, in0=z[:, 1:S + 1], scalar=tap[:, 1:2], in1=acc,
                                                   op0=ALU.mult, op1=ALU.add))
                step.sync(dve.scalar_tensor_tensor(out=acc, in0=z[:, 2:S + 2], scalar=tap[:, 2:3], in1=acc,
                                                   op0=ALU.mult, op1=ALU.add))
                dve.wait_ge(g_copied, 2 * HT * (ct + i + 1))
                dve.tensor_tensor(yT[:, bass.ds(ct + i, 1), :].rearrange("p a s -> p (a s)"), acc, gb,
                                  ALU.mult).then_inc(y_ready, 1)
                dve.wait_ge(y_ready, ct + i + 1)

            with dve.Fori(0, KD // 2) as pair:
                ct = pair * 2
                for i in range(2):
                    conv_tile(ct, i)

            def add(t):
                for h in range(2):
                    n = 2 * t + h
                    dve.wait_ge(out_products, n + 1)
                    xt = c.x[:, t, h * BANK:(h + 1) * BANK]
                    dve.tensor_tensor(xt, xt, c.ps[:, n % 4, :], ALU.add).then_inc(x_added, 1)

            for t in range(NT + 1):
                if t < NT:
                    add(t)
                if t >= 1:
                    norm1.dve_evacuate(dve, t - 1)
                if t < NT:
                    norm1.dve_var(dve, t)

        @block.tensor
        def _(pe):
            pe.wait_ge(consts, N_CONST)
            for t in range(NT):
                norm0.pe_turn(pe, t)

            def multiply(ct, i):
                pe.wait_ge(w_in_loaded[i], 24 * ct + 48)
                for h in range(HT):
                    n = HT * (ct + i) + h
                    wait(pe, z_half, n - 1)
                    wait(pe, g_copied, 2 * (n - 1))
                    for j in range(3):
                        for k in range(KD):
                            last = pe.matmul(c.ps[:, 3 * h + j, :], w_in[:, i, k, j, :],
                                             c.hT[:, k, h * BANK:(h + 1) * BANK],
                                             start=(k == 0), stop=(k == KD - 1))
                    last.then_inc(products, 1)

            pe.wait_ge(norm0.evacuated, 2 * NT)
            multiply(0, 0)
            multiply(0, 1)
            with pe.Fori(1, KD // 2) as pair:
                ct = pair * 2
                for i in range(2):
                    multiply(ct, i)
            pe.wait_ge(y_ready, KD)
            pe.wait_ge(w_out_loaded, 16)
            pe.wait_ge(small_loaded, 16 * 13)
            for t in range(NT + 1):
                if t < NT:
                    for h in range(2):
                        n = 2 * t + h
                        wait(pe, x_added, n - 3)
                        for k in range(KD):
                            last = pe.matmul(c.ps[:, n % 4, :], yT[:, k, t * P:(t + 1) * P],
                                             w_out[:, k, h * BANK:(h + 1) * BANK],
                                             start=(k == 0), stop=(k == KD - 1))
                        last.then_inc(out_products, 1)
                if t >= 1:
                    norm1.pe_turn(pe, t - 1)
                    norm1.pe_route(pe, t - 1)

    sems.clear()


def moe_phase(c, layer, last):
    nc, ins = c.nc, c.ins
    sems = Sems(nc, f"moe{layer}")
    piece = c.carve()
    w_gate = piece(2, 2, 4 * FF)
    w_up = piece(2, 2, 4 * FF)
    w_down = piece(2, KF, D)
    assert 3 * 2 * D <= piece.at[0]
    gathered = piece(2, BANK)
    xT = piece(2, 4, 2, RANKS)
    gate_up = piece(2, FF)
    silu = piece(2, KF, RANKS)
    hidden = piece(2, KF, RANKS)
    y = piece(2, BANK)
    earlier = piece(NT + 1, NE)
    rank = piece(2, NT)
    gates = piece(2, NT)
    idx_f = piece(4, NE)
    tiny = piece(24, NT)
    bias = piece(NL)
    piece = c.carve(c.hT[:, :, :].rearrange("p k s -> p (k s)"))
    chosen = piece(2, NT, NE)
    coded = piece(2, NT, NE)
    onehot = piece(2 * NT, P)
    big = piece(4, NT * NE)
    small = piece(15, NT, EG)
    y_pair = c.arena[:, 0:3 * 2 * D].rearrange("p (r k d) -> p r k d", r=3, k=2)

    gather_idx, scatter_idx, col_idx, n_rounds = c.gather_idx, c.scatter_idx, c.col_idx, c.n_rounds
    bias_loaded = sems("bias_loaded")
    cleared = sems("cleared")
    w_gate_up_loaded = [sems(f"w_gate_up_loaded{i}") for i in range(2)]
    w_down_loaded = [sems(f"w_down_loaded{i}") for i in range(2)]
    route_step = sems("route_step")
    exp_in = sems("exp_in")
    exp_out = sems("exp_out")
    chosen_ready = sems("chosen_ready")
    counted = sems("counted")
    rounds_ready = sems("rounds_ready")
    onehot_ready = sems("onehot_ready")
    idx_products = sems("idx_products")
    idx_ready = sems("idx_ready")
    round_step = sems("round_step")
    pool_step = sems("pool_step")
    rounds_begun = sems("rounds_begun")
    gathers_begun = sems("gathers_begun")
    scatters_begun = sems("scatters_begun")
    gather_done = [sems(f"gather_done{i}") for i in range(2)]
    y_stored = sems("y_stored")
    scatter_done = [sems(f"scatter_done{i}") for i in range(2)]
    x_turned = sems("x_turned")
    xT_ready = sems("xT_ready")
    gate_up_products = sems("gate_up_products")
    gate_up_copied = sems("gate_up_copied")
    h_turned = sems("h_turned")
    silu_ready = sems("silu_ready")
    hidden_ready = sems("hidden_ready")
    y_products = sems("y_products")
    y_copied = sems("y_copied")
    y_pair_loaded = [sems(f"y_pair_loaded{i}") for i in range(3)]
    first_scaled = sems("first_scaled")
    summed = sems("summed")
    x_added = sems("x_added")
    stored = sems("stored")
    norm = None if last else Norm(c, sems, 2, False, (0, 1))

    def done(g):
        return g + 1 + AHEAD

    def free(g):
        return g + 1

    gate_dram = ins["exp_w_gate"][layer].rearrange("e (h p j) f -> p e h (j f)", h=2, p=P)
    up_dram = ins["exp_w_up"][layer].rearrange("e (h p j) f -> p e h (j f)", h=2, p=P)
    down_dram = ins["exp_w_down"][layer].rearrange("e (j p) d -> p e j d", p=P)
    h_halves = c.h_rows.rearrange("t (h d) -> (t h) d", h=2)
    y_halves = c.y_rows.rearrange("t (h d) -> (t h) d", h=2)

    def rounds(eng):
        eng.wait_ge(rounds_ready, 1)
        return eng.value_load(n_rounds[0:1, 0:1], min_val=1, max_val=MAXR)

    with nc.Block() as block:

        @block.sync
        def _(sp):
            def load_gate_up(slot, e):
                for w, dram in ((w_gate, gate_dram), (w_up, up_dram)):
                    src = dram[:, bass.ds(e, 1), :, :].rearrange("p a h f -> p (a h) f")
                    sp.dma_start(w[:, slot, :, :], src).then_inc(w_gate_up_loaded[slot], 16)

            def load_down(slot, e):
                src = down_dram[:, bass.ds(e, 1), :, :].rearrange("p a j d -> p (a j) d")
                sp.dma_start(w_down[:, slot, :, :], src).then_inc(w_down_loaded[slot], 16)

            for slot in range(2):
                load_gate_up(slot, slot)
                load_down(slot, slot)
            count = rounds(sp)
            with sp.Fori(1, count * (NE // 2)) as pair:
                g = pair * 2
                for slot in range(2):
                    e = (g + slot) % NE
                    sp.wait_ge(gate_up_products, g + slot + free(0))
                    load_gate_up(slot, e)
                    sp.wait_ge(y_products, g + slot + free(0))
                    load_down(slot, e)
            sp.wait_ge(y_stored, count * NE + AHEAD)
            for t in range(NT):
                if t >= 3:
                    sp.wait_ge(x_added, t - 2)
                src = c.y_rows.rearrange("(k t p) d -> t p k d", k=2, p=P)[t]
                sp.dma_start(y_pair[:, t % 3, :, :], src).then_inc(y_pair_loaded[t % 3], 16)
            if last:
                for t in range(NT):
                    sp.wait_ge(x_added, t + 1)
                    sp.dma_start(c.out[0, t * P:(t + 1) * P, :], c.x[:, t, :]).then_inc(stored, 16)
                sp.wait_ge(stored, 16 * NT)

        @block.gpsimd
        def _(pool):
            pool.dma_start(bias[:, 0:NG], ins["router_b_group"][layer].partition_broadcast(P)).then_inc(bias_loaded, 16)
            pool.dma_start(bias[:, NG:NL], ins["router_b_expert"][layer].partition_broadcast(P)).then_inc(bias_loaded, 16)
            pool.memset(gathered, 0.0).then_inc(cleared, 1)
            pool.sem_inc(y_stored, AHEAD)
            pool.wait_ge(cleared, 1)
            count = rounds(pool)
            step = Chain(pool, pool_step)

            def gather(g, e, slot, n):
                pool.wait_ge(x_turned, g + free(0))
                pool.sem_inc(gathers_begun, 1)
                pool.tensor_copy(col_idx[:, slot, :], gather_idx[:, bass.ds(e, 1)]).then_inc(pool_step, 1)
                pool.wait_ge(pool_step, n + 1)
                pool.sem_inc(gathers_begun, 1)
                pool.indirect_dma_start(gathered[:, slot, :], None, h_halves,
                                        bass.IndirectOffsetOnAxis(ap=col_idx[:, slot, :], axis=0),
                                        bounds_check=2 * S - 1, oob_is_err=False).then_inc(gather_done[slot], 16)

            def scatter(g, e, slot, n):
                pool.wait_ge(y_copied, g + done(0))
                pool.sem_inc(scatters_begun, 1)
                pool.tensor_copy(col_idx[:, 2 + slot, :], scatter_idx[:, bass.ds(e, 1)]).then_inc(pool_step, 1)
                pool.wait_ge(pool_step, n + 1)
                pool.sem_inc(scatters_begun, 1)
                pool.indirect_dma_start(y_halves, bass.IndirectOffsetOnAxis(ap=col_idx[:, 2 + slot, :], axis=0),
                                        y[:, slot, :], None,
                                        bounds_check=4 * S - 1, oob_is_err=False).then_inc(scatter_done[slot], 16)

            def complete(g, slot):
                pool.wait_ge(scatter_done[slot], g * 8 + (16 - 8 * slot))
                pool.sem_inc(y_stored, 1)

            with pool.Fori(0, count) as r:
                pool.wait_ge(idx_ready, 2 * r + 2)
                pool.sem_inc(rounds_begun, 1)
                g0, n0 = r * NE, r * (2 * NE)
                for slot in range(2):
                    gather(g0 + slot, slot, slot, n0 + slot)
                with pool.Fori(1, NE // 2) as pair:
                    e = pair * 2
                    for slot in range(2):
                        gather(g0 + e + slot, e + slot, slot, n0 + 2 * e + (2 * slot - 2))
                        if slot:
                            complete(g0 + e + (slot - 3), 1 - slot)
                        scatter(g0 + e + (slot - 2), e + (slot - 2), slot, n0 + 2 * e + (2 * slot - 1))
                    complete(g0 + e - 1, 1)
                for slot in range(2):
                    scatter(g0 + (NE - 2 + slot), NE - 2 + slot, slot, n0 + (2 * NE - 2 + slot))
                    complete(g0 + (NE - 2 + slot), slot)
            if norm:
                for t in range(NT):
                    norm.pool_rstd(pool, t)

        @block.scalar
        def _(act):
            for i in range(2):
                act.wait_ge(exp_in, i + 1)
                act.activation(small[:, i, :, :], small[:, i, :, :], ACT.Exp).then_inc(exp_out, 1)
            for s in (gate_up_copied, silu_ready, y_copied):
                act.sem_inc(s, AHEAD)
            count = rounds(act)

            def expert(g, slot):
                act.wait_ge(gate_up_products, g + done(0))
                act.wait_ge(h_turned, g + free(0))
                act.activation(gate_up[:, slot, :], c.ps[:, 2 + slot, 0:FF], ACT.Copy).then_inc(gate_up_copied, 1)
                act.wait_ge(h_turned, g + done(0))
                act.wait_ge(hidden_ready, g + free(0))
                turned = c.ps[:, 4 + slot, 0:FF].rearrange("p (j m) -> p j m", m=P)
                act.activation(silu[:, slot, :, :], turned[:, :, 0:RANKS], ACT.Silu).then_inc(silu_ready, 1)
                act.wait_ge(y_products, g + done(0))
                act.wait_ge(y_stored, g + free(0))
                act.activation(y[:, slot, :], c.ps[:, 6 + slot, :], ACT.Copy).then_inc(y_copied, 1)

            with act.Fori(0, count) as r:
                with act.Fori(0, NE // 2) as pair:
                    e = pair * 2
                    for slot in range(2):
                        expert(r * NE + e + slot, slot)

            for t in range(NT + (2 if norm else 0)):
                if t < NT:
                    act.wait_ge(y_pair_loaded[t % 3], 16 * (t // 3 + 1))
                    first = y_pair[:, t % 3, 0, :]
                    act.activation(first, first, ACT.Copy, scale=gates[:, 0, t:t + 1]).then_inc(first_scaled, 1)
                if norm and 1 <= t < NT + 1:
                    act.wait_ge(x_added, t)
                    norm.act_squares(act, t - 1)
                if norm and t >= 2:
                    norm.act_rows(act, t - 2)

        @block.vector
        def _(dve):
            for s in (xT_ready, hidden_ready):
                dve.sem_inc(s, AHEAD)
            step = Chain(dve, route_step)
            lg = c.logits[:, :, 0:NG]
            le = c.logits[:, :, NG:NL].rearrange("p t (g j) -> p t g j", j=EG)
            bg = bc(bias[:, 0:NG], 1, NT)
            s_ = [small[:, i, :, :] for i in range(15)]
            t_ = [tiny[:, i, :] for i in range(24)]
            b_ = [big[:, i, :].rearrange("p (t e) -> p t e", e=NE) for i in range(4)]

            def tt(out, a, b, op):
                step.sync(dve.tensor_tensor(out, a, b, op))

            def red(out, a, op):
                step.sync(dve.tensor_reduce(out, a, X, op))

            def first_max(onehot_out, values, s1, t1):
                red(t1, values, ALU.max)
                tt(s1, values, bc(t1, 2, EG), ALU.is_equal)
                tt(s1, s1, bc(c.from_last[:, :], 1, NT), ALU.mult)
                red(t1, s1, ALU.max)
                tt(onehot_out, s1, bc(t1, 2, EG), ALU.is_equal)

            dve.wait_ge(bias_loaded, 32)
            red(t_[0], lg, ALU.max)
            dve.tensor_tensor(s_[0], lg, bc(t_[0], 2, NG), ALU.subtract).then_inc(exp_in, 1)
            tt(s_[2], lg, bg, ALU.add)
            group = s_[3]
            first_max(group, s_[2], s_[4], t_[1])
            four = b_[0].rearrange("p t (g j) -> p t g j", j=EG)
            tt(four, le, bc(group, 3, EG), ALU.mult)
            red(s_[5], four.rearrange("p t g j -> p t j g"), ALU.add)
            be = bc(bias[:, NG:NL].rearrange("p (g j) -> p g j", j=EG), 1, NT)
            four1 = b_[1].rearrange("p t (g j) -> p t g j", j=EG)
            tt(four1, bc(group, 3, EG), be, ALU.mult)
            red(s_[6], four1.rearrange("p t g j -> p t j g"), ALU.add)
            red(t_[2], s_[5], ALU.max)
            dve.tensor_tensor(s_[1], s_[5], bc(t_[2], 2, EG), ALU.subtract).then_inc(exp_in, 1)
            tt(s_[7], s_[5], s_[6], ALU.add)
            first_max(s_[8], s_[7], s_[9], t_[3])
            step.sync(dve.scalar_tensor_tensor(out=s_[10], in0=s_[8], scalar=-1e30, in1=s_[7],
                                               op0=ALU.mult, op1=ALU.add))
            first_max(s_[11], s_[10], s_[12], t_[4])
            for k, oh in ((0, s_[8]), (1, s_[11])):
                ch = chosen[:, k, :, :].rearrange("p t (g j) -> p t g j", j=EG)
                tt(ch, bc(group, 3, EG), bc(oh, 2, NG), ALU.mult)
            both = b_[2]
            tt(both, chosen[:, 0, :, :], chosen[:, 1, :, :], ALU.add)
            step.sync(dve.memset(earlier[:, 0, :], 0.0))
            for t in range(NT):
                ins_ = dve.tensor_tensor(earlier[:, t + 1, :], earlier[:, t, :], both[:, t, :], ALU.add)
                step.sync(ins_)
            dve.sem_inc(chosen_ready, 1)
            for k in range(2):
                tt(coded[:, k, :, :], chosen[:, k, :, :], bc(c.code[:, k, :], 2, NE), ALU.mult)
            dve.wait_ge(counted, 2)
            red(tiny[:, 5, 0:1], c.ps[:, 1, 0:NE], ALU.max)
            step.sync(dve.tensor_scalar(idx_f[:, 0, 0:MAXR], c.round_start[:, :], tiny[:, 5, 0:1], None, ALU.is_lt))
            red(tiny[:, 5, 1:2], idx_f[:, 0, 0:MAXR], ALU.add)
            dve.tensor_copy(n_rounds[:, :], tiny[:, 5, 1:2]).then_inc(rounds_ready, 1)
            for k in range(2):
                tt(b_[0], chosen[:, k, :, :], c.ps[:, 0, :].rearrange("p (t e) -> p t e", e=NE), ALU.mult)
                red(rank[:, k, :], b_[0], ALU.add)
            dve.wait_ge(exp_out, 2)
            tt(s_[13], s_[0], group, ALU.mult)
            red(t_[6], s_[13], ALU.add)
            red(t_[7], s_[0], ALU.add)
            step.sync(dve.reciprocal(t_[8], t_[7]))
            tt(t_[9], t_[6], t_[8], ALU.mult)
            red(t_[10], s_[1], ALU.add)
            step.sync(dve.reciprocal(t_[11], t_[10]))
            for k, oh in ((0, s_[8]), (1, s_[11])):
                tt(s_[14], s_[1], oh, ALU.mult)
                red(t_[12 + k], s_[14], ALU.add)
                tt(t_[12 + k], t_[12 + k], t_[11], ALU.mult)
            tt(t_[14], t_[12], t_[13], ALU.add)
            step.sync(dve.reciprocal(t_[15], t_[14]))
            for k in range(2):
                tt(t_[16], t_[12 + k], t_[15], ALU.mult)
                tt(gates[:, k, :], t_[16], t_[9], ALU.mult)
            count = rounds(dve)

            PER_ROUND = 7

            def expert_x(g, slot):
                dve.wait_ge(x_turned, g + done(0))
                dve.wait_ge(gate_up_products, g + free(0))
                dve.tensor_tensor(xT[:, slot, :, :, :].rearrange("p j h m -> p (j h) m"),
                                  c.ps[:, slot, :].rearrange("p (a m) -> p a m", m=RANKS),
                                  bc(c.xw[:, layer, :, :].rearrange("p j h -> p (j h)"), 2, RANKS),
                                  ALU.mult).then_inc(xT_ready, 1)

            def expert_h(g, slot):
                dve.wait_ge(silu_ready, g + done(0))
                dve.wait_ge(y_products, g + free(0))
                turned = c.ps[:, 4 + slot, 0:FF].rearrange("p (j m) -> p j m", m=P)
                dve.tensor_tensor(hidden[:, slot, :, :], silu[:, slot, :, :], turned[:, :, RANKS:P],
                                  ALU.mult).then_inc(hidden_ready, 1)

            with dve.Fori(0, count) as r:
                step = Chain(dve, round_step)
                step.at(r * PER_ROUND)
                dve.wait_ge(idx_products, r + 1)
                rank_all = rank.rearrange("p k t -> p (k t)")
                dve.tensor_tensor(onehot, bc(rank_all, 2, P),
                                  bc(c.rank_of_col[:, :, :].rearrange("p a b -> p (a b)"), 1, 2 * NT),
                                  ALU.is_equal).then_inc(onehot_ready, 1)
                dve.wait_ge(onehot_ready, r + 1)
                step.mark(dve.tensor_scalar(rank_all, rank_all, -float(RANKS), None, ALU.add))
                dve.wait_ge(idx_products, r + 2)
                step.sync(dve.tensor_copy(idx_f[:, 0, :], c.ps[:, 0, 0:NE]))
                code = idx_f[:, 0, :]
                step.mark(dve.tensor_scalar(idx_f[:, 1, :], code, 2.0, c.upper_half[:, 0:1], ALU.mult, ALU.add))
                step.mark(dve.tensor_scalar(idx_f[:, 2, :], code, 0.5, 1e6, ALU.is_lt, ALU.mult))
                step.sync(dve.tensor_scalar(idx_f[:, 3, :], code, float(S) + 0.5, -2.0 * S, ALU.is_gt, ALU.mult))
                step.sync(dve.tensor_tensor(idx_f[:, 1, :], idx_f[:, 1, :], idx_f[:, 2, :], ALU.add))
                step.sync(dve.tensor_tensor(idx_f[:, 3, :], idx_f[:, 1, :], idx_f[:, 3, :], ALU.add))
                assert step.n == PER_ROUND
                dve.wait_ge(y_stored, r * NE + AHEAD)
                dve.tensor_copy(gather_idx[:, :], idx_f[:, 3, :]).then_inc(idx_ready, 1)
                dve.tensor_copy(scatter_idx[:, :], idx_f[:, 1, :]).then_inc(idx_ready, 1)
                g0 = r * NE
                expert_x(g0, 0)
                with dve.Fori(0, NE // 2 - 1) as pair:
                    e = pair * 2
                    for slot in range(2):
                        expert_x(g0 + e + slot + 1, 1 - slot)
                        expert_h(g0 + e + slot, slot)
                expert_x(g0 + NE - 1, 1)
                expert_h(g0 + NE - 2, 0)
                expert_h(g0 + NE - 1, 1)

            def combine(t):
                dve.wait_ge(first_scaled, t + 1)
                y0, y1 = y_pair[:, t % 3, 0, :], y_pair[:, t % 3, 1, :]
                dve.scalar_tensor_tensor(out=y0, in0=y1, scalar=gates[:, 1, t:t + 1], in1=y0,
                                         op0=ALU.mult, op1=ALU.add).then_inc(summed, 1)
                dve.wait_ge(summed, t + 1)
                dve.tensor_tensor(c.x[:, t, :], c.x[:, t, :], y0, ALU.add).then_inc(x_added, 1)

            for t in range(NT + (3 if norm else 0)):
                if t < NT:
                    combine(t)
                if norm and 1 <= t < NT + 1:
                    norm.dve_var(dve, t - 1)
                if norm and t >= 3:
                    norm.dve_evacuate(dve, t - 3)

        @block.tensor
        def _(pe):
            for s in (x_turned, gate_up_products, h_turned, y_products):
                pe.sem_inc(s, AHEAD)
            pe.sem_inc(idx_products, 1)
            pe.wait_ge(chosen_ready, 1)
            tok = c.ps[:, 0, :]
            pe.matmul(tok, c.before[:, :], big[:, 2, :], start=True, stop=False)
            pe.matmul(tok, c.ones[:, :], earlier[:, 0:NT, :].rearrange("p t e -> p (t e)"),
                      start=False, stop=True).then_inc(counted, 1)
            pe.matmul(c.ps[:, 1, 0:NE], c.ones[:, :], earlier[:, NT, :], start=True, stop=True).then_inc(counted, 1)
            count = rounds(pe)
            pe.wait_ge(cleared, 1)

            def turn_x(g, slot):
                pe.wait_ge(gather_done[slot], g * 8 + (16 - 8 * slot))
                pe.wait_ge(xT_ready, g + free(0))
                rows = gathered[:, slot, :].rearrange("p (m j) -> p j m", j=4)
                for j in range(4):
                    last_ = pe.transpose(c.ps[:, slot, j * P:(j + 1) * P], rows[:, j, :], c.ident[:, :])
                last_.then_inc(x_turned, 1)

            def gate_and_up(g, slot):
                pe.wait_ge(xT_ready, g + done(0))
                pe.wait_ge(w_gate_up_loaded[slot], g * 16 + (32 - 16 * slot))
                pe.wait_ge(gate_up_copied, g + free(0))
                for half in range(2):
                    for j in range(4):
                        for row, w in ((0, w_gate), (RANKS, w_up)):
                            last_ = pe.matmul(c.ps[row:row + RANKS, 2 + slot, 0:FF], xT[:, slot, j, half, :],
                                              w[:, slot, half, j * FF:(j + 1) * FF],
                                              start=(half + j == 0), stop=(half == 1 and j == 3))
                last_.then_inc(gate_up_products, 1)

            def turn_h(g, slot):
                pe.wait_ge(gate_up_copied, g + done(0))
                pe.wait_ge(hidden_ready, g + free(0))
                for j in range(KF):
                    last_ = pe.transpose(c.ps[:, 4 + slot, j * P:(j + 1) * P],
                                         gate_up[:, slot, j * P:(j + 1) * P], c.ident[:, :])
                last_.then_inc(h_turned, 1)

            def down(g, slot):
                pe.wait_ge(hidden_ready, g + done(0))
                pe.wait_ge(w_down_loaded[slot], g * 8 + (16 - 8 * slot))
                pe.wait_ge(y_copied, g + free(0))
                for j in range(KF):
                    for half in range(2):
                        last_ = pe.matmul(c.ps[half * RANKS:(half + 1) * RANKS, 6 + slot, :], hidden[:, slot, j, :],
                                          w_down[:, slot, j, half * BANK:(half + 1) * BANK],
                                          start=(j == 0), stop=(j == KF - 1))
                last_.then_inc(y_products, 1)

            with pe.Fori(0, count) as r:
                pe.wait_ge(onehot_ready, r + 1)
                for n in range(2 * NT):
                    last_ = pe.matmul(c.ps[:, 0, 0:NE], onehot[:, n, :], coded[:, n // NT, n % NT, :],
                                      start=(n == 0), stop=(n == 2 * NT - 1))
                last_.then_inc(idx_products, 1)
                g0 = r * NE
                turn_x(g0, 0)
                with pe.Fori(0, NE // 2 - 1) as pair:
                    e = pair * 2
                    for slot in range(2):
                        gate_and_up(g0 + e + slot, slot)
                        turn_x(g0 + e + slot + 1, 1 - slot)
                        turn_h(g0 + e + slot, slot)
                        down(g0 + e + slot, slot)
                gate_and_up(g0 + NE - 2, 0)
                turn_x(g0 + NE - 1, 1)
                turn_h(g0 + NE - 2, 0)
                down(g0 + NE - 2, 0)
                gate_and_up(g0 + NE - 1, 1)
                turn_h(g0 + NE - 1, 1)
                down(g0 + NE - 1, 1)
            if norm:
                for t in range(NT):
                    norm.pe_turn(pe, t)

    sems.clear()


def attention_phase(c):
    nc, ins = c.nc, c.ins
    sems = Sems(nc, "mla")
    piece = c.carve()
    latT = piece(KQ + KKV, S)
    w_q = piece(KQ, NH * QD)
    w_kv = piece(KKV, NH * (NOPE + VD))
    heads_at = piece.at[0]
    qkT = piece(2, 2, S)
    ropeT = piece(2, 2, S)
    v = piece(2, NT, VD)
    probsT = piece(2, NT, 2 * P)
    piece_t = c.carve(c.turned[:, :, :, :].rearrange("p a k m -> p (a k m)"))
    piece_r = c.carve(c.rows[:, 2:4, :].rearrange("p a d -> p (a d)"))
    k_rope = piece_t(NT, ROPE)
    cos_q = piece_t(NT, ROPE)
    sin_q = piece_t(NT, ROPE)
    q_k_rows = piece_r(2, 2 * NOPE + 2 * ROPE)
    raw = piece_r(2, QD + NOPE + VD)
    junk = (piece_t(QD + NOPE), c.logits[:, :, :].rearrange("p t n -> p (t n)")[:, 0:QD + NOPE])
    rot = piece_r(2, ROPE)
    head_sumsq = piece(2, 2)
    head_sum2 = piece(2, 2)
    head_var = piece(2, 2)
    head_rstd = piece(2, 2)
    k_rope_sumsq = piece(NT, 2)
    row_max = piece(2, 1)
    minus_max = piece(2, 1)
    row_sum = piece(2, 1)
    row_rec = piece(2, 1)
    lat_gain = piece(KQ + KKV)
    nope_gain = piece(2)
    lat_sumsq = piece(NT, 2)
    lat_var = piece(NT, 2)
    lat_rstd = piece(NT, 2)
    early = [heads_at]

    def early_piece(*shape):
        n = int(np.prod(shape))
        a = c.arena[:, early[0]:early[0] + n]
        early[0] += n
        assert early[0] <= heads_at + 10240 + 4096
        if len(shape) == 2:
            a = a.rearrange("p (a b) -> p a b", b=shape[1])
        return a

    w_lat = early_piece(KD, LAT)
    lat_rows = early_piece(2, QL + KVL)
    k_raw = early_piece(NT, ROPE)
    lat_junk = early_piece(2, QL + KVL)
    pos_f = early_piece(NT)
    inv_freq = early_piece(ROPE // 2)
    angle = early_piece(NT, ROPE // 2)
    turns_ = early_piece(NT, ROPE // 2)
    sine = early_piece(NT, ROPE // 2)
    cosine = early_piece(NT, ROPE // 2)
    k_tmp = early_piece(NT, ROPE)
    k_tmp2 = early_piece(NT, ROPE)
    rope_gain = early_piece(2, ROPE)
    w_out = c.arena[:, 0:KD * D].rearrange("p (k d) -> p k d", k=KD)
    assert KD * D <= heads_at
    probs = c.rows
    oT = c.hT
    HR = ROPE // 2
    SCALE = float(QD) ** -0.5

    lat_w_loaded = sems("lat_w_loaded")
    up_w_loaded = sems("up_w_loaded")
    small_loaded = sems("small_loaded")
    out_w_loaded = sems("out_w_loaded")
    freq_set = sems("freq_set")
    trig_step = sems("trig_step")
    sin_in = sems("sin_in")
    sin_out = sems("sin_out")
    lat_products = sems("lat_products")
    lat_squares = sems("lat_squares")
    lat_step = sems("lat_step")
    lat_var_ready = sems("lat_var_ready")
    lat_rstd_ready = sems("lat_rstd_ready")
    lat_scaled = sems("lat_scaled")
    lat_turned = sems("lat_turned")
    latT_ready = sems("latT_ready")
    k_rope_ready = sems("k_rope_ready")
    up_products = sems("up_products")
    raw_copied = sems("raw_copied")
    head_squares = sems("head_squares")
    head_step = sems("head_step")
    head_var_ready = sems("head_var_ready")
    head_rstd_ready = sems("head_rstd_ready")
    rows_normed = sems("rows_normed")
    rot_step = sems("rot_step")
    rows_ready = sems("rows_ready")
    v_copied = sems("v_copied")
    qk_turned = sems("qk_turned")
    qkT_ready = sems("qkT_ready")
    ropeT_ready = sems("ropeT_ready")
    scores = sems("scores")
    max_found = sems("max_found")
    bias_ready = sems("bias_ready")
    exps = sems("exps")
    rec_ready = sems("rec_ready")
    probs_ready = sems("probs_ready")
    probs_turned = [sems(f"probs_turned{g}") for g in range(2)]
    probsT_ready = [sems(f"probsT_ready{g}") for g in range(2)]
    pair_products = sems("pair_products")
    pair_copied = sems("pair_copied")
    out_products = sems("out_products")
    x_added = sems("x_added")
    norm = Norm(c, sems, 3, True, (5, 6), logit_bank=7)

    freqs = (10000.0 ** (-np.arange(0, ROPE, 2) / ROPE)).astype(np.float32)
    TWO_PI = 2 * np.pi
    PI_A = float(np.float32(6.28125))
    PI_B = float(np.float32(np.round((TWO_PI - PI_A) * 2**22) / 2**22))
    PI_C = float(np.float32(TWO_PI - PI_A - PI_B))
    ROUND = 1.5 * 2.0**23
    PI_MAX = float(np.nextafter(np.float32(np.pi), np.float32(0)))

    LAST = NH - 1
    PROB_BANKS = ((5, 6), (6, 5))

    with nc.Block() as block:

        @block.sync
        def _(sp):
            sp.dma_start(w_lat, ins["mla_w_down"][0].rearrange("(k p) m -> p k m", p=P)).then_inc(lat_w_loaded, 16)
            sp.dma_start(c.pos_i[:, :], ins["positions"][0].rearrange("(t p) -> p t", p=P)).then_inc(small_loaded, 16)
            sp.dma_start(lat_gain[:, 0:KQ], ins["mla_q_lat_norm"][0].rearrange("(k p) -> p k", p=P)).then_inc(small_loaded, 16)
            sp.dma_start(lat_gain[:, KQ:KQ + KKV], ins["mla_kv_lat_norm"][0].rearrange("(k p) -> p k", p=P)).then_inc(small_loaded, 16)
            for i, name in enumerate(("mla_q_head_norm", "mla_k_head_norm")):
                sp.dma_start(nope_gain[:, i:i + 1], ins[name][0, 0:NOPE].rearrange("(p a) -> p a", a=1)).then_inc(small_loaded, 16)
                sp.dma_start(rope_gain[:, i, :], ins[name][0, NOPE:QD].partition_broadcast(P)).then_inc(small_loaded, 16)
            load_router(sp, c, 1, small_loaded)
            sp.dma_start(w_q, ins["mla_w_q_up"][0].rearrange("(k p) m -> p k m", p=P)).then_inc(up_w_loaded, 16)
            sp.dma_start(w_kv, ins["mla_w_kv_up"][0].rearrange("(k p) m -> p k m", p=P)).then_inc(up_w_loaded, 16)
            sp.wait_ge(up_products, NH * NT)
            sp.dma_start(w_out, ins["mla_w_out"][0].rearrange("(k p) d -> p k d", p=P)).then_inc(out_w_loaded, 16)
            for t in range(NT):
                norm.sp_store(sp, t)
            for t in range(4):
                sp.wait_ge(norm.rows_stored[t], 16 * NT // 4)

        @block.gpsimd
        def _(pool):
            for i in range(HR):
                pool.memset(inv_freq[:, i:i + 1], float(freqs[i])).then_inc(freq_set, 1)
            pool.memset(k_rope_sumsq[:, :, 0:1], 0.0).then_inc(freq_set, 1)
            for t in range(NT):
                pool.wait_ge(lat_var_ready, t + 1)
                pool.tensor_tensor(lat_rstd[:, t, :], lat_var[:, t, :], c.minus_half[:, :], ALU.pow).then_inc(lat_rstd_ready, 1)

            def head_tile(p, h, par, i):
                if i == 0:
                    wait(pool, pair_products, 4 * (h - 1))
                pool.wait_ge(head_var_ready, p + 1)
                pool.tensor_tensor(head_rstd[:, i % 2, :], head_var[:, i % 2, :], c.minus_half[:, :],
                                   ALU.pow).then_inc(head_rstd_ready, 1)
                pool.tensor_copy(v[:, par, i, :], raw[:, i % 2, QD + NOPE:]).then_inc(v_copied, 1)

            for i in range(NT):
                head_tile(i, 0, 0, i)
            for i in range(NT):
                head_tile(NT + i, 1, 1, i)
            with pool.Fori(1, NH // 2) as pair:
                for par in range(2):
                    for i in range(NT):
                        h = pair * 2 + par
                        head_tile(h * NT + i, h, par, i)
            for t in range(NT):
                norm.pool_rstd(pool, t)

        @block.scalar
        def _(act):
            for i, (src, dst) in enumerate(((angle, sine), (turns_, cosine))):
                act.wait_ge(sin_in, i + 1)
                act.activation(dst, src, ACT.Sin).then_inc(sin_out, 1)
            for t in range(NT + 1):
                if t < NT:
                    act.wait_ge(lat_products, 2 * t + 2)
                    wait(act, lat_var_ready, t - 1)
                    a, b = 2 * (t % 2), 2 * (t % 2) + 1
                    act.activation(lat_junk[:, t % 2, 0:QL], c.ps[:, a, 0:QL], ACT.Square,
                                   accum_out=lat_sumsq[:, t, 0:1]).then_inc(lat_squares, 1)
                    act.activation(lat_junk[:, t % 2, QL:], c.ps[:, b, 0:KVL], ACT.Square,
                                   accum_out=lat_sumsq[:, t, 1:2]).then_inc(lat_squares, 1)
                    act.activation(k_raw[:, t, :], c.ps[:, b, KVL:KVL + ROPE], ACT.Copy).then_inc(lat_scaled, 1)
                if t >= 1:
                    u = t - 1
                    a, b = 2 * (u % 2), 2 * (u % 2) + 1
                    act.wait_ge(lat_rstd_ready, u + 1)
                    wait(act, lat_turned, 2 * (u - 1))
                    act.activation(lat_rows[:, u % 2, 0:QL], c.ps[:, a, 0:QL], ACT.Copy,
                                   scale=lat_rstd[:, u, 0:1]).then_inc(lat_scaled, 1)
                    act.activation(lat_rows[:, u % 2, QL:], c.ps[:, b, 0:KVL], ACT.Copy,
                                   scale=lat_rstd[:, u, 1:2]).then_inc(lat_scaled, 1)

            def squares(p, slot):
                act.wait_ge(up_products, p + 1)
                wait(act, rows_ready, p - 1)
                wait(act, v_copied, p - 1)
                act.activation(raw[:, slot, :], c.ps[:, 4, 0:QD + NOPE + VD], ACT.Copy).then_inc(raw_copied, 1)
                act.wait_ge(raw_copied, p + 1)
                act.activation(junk[slot][:, 0:QD], raw[:, slot, 0:QD], ACT.Square,
                               accum_out=head_sumsq[:, slot, 0:1]).then_inc(head_squares, 1)
                act.activation(junk[slot][:, QD:], raw[:, slot, QD:QD + NOPE], ACT.Square,
                               accum_out=head_sumsq[:, slot, 1:2]).then_inc(head_squares, 1)

            def copy_rope(p, h, i, bank):
                act.wait_ge(qkT_ready, p + 1)
                act.activation(ropeT[0:ROPE, h % 2, :, i * P:(i + 1) * P],
                               c.ps[0:ROPE, bank, 2 * P:4 * P].rearrange("p (a m) -> p a m", m=P),
                               ACT.Copy).then_inc(ropeT_ready, 1)

            def exp(s, slot):
                act.wait_ge(bias_ready, s + 1)
                wait(act, probs_turned[1], s - 1)
                act.activation(probs[:, slot, :], c.ps[:, 2 * slot:2 * slot + 2, :].rearrange("p a b -> p (a b)"),
                               ACT.Exp, bias=minus_max[:, slot, :], scale=SCALE,
                               accum_out=row_sum[:, slot, :]).then_inc(exps, 1)

            def copy_probs(s, i, q):
                act.wait_ge(probs_turned[1], s + 1)
                wait(act, pair_products, q - 1)
                act.activation(probsT[:, (i // 2) % 2, 4:8, (i % 2) * P:(i % 2 + 1) * P],
                               c.ps[:, PROB_BANKS[i % 2][1], :].rearrange("p (a m) -> p a m", m=P),
                               ACT.Copy).then_inc(probsT_ready[1], 1)

            def copy_out(q, h, j):
                act.wait_ge(pair_products, q + 1)
                act.activation(oT[:, bass.ds(h, 1), j * 2 * P:(j + 1) * 2 * P].rearrange("p a m -> p (a m)"),
                               c.ps[:, 7, 0:2 * P], ACT.Copy).then_inc(pair_copied, 1)

            def step(h, i, par, first=False, ends=False):
                s = h * NT + i
                if i == 0:
                    copy_rope(s + NT - 1, par, NT - 1, 5)
                exp(s, i % 2)
                if i > 0 and not ends:
                    copy_rope(s + NT - 1, par + 1, i - 1, 5 + i % 2)
                if not ends:
                    squares(s + NT, i % 2)
                if not (first and i == 0):
                    copy_probs(s - 1, (i - 1) % NT, 4 * h + (i - 1) // 2)
                if i % 2 == 0 and not (first and i == 0):
                    copy_out(4 * h + i // 2 - 1, h if i else h - 1, (i // 2 - 1) % 4)

            for p in range(NT):
                squares(p, p % 2)
                if p >= 1:
                    copy_rope(p - 1, 0, p - 1, 5 + (p - 1) % 2)
            for i in range(NT):
                step(0, i, 0, first=True)
            with act.Fori(0, (LAST - 1) // 2) as pair:
                h = pair * 2 + 1
                for par in (1, 0):
                    for i in range(NT):
                        step(h + (1 - par), i, par)
            for i in range(NT):
                step(LAST, i, 1, ends=True)
            n = NH * NT
            copy_probs(n - 1, NT - 1, 4 * NH - 1)
            copy_out(4 * NH - 1, LAST, 3)
            for t in range(NT):
                act.wait_ge(x_added, 2 * t + 2)
                norm.act_squares(act, t)
                norm.act_rows(act, t)
                norm.act_logits(act, t)

        @block.vector
        def _(dve):
            trig = Chain(dve, trig_step)
            dve.wait_ge(freq_set, HR + 1)
            dve.wait_ge(small_loaded, 16 * 9)
            trig.sync(dve.tensor_copy(pos_f, c.pos_i[:, :]))
            trig.sync(dve.tensor_tensor(angle, bc(pos_f, 2, HR), bc(inv_freq, 1, NT), ALU.mult))
            trig.sync(dve.tensor_scalar(turns_, angle, 1.0 / TWO_PI, ROUND, ALU.mult, ALU.add))
            trig.sync(dve.tensor_scalar(turns_, turns_, -ROUND, None, ALU.add))
            for part in (PI_A, PI_B, PI_C):
                trig.sync(dve.scalar_tensor_tensor(out=angle, in0=turns_, scalar=-part, in1=angle,
                                                   op0=ALU.mult, op1=ALU.add))
            trig.sync(dve.tensor_scalar(turns_, angle, PI_MAX / 2, -TWO_PI, ALU.is_gt, ALU.mult))
            trig.sync(dve.scalar_tensor_tensor(out=turns_, in0=angle, scalar=TWO_PI / 4, in1=turns_,
                                               op0=ALU.add, op1=ALU.add))
            dve.tensor_scalar(angle, angle, PI_MAX, -PI_MAX, ALU.min, ALU.max).then_inc(sin_in, 1)
            dve.tensor_scalar(turns_, turns_, PI_MAX, -PI_MAX, ALU.min, ALU.max).then_inc(sin_in, 1)

            lat = Chain(dve, lat_step)
            for t in range(NT + 2):
                if t < NT:
                    dve.wait_ge(lat_squares, 2 * t + 2)
                    lat.mark(dve.tensor_scalar(lat_var[:, t, 0:1], lat_sumsq[:, t, 0:1], 1.0 / QL, EPS, ALU.mult, ALU.add))
                    dve.tensor_scalar(lat_var[:, t, 1:2], lat_sumsq[:, t, 1:2], 1.0 / KVL, EPS,
                                      ALU.mult, ALU.add).then_inc(lat_var_ready, 1)
                if t >= 2:
                    u = t - 2
                    for g, (k0, n) in enumerate(((0, KQ), (KQ, KKV))):
                        dve.wait_ge(lat_turned, 2 * u + g + 1)
                        dve.tensor_tensor(latT[:, k0:k0 + n, u * P:(u + 1) * P],
                                          c.ps[:, 5 + g, 0:n * P].rearrange("p (a m) -> p a m", m=P),
                                          bc(lat_gain[:, k0:k0 + n], 2, P), ALU.mult).then_inc(latT_ready, 1)

            dve.wait_ge(sin_out, 2)
            dve.wait_ge(lat_scaled, 3 * NT)

            def tables(cos_w, sin_w, gain):
                g = rope_gain[:, gain, :]
                for half in range(2):
                    a, b = half * HR, (half + 1) * HR
                    o = (1 - half) * HR
                    trig.mark(dve.tensor_tensor(cos_w[:, :, a:b], cosine, bc(g[:, a:b], 1, NT), ALU.mult))
                    trig.mark(dve.scalar_tensor_tensor(out=sin_w[:, :, a:b], in0=sine, scalar=(-1.0, 1.0)[half],
                                                       in1=bc(g[:, o:o + HR], 1, NT), op0=ALU.mult, op1=ALU.mult))

            tables(cos_q, sin_q, 0)
            tables(k_tmp, k_tmp2, 1)
            trig.sync()
            trig.mark(dve.tensor_tensor(k_tmp, k_tmp, k_raw, ALU.mult))
            trig.mark(dve.tensor_tensor(k_tmp2[:, :, 0:HR], k_tmp2[:, :, 0:HR], k_raw[:, :, HR:], ALU.mult))
            trig.sync(dve.tensor_tensor(k_tmp2[:, :, HR:], k_tmp2[:, :, HR:], k_raw[:, :, 0:HR], ALU.mult))
            trig.sync(dve.tensor_tensor(k_rope, k_tmp, k_tmp2, ALU.add))
            trig.sync(dve.tensor_tensor(k_tmp, k_raw, k_raw, ALU.mult))
            trig.sync(dve.tensor_reduce(k_rope_sumsq[:, :, 1], k_tmp, X, ALU.add))

            def norm_rows(p, slot, i):
                dve.wait_ge(head_squares, 2 * p + 2)
                wait(dve, head_rstd_ready, p - 1)
                dve.tensor_tensor(head_sum2[:, slot, :], head_sumsq[:, slot, :], k_rope_sumsq[:, i, :],
                                  ALU.add).then_inc(head_step, 1)
                dve.wait_ge(head_step, p + 1)
                dve.tensor_scalar(head_var[:, slot, :], head_sum2[:, slot, :], 1.0 / QD, EPS,
                                  ALU.mult, ALU.add).then_inc(head_var_ready, 1)
                dve.wait_ge(head_rstd_ready, p + 1)
                wait(dve, qk_turned, p - 1)
                rows = q_k_rows[:, slot, :]
                rope_in = rot[:, 0, :]
                dve.tensor_scalar(rope_in, raw[:, slot, NOPE:QD], head_rstd[:, slot, 0:1], None,
                                  ALU.mult).then_inc(rows_normed, 1)
                dve.tensor_scalar(rows[:, 0:NOPE], raw[:, slot, 0:NOPE], head_rstd[:, slot, 0:1], None,
                                  ALU.mult).then_inc(rows_normed, 1)
                dve.tensor_scalar(rows[:, NOPE:2 * NOPE], raw[:, slot, QD:QD + NOPE], head_rstd[:, slot, 1:2], None,
                                  ALU.mult).then_inc(rows_normed, 1)
                dve.tensor_scalar(rows[:, 2 * NOPE + ROPE:], k_rope[:, i, :], head_rstd[:, slot, 1:2], None,
                                  ALU.mult).then_inc(rows_normed, 1)
                dve.wait_ge(rows_normed, 4 * p + 4)
                q_rot = rows[:, 2 * NOPE:2 * NOPE + ROPE]
                dve.tensor_tensor(rot[:, 1, 0:HR], rope_in[:, HR:], sin_q[:, i, 0:HR], ALU.mult).then_inc(rot_step, 1)
                dve.tensor_tensor(rot[:, 1, HR:], rope_in[:, 0:HR], sin_q[:, i, HR:], ALU.mult).then_inc(rot_step, 1)
                dve.tensor_tensor(q_rot, rope_in, cos_q[:, i, :], ALU.mult).then_inc(rot_step, 1)
                dve.wait_ge(rot_step, 3 * p + 3)
                dve.tensor_tensor(q_rot, q_rot, rot[:, 1, :], ALU.add).then_inc(rows_ready, 1)
                dve.wait_ge(rows_ready, p + 1)

            def gain_qk(p, h, i, bank):
                dve.wait_ge(qk_turned, p + 1)
                dve.tensor_tensor(qkT[:, h % 2, :, i * P:(i + 1) * P],
                                  c.ps[:, bank, 0:2 * P].rearrange("p (a m) -> p a m", m=P),
                                  bc(nope_gain, 2, P), ALU.mult).then_inc(qkT_ready, 1)

            def find_max(s, slot):
                dve.wait_ge(scores, s + 1)
                dve.tensor_reduce(row_max[:, slot, :], c.ps[:, 2 * slot:2 * slot + 2, :].rearrange("p a b -> p (a b)"),
                                  X, ALU.max).then_inc(max_found, 1)
                dve.wait_ge(max_found, s + 1)
                dve.tensor_scalar(minus_max[:, slot, :], row_max[:, slot, :], -SCALE, None,
                                  ALU.mult).then_inc(bias_ready, 1)

            def copy_probs(s, i, q):
                dve.wait_ge(probs_turned[0], s + 1)
                wait(dve, pair_products, q - 1)
                dve.tensor_copy(probsT[:, (i // 2) % 2, 0:4, (i % 2) * P:(i % 2 + 1) * P],
                                c.ps[:, PROB_BANKS[i % 2][0], :].rearrange("p (a m) -> p a m", m=P)
                                ).then_inc(probsT_ready[0], 1)

            def divide(s, slot):
                dve.wait_ge(exps, s + 1)
                dve.reciprocal(row_rec[:, slot, :], row_sum[:, slot, :]).then_inc(rec_ready, 1)
                dve.wait_ge(rec_ready, s + 1)
                dve.tensor_scalar(probs[:, slot, :], probs[:, slot, :], row_rec[:, slot, :], None,
                                  ALU.mult).then_inc(probs_ready, 1)

            def step(h, i, par, first=False, ends=False):
                s = h * NT + i
                if i == 0:
                    gain_qk(s + NT - 1, par, NT - 1, 5)
                find_max(s, i % 2)
                if i > 0 and not ends:
                    gain_qk(s + NT - 1, par + 1, i - 1, 5 + i % 2)
                if not (first and i == 0):
                    copy_probs(s - 1, (i - 1) % NT, 4 * h + (i - 1) // 2)
                divide(s, i % 2)
                if not ends:
                    norm_rows(s + NT, i % 2, i)

            for p in range(NT):
                norm_rows(p, p % 2, p)
                if p >= 1:
                    gain_qk(p - 1, 0, p - 1, 5 + (p - 1) % 2)
            for i in range(NT):
                step(0, i, 0, first=True)
            with dve.Fori(0, (LAST - 1) // 2) as pair:
                h = pair * 2 + 1
                for par in (1, 0):
                    for i in range(NT):
                        step(h + (1 - par), i, par)
            for i in range(NT):
                step(LAST, i, 1, ends=True)
            copy_probs(NH * NT - 1, NT - 1, 4 * NH - 1)

            def add(t):
                for h in range(2):
                    n = 2 * t + h
                    dve.wait_ge(out_products, n + 1)
                    xt = c.x[:, t, h * BANK:(h + 1) * BANK]
                    dve.tensor_tensor(xt, xt, c.ps[:, n % 4, :], ALU.add).then_inc(x_added, 1)

            for t in range(NT + 1):
                if t < NT:
                    add(t)
                if t >= 1:
                    norm.dve_evacuate(dve, t - 1)
                if t < NT:
                    norm.dve_var(dve, t)

        @block.tensor
        def _(pe):
            def turn_latents(t):
                pe.wait_ge(lat_scaled, min(3 * t + 4, 3 * NT))
                for g, (k0, n) in enumerate(((0, KQ), (KQ, KKV))):
                    wait(pe, latT_ready, 2 * t + g - 1)
                    for j in range(n):
                        last = pe.transpose(c.ps[:, 5 + g, j * P:(j + 1) * P],
                                            lat_rows[:, t % 2, (k0 + j) * P:(k0 + j + 1) * P], c.ident[:, :])
                    last.then_inc(lat_turned, 1)

            pe.wait_ge(lat_w_loaded, 16)
            for t in range(NT + 1):
                if t < NT:
                    wait(pe, lat_scaled, 3 * t - 2 if t >= 2 else 0)
                    a, b = 2 * (t % 2), 2 * (t % 2) + 1
                    for bank, m0, m1 in ((a, 0, QL), (b, QL, LAT)):
                        for k in range(KD):
                            last = pe.matmul(c.ps[:, bank, 0:m1 - m0], c.hT[:, k, t * P:(t + 1) * P],
                                             w_lat[:, k, m0:m1], start=(k == 0), stop=(k == KD - 1))
                        last.then_inc(lat_products, 1)
                if t >= 1:
                    turn_latents(t - 1)

            def up(p, h, i):
                wait(pe, raw_copied, p)
                lat_cols = slice(i * P, (i + 1) * P)
                wq = w_q.rearrange("p k (h m) -> p k h m", h=NH)
                wkv = w_kv.rearrange("p k (h m) -> p k h m", h=NH)
                for k in range(KQ):
                    pe.matmul(c.ps[:, 4, 0:QD], latT[:, k, lat_cols],
                              wq[:, k, bass.ds(h, 1), :].rearrange("p a m -> p (a m)"),
                              start=(k == 0), stop=(k == KQ - 1))
                for k in range(KKV):
                    last = pe.matmul(c.ps[:, 4, QD:QD + NOPE + VD], latT[:, KQ + k, lat_cols],
                                     wkv[:, k, bass.ds(h, 1), :].rearrange("p a m -> p (a m)"),
                                     start=(k == 0), stop=(k == KKV - 1))
                last.then_inc(up_products, 1)

            def turn_qk(p, slot, bank):
                pe.wait_ge(rows_ready, p + 1)
                rows = q_k_rows[:, slot, :]
                for j in range(2):
                    pe.transpose(c.ps[:, bank, j * P:(j + 1) * P], rows[:, j * NOPE:(j + 1) * NOPE], c.ident[:, :])
                for j in range(2):
                    at = 2 * NOPE + j * ROPE
                    last = pe.transpose(c.ps[0:ROPE, bank, (2 + j) * P:(3 + j) * P], rows[:, at:at + ROPE], c.ident[:, :])
                last.then_inc(qk_turned, 1)

            def score(s, h, par, i, slot):
                wait(pe, exps, s - 1)
                if i == 0:
                    pe.wait_ge(qkT_ready, s + NT)
                    pe.wait_ge(ropeT_ready, s + NT)
                q = slice(i * P, (i + 1) * P)
                for half in range(2):
                    keys = slice(half * BANK, (half + 1) * BANK)
                    pe.matmul(c.ps[:, 2 * slot + half, :], qkT[:, par, 0, q], qkT[:, par, 1, keys],
                              start=True, stop=False)
                    last = pe.matmul(c.ps[:, 2 * slot + half, :], ropeT[0:ROPE, par, 0, q], ropeT[0:ROPE, par, 1, keys],
                                     start=False, stop=True)
                last.then_inc(scores, 1)

            def turn_probs(s, i):
                pe.wait_ge(probs_ready, s + 1)
                for g in range(2):
                    wait(pe, probsT_ready[1 - g], s)
                    for j in range(4):
                        kt = 4 * g + j
                        last = pe.transpose(c.ps[:, PROB_BANKS[i % 2][g], j * P:(j + 1) * P],
                                            probs[:, i % 2, kt * P:(kt + 1) * P], c.ident[:, :])
                    last.then_inc(probs_turned[g], 1)

            def weigh(q, h, par, j):
                pe.wait_ge(v_copied, NT * h + NT)
                for g in range(2):
                    pe.wait_ge(probsT_ready[g], 2 * q + 2)
                wait(pe, pair_copied, q)
                for kt in range(NT):
                    last = pe.matmul(c.ps[:, 7, 0:2 * P], v[:, par, kt, :], probsT[:, j % 2, kt, :],
                                     start=(kt == 0), stop=(kt == NT - 1))
                last.then_inc(pair_products, 1)

            def step(h, i, par, first=False, ends=False):
                s = h * NT + i

                def turn_last():
                    if i == 0 or not ends:
                        p = s + NT - 1
                        if first and i == 0:
                            pe.wait_ge(qkT_ready, p)
                            pe.wait_ge(ropeT_ready, p)
                        else:
                            wait(pe, probsT_ready[0], s - 1)
                        turn_qk(p, (i + 1) % 2, 5 + i % 2)

                if i == 0:
                    turn_last()
                score(s, h, par, i, i % 2)
                if i > 0:
                    turn_last()
                if not ends:
                    up(s + NT, h + 1, i)
                if not (first and i == 0):
                    n = NH * NT if ends else s + NT
                    pe.wait_ge(qkT_ready, n)
                    pe.wait_ge(ropeT_ready, n)
                    turn_probs(s - 1, (i - 1) % NT)
                    if i % 2 == 0:
                        weigh(4 * h + i // 2 - 1, h if i else h - 1, par if i else 1 - par, (i // 2 - 1) % 4)

            pe.wait_ge(up_w_loaded, 32)
            pe.wait_ge(latT_ready, 2 * NT)
            for p in range(NT):
                up(p, 0, p)
                if p >= 1:
                    wait(pe, qkT_ready, p - 2)
                    wait(pe, ropeT_ready, p - 2)
                    turn_qk(p - 1, (p - 1) % 2, 5 + (p - 1) % 2)
            for i in range(NT):
                step(0, i, 0, first=True)
            with pe.Fori(0, (LAST - 1) // 2) as pair:
                h = pair * 2 + 1
                for par in (1, 0):
                    for i in range(NT):
                        step(h + (1 - par), i, par)
            for i in range(NT):
                step(LAST, i, 1, ends=True)
            turn_probs(NH * NT - 1, NT - 1)
            weigh(4 * NH - 1, LAST, 1, 3)
            pe.wait_ge(out_w_loaded, 16)
            pe.wait_ge(pair_copied, 4 * NH)
            for t in range(NT + 1):
                if t < NT:
                    for h in range(2):
                        n = 2 * t + h
                        wait(pe, x_added, n - 3)
                        for k in range(KD):
                            last = pe.matmul(c.ps[:, n % 4, :], oT[:, k, t * P:(t + 1) * P],
                                             w_out[:, k, h * BANK:(h + 1) * BANK],
                                             start=(k == 0), stop=(k == KD - 1))
                        last.then_inc(out_products, 1)
                if t >= 1:
                    norm.pe_turn(pe, t - 1)
                    norm.pe_route(pe, t - 1)

    sems.clear()


def build_trunk(nc, ins, out):
    with ExitStack() as ctx:
        ctx.enter_context(nc.allow_non_contiguous_dma(reason="gains of a few KiB, one to a partition"))
        c = Core(nc, ins, out, ctx)
        conv_phase(c)
        moe_phase(c, 0, last=False)
        attention_phase(c)
        moe_phase(c, 1, last=True)


NAMES = ["x", "positions", "conv_norm_w", "conv_w_in", "conv_k", "conv_w_out", "mla_norm_w", "mla_w_down",
         "mla_q_lat_norm", "mla_kv_lat_norm", "mla_w_q_up", "mla_w_kv_up", "mla_q_head_norm", "mla_k_head_norm",
         "mla_w_out", "ffn_norm_w", "router_w_group", "router_b_group", "router_w_expert", "router_b_expert",
         "exp_w_gate", "exp_w_up", "exp_w_down"]


def kernel(**inputs):
    import concourse.bacc as bacc
    from concourse.bass_utils import run_bass_kernel_spmd

    nc = bacc.Bacc("TRN2", target_bir_lowering=False, num_devices=1)
    arrays, aps = {}, {}
    for name in NAMES:
        a = np.ascontiguousarray(inputs[name])
        arrays[f"in_{name}"] = a
        aps[name] = nc.dram_tensor(f"in_{name}", a.shape, mybir.dt.from_np(a.dtype), kind="ExternalInput").ap()
    out = nc.dram_tensor("out", inputs["x"].shape, F32, kind="ExternalOutput").ap()
    build_trunk(nc, aps, out)
    result = run_bass_kernel_spmd(nc, [arrays], core_ids=[0])
    return result.results[0]["out"]
```

```python
from contextlib import ExitStack

import numpy as np

import concourse.bass as bass
from concourse import mybir

F32 = mybir.dt.float32
I32 = mybir.dt.int32
F32R = mybir.dt.float32r
ALU = mybir.AluOpType
ACT = mybir.ActivationFunctionType
X = mybir.AxisListType.X

P = 128
D, S = 1024, 1024
KD = D // P
NT = S // P
EPS = 1e-6
BANK = 512
NE, NG, EG = 64, 8, 8
NL = NG + NE
FF = 384
KF = FF // P
RANKS = 64
MAXR = 2 * S // RANKS
NH, NOPE, ROPE, VD = 8, 128, 64, 128
QD = NOPE + ROPE
QL, KVL = 384, 256
LAT = QL + KVL + ROPE
KQ, KKV = QL // P, KVL // P
AHEAD = 2


def wait(eng, sem, value):
    if isinstance(value, int) and value <= 0:
        return
    eng.wait_ge(sem, value)


class Chain:

    def __init__(self, eng, sem):
        self.eng, self.sem, self.base, self.n = eng, sem, 0, 0

    def at(self, base):
        self.base, self.n = base, 0

    def mark(self, ins):
        ins.then_inc(self.sem, 1)
        self.n += 1

    def sync(self, ins=None):
        if ins is not None:
            self.mark(ins)
        self.eng.wait_ge(self.sem, self.base + self.n)


class Core:

    def __init__(self, nc, ins, out, ctx):
        self.nc, self.ins, self.out = nc, ins, out

        def sb(name, shape, dt=F32):
            return ctx.enter_context(nc.sbuf_tensor(name, shape, dt))

        self.x = sb("x", [P, NT, D])
        self.hT = sb("hT", [P, KD, S])
        self.rows = sb("rows", [P, 4, D])
        self.turned = sb("turned", [P, 2, KD, P])
        self.logits = sb("logits", [P, NT, NL])
        self.w_router = sb("w_router", [P, KD, NL])
        self.ident = sb("ident", [P, P])
        self.before = sb("before", [P, P])
        self.ones = sb("ones", [P, P])
        self.rank_of_col = sb("rank_of_col", [P, 2, RANKS])
        self.code = sb("code", [P, 2, NT])
        self.from_last = sb("from_last", [P, EG])
        self.round_start = sb("round_start", [P, MAXR])
        self.upper_half = sb("upper_half", [P, 1])
        self.minus_half = sb("minus_half", [P, 2])
        self.sumsq = sb("sumsq", [P, NT])
        self.var = sb("var", [P, NT])
        self.rstd = sb("rstd", [P, NT])
        self.norm_w = sb("norm_w", [P, 4, KD])
        self.xw = sb("xw", [P, 2, 4, 2])
        self.gather_idx = sb("gather_idx", [P, NE], I32)
        self.scatter_idx = sb("scatter_idx", [P, NE], I32)
        self.col_idx = sb("col_idx", [P, 4, 1], I32)
        self.n_rounds = sb("n_rounds", [P, 1], I32)
        self.pos_i = sb("pos_i", [P, NT], I32)
        self.arena_words = 28300
        self.arena_at = -(-nc.sbuf_base // 32) * 32
        self.arena = sb("arena", [P, self.arena_words])
        self.route_words = 2900
        piece = self.carve(self.arena[:, self.arena_words - self.route_words:])
        self.chosen = piece(2, NT, NE)
        self.coded = piece(2, NT, NE)
        self.earlier = piece(NT + 1, NE)
        self.route_big = piece(3, NE)
        self.route_small = piece(8, EG)
        self.route_tiny = piece(8)
        self.whole_arena = self.arena[:, :]
        self.arena_words -= self.route_words
        self.exps = sb("exps", [P, 2, NT, EG])
        self.picked = sb("picked", [P, 3, NT, EG])
        self.bias = sb("bias", [P, NL])
        self.ps = ctx.enter_context(nc.psum_tensor("ps", [P, 8, BANK], F32))
        self.h_rows = nc.dram_tensor("h_rows", [S, D], F32, kind="Internal").ap()
        self.y_rows = nc.dram_tensor("y_rows", [2 * S, D], F32, kind="Internal").ap()

    def typed(self, name, at, shape, dt):
        t = self.nc.alloc_sbuf_tensor_at(name, shape, dt, offset=self.arena_at + 4 * at)
        return t[tuple(slice(None) for _ in shape)]

    def carve(self, place=None):
        at = [0]
        place = self.arena[:, 0:self.arena_words] if place is None else place
        words = place.shape[1]

        def piece(*shape):
            n = int(np.prod(shape))
            a = place[:, at[0]:at[0] + n]
            at[0] += n
            assert at[0] <= words, (at[0], words)
            if len(shape) == 2:
                a = a.rearrange("p (a b) -> p a b", b=shape[1])
            elif len(shape) == 3:
                a = a.rearrange("p (a b c) -> p a b c", b=shape[1], c=shape[2])
            elif len(shape) == 4:
                a = a.rearrange("p (a b c d) -> p a b c d", b=shape[1], c=shape[2], d=shape[3])
            return a

        piece.at = at
        return piece


def bc(ap, axis, n):
    a = ap.unsqueeze(axis)
    shape = list(a.shape)
    shape[axis] = n
    return a.broadcast_to(shape)


class Sems:

    def __init__(self, nc, tag):
        self.nc, self.tag, self.all = nc, tag, []

    def __call__(self, name):
        s = self.nc.alloc_semaphore(f"{self.tag}_{name}")
        self.all.append(s)
        return s

    def clear(self):
        self.nc.clear_and_free_semaphores(self.all)
        self.nc.all_engine_barrier()


class Norm:

    def __init__(self, c, sems, which, route, banks, logit_bank=None, split=None):
        self.split = split
        self.c, self.w, self.route, self.banks, self.logit_bank = c, which, route, banks, logit_bank
        named = sems

        def sems(name):
            return named(f"{name}_{which}")

        self.squares = sems("norm_squares")
        self.var_ready = sems("norm_var_ready")
        self.rstd_ready = sems("norm_rstd_ready")
        self.rows_ready = sems("norm_rows_ready")
        self.turns = sems("norm_turns")
        self.evacuated = sems("norm_evacuated")
        self.high_ready = sems("norm_high_ready")
        if route:
            self.logits_ready = sems("norm_logits_ready")
            self.logits_copied = sems("norm_logits_copied")
            self.route_step = sems("norm_route_step")
            self.rows_stored = [sems(f"norm_rows_stored{i}") for i in range(4)]

    def act_squares(self, act, t):
        c = self.c
        if t >= 4:
            act.wait_ge(self.turns, 2 * (t - 3))
            if self.route:
                act.wait_ge(self.rows_stored[t % 4], 16 * (t // 4))
        act.activation(c.rows[:, t % 4, :], c.x[:, t, :], ACT.Square,
                       accum_out=c.sumsq[:, t:t + 1]).then_inc(self.squares, 1)

    def dve_var(self, dve, t):
        c = self.c
        dve.wait_ge(self.squares, t + 1)
        dve.tensor_scalar(c.var[:, t:t + 1], c.sumsq[:, t:t + 1], 1.0 / D, EPS,
                          ALU.mult, ALU.add).then_inc(self.var_ready, 1)

    def pool_rstd(self, pool, t):
        c = self.c
        pool.wait_ge(self.var_ready, t + 1)
        pool.tensor_tensor(c.rstd[:, t:t + 1], c.var[:, t:t + 1], c.minus_half[:, 0:1],
                           ALU.pow).then_inc(self.rstd_ready, 1)

    def act_rows(self, act, t):
        c = self.c
        act.wait_ge(self.rstd_ready, t + 1)
        act.activation(c.rows[:, t % 4, :], c.x[:, t, :], ACT.Copy,
                       scale=c.rstd[:, t:t + 1]).then_inc(self.rows_ready, 1)

    def sp_store(self, sp, t):
        c = self.c
        sp.wait_ge(self.rows_ready, t + 1)
        sp.dma_start(c.h_rows[t * P:(t + 1) * P, :], c.rows[:, t % 4, :]).then_inc(self.rows_stored[t % 4], 16)

    def pe_turn(self, pe, t):
        c = self.c
        pe.wait_ge(self.rows_ready, t + 1)
        for g in range(2):
            n = 2 * t + g
            wait(pe, self.evacuated, n - 1)
            for j in range(4):
                k = 4 * g + j
                ins = pe.transpose(c.ps[:, self.banks[g], j * P:(j + 1) * P],
                                   c.rows[:, t % 4, k * P:(k + 1) * P], c.ident[:, :])
            ins.then_inc(self.turns, 1)

    def dve_evacuate(self, dve, t):
        if self.split is not None:
            return self.dve_evacuate_split(dve, t)
        c = self.c
        for g in range(2):
            dve.wait_ge(self.turns, 2 * t + g + 1)
            if self.route:
                if g == 0:
                    wait(dve, self.logits_ready, t - 1)
                out = c.turned[:, t % 2, 4 * g:4 * g + 4, :]
            else:
                out = c.hT[:, 4 * g:4 * g + 4, t * P:(t + 1) * P]
            dve.tensor_tensor(out, c.ps[:, self.banks[g], :].rearrange("p (a b) -> p a b", b=P),
                              bc(c.norm_w[:, self.w, 4 * g:4 * g + 4], 2, P),
                              ALU.mult).then_inc(self.evacuated, 1)

    def dve_evacuate_split(self, dve, t):
        c = self.c
        cols = slice(t * P, (t + 1) * P)
        for g in range(2):
            dve.wait_ge(self.turns, 2 * t + g + 1)
            dve.tensor_tensor(self.split[:, 0, 4 * g:4 * g + 4, cols],
                              c.ps[:, self.banks[g], :].rearrange("p (a b) -> p a b", b=P),
                              bc(c.norm_w[:, self.w, 4 * g:4 * g + 4], 2, P), ALU.mult).then_inc(self.high_ready, 1)
        for g in range(2):
            dve.wait_ge(self.high_ready, 2 * t + g + 1)
            for j in range(4):
                k = 4 * g + j
                ins = dve.scalar_tensor_tensor(out=self.split[:, 1, k, cols], in0=c.ps[:, self.banks[g], j * P:(j + 1) * P],
                                               scalar=c.norm_w[:, self.w, k:k + 1], in1=self.split[:, 0, k, cols],
                                               op0=ALU.mult, op1=ALU.subtract)
            ins.then_inc(self.evacuated, 1)

    def pe_route(self, pe, t):
        c = self.c
        pe.wait_ge(self.evacuated, 2 * t + 2)
        wait(pe, self.logits_copied, t)
        at = (t % 2) * P
        for k in range(KD):
            ins = pe.matmul(c.ps[:, self.logit_bank, at:at + NL], c.turned[:, t % 2, k, :],
                            c.w_router[:, k, :], start=(k == 0), stop=(k == KD - 1))
        ins.then_inc(self.logits_ready, 1)

    def act_logits(self, act, t):
        c = self.c
        act.wait_ge(self.logits_ready, t + 1)
        at = (t % 2) * P
        act.activation(c.logits[:, t, :], c.ps[:, self.logit_bank, at:at + NL],
                       ACT.Copy).then_inc(self.logits_copied, 1)


    def dve_route(self, dve, t):
        c = self.c
        step = Chain(dve, self.route_step)
        step.at(t * self.ROUTE_STEPS)
        lg = c.logits[:, t, 0:NG]
        le = c.logits[:, t, NG:NL].rearrange("p (g j) -> p g j", j=EG)
        big = [c.route_big[:, i, :].rearrange("p (g j) -> p g j", j=EG) for i in range(3)]
        small = [c.route_small[:, i, :] for i in range(8)]
        tiny = [c.route_tiny[:, i:i + 1] for i in range(8)]
        group, first, second = (c.picked[:, i, t, :] for i in range(3))

        def tt(out, a, b, op, wait_=True):
            step.mark(dve.tensor_tensor(out, a, b, op))
            if wait_:
                step.sync()

        def reduce(out, a, op, wait_=True):
            step.mark(dve.tensor_reduce(out, a, X, op))
            if wait_:
                step.sync()

        def first_largest(out, values, s, m):
            reduce(m, values, ALU.max)
            step.sync(dve.scalar_tensor_tensor(out=s, in0=values, scalar=m, in1=c.from_last[:, :],
                                               op0=ALU.is_equal, op1=ALU.mult))
            reduce(m, s, ALU.max)
            step.sync(dve.tensor_scalar(out, s, m, None, ALU.is_equal))

        dve.wait_ge(self.logits_copied, t + 1)
        wait(dve, self.route_step, t * self.ROUTE_STEPS)
        reduce(tiny[0], lg, ALU.max, False)
        tt(small[0], lg, c.bias[:, 0:NG], ALU.add)
        first_largest(group, small[0], small[1], tiny[1])
        tt(big[0], le, bc(group, 2, EG), ALU.mult, False)
        tt(big[1], bc(group, 2, EG), c.bias[:, NG:NL].rearrange("p (g j) -> p g j", j=EG), ALU.mult)
        reduce(small[2], big[0].rearrange("p g j -> p j g"), ALU.add, False)
        reduce(small[3], big[1].rearrange("p g j -> p j g"), ALU.add, False)
        step.mark(dve.tensor_scalar(c.exps[:, 0, t, :], lg, tiny[0], None, ALU.subtract))
        step.sync()
        tt(small[4], small[2], small[3], ALU.add, False)
        reduce(tiny[2], small[2], ALU.max)
        step.mark(dve.tensor_scalar(c.exps[:, 1, t, :], small[2], tiny[2], None, ALU.subtract))
        first_largest(first, small[4], small[5], tiny[3])
        step.sync(dve.scalar_tensor_tensor(out=small[6], in0=first, scalar=-1e30, in1=small[4],
                                           op0=ALU.mult, op1=ALU.add))
        first_largest(second, small[6], small[7], tiny[4])
        for k, pick in enumerate((first, second)):
            tt(c.chosen[:, k, t, :].rearrange("p (g j) -> p g j", j=EG), bc(group, 2, EG), bc(pick, 1, NG),
               ALU.mult, False)
        step.sync()
        tt(c.route_big[:, 2, :], c.chosen[:, 0, t, :], c.chosen[:, 1, t, :], ALU.add, False)
        for k in range(2):
            step.mark(dve.tensor_scalar(c.coded[:, k, t, :], c.chosen[:, k, t, :], c.code[:, k, t:t + 1], None,
                                        ALU.mult))
        step.sync()
        tt(c.earlier[:, t + 1, :], c.earlier[:, t, :], c.route_big[:, 2, :], ALU.add)
        assert step.n == self.ROUTE_STEPS, step.n

    ROUTE_STEPS = 29


def load_router(eng, c, layer, sem):
    eng.dma_start(c.bias[:, 0:NG], c.ins["router_b_group"][layer].partition_broadcast(P)).then_inc(sem, 16)
    eng.dma_start(c.bias[:, NG:NL], c.ins["router_b_expert"][layer].partition_broadcast(P)).then_inc(sem, 16)
    eng.dma_start(c.w_router[:, :, 0:NG],
                  c.ins["router_w_group"][layer].rearrange("(k p) g -> p k g", p=P)).then_inc(sem, 16)
    eng.dma_start(c.w_router[:, :, NG:NL],
                  c.ins["router_w_expert"][layer].rearrange("(k p) e -> p k e", p=P)).then_inc(sem, 16)


def conv_phase(c):
    nc, ins = c.nc, c.ins
    sems = Sems(nc, "conv")
    HIGH, LOW = 0, 1
    PARTS = ((HIGH, HIGH), (HIGH, LOW), (LOW, HIGH))
    hT_split = c.typed("hT_split", 0, [P, 2, KD, S], F32R)
    w_split = c.typed("w_split", 2 * KD * S, [P, 3, 2, KD, P], F32R)
    piece = c.carve(c.whole_arena[:, 2 * KD * S + 6 * KD * P:])
    w_raw = piece(2, KD, P)
    taps = piece(KD, 3)
    w_out_high = hT_split[:, :, :, BANK:]
    w_out_low = c.typed("w_out_low", 2 * KD * S, [P, 2, KD, BANK], F32R)
    y_split = hT_split[:, HIGH, :, 0:BANK].rearrange("p k (i a m) -> p i a k m", i=2, a=2)
    w_out = c.arena[:, 0:2 * KD * S].rearrange("p (h k s) -> p h k s", h=2, s=S)[:, :, :, 0:BANK]
    yT = c.hT
    piece = c.carve(c.rows[:, :, :].rearrange("p a d -> p (a d)"))
    z = piece(S + 2)
    acc = piece(S)
    gb = piece(S)
    gc = c.turned[:, 0, :, :].rearrange("p k m -> p (k m)").rearrange("p (h m) -> p h m", h=2)
    HT = S // BANK
    UNITS = 3 * KD

    x_loaded = [sems(f"x_loaded{t}") for t in range(NT)]
    w_raw_loaded = [sems(f"w_raw_loaded{i}") for i in range(2)]
    w_high_ready = sems("w_high_ready")
    w_low_ready = sems("w_low_ready")
    unit_used = [sems(f"unit_used{j}") for j in range(2)]
    w_out_loaded = [sems(f"w_out_loaded{h}") for h in range(2)]
    w_out_high_ready = sems("w_out_high_ready")
    w_out_low_ready = [sems(f"w_out_low_ready{h}") for h in range(2)]
    y_high_ready = sems("y_high_ready")
    y_low_ready = sems("y_low_ready")
    gain_loaded = sems("gain_loaded")
    small_loaded = sems("small_loaded")
    consts = sems("consts")
    z_edges = sems("z_edges")
    products = sems("products")
    g_copied = sems("g_copied")
    z_half = sems("z_half")
    conv_step = sems("conv_step")
    y_ready = sems("y_ready")
    out_products = sems("out_products")
    x_added = sems("x_added")
    earlier_cleared = sems("earlier_cleared")
    norm0 = Norm(c, sems, 0, False, (6, 7), split=hT_split)
    norm1 = Norm(c, sems, 1, True, (6, 7), logit_bank=5)
    w_in_dram = ins["conv_w_in"][0].rearrange("(k p) (j c m) -> p k j c m", p=P, j=3, m=P)

    def low_w_out(eng, h):
        for q in range(2):
            eng.wait_ge(w_out_high_ready, 2 * h + q + 1)
            ks = slice(4 * q, 4 * q + 4)
            eng.tensor_tensor(w_out_low[:, h, ks, :], w_out[:, h, ks, :], w_out_high[:, h, ks, :],
                              ALU.subtract).then_inc(w_out_low_ready[h], 1)

    with nc.Block() as block:

        @block.sync
        def _(sp):
            def gain(i, name, row):
                sp.dma_start(c.norm_w[:, i, :], ins[name][row].rearrange("(k p) -> p k", p=P)).then_inc(
                    gain_loaded if i == 0 else small_loaded, 16)

            gain(0, "conv_norm_w", 0)
            for t in range(NT):
                sp.dma_start(c.x[:, t, :], ins["x"][0, t * P:(t + 1) * P, :]).then_inc(x_loaded[t], 16)

            def load_unit(ct, j, slot):
                sp.dma_start(w_raw[:, slot, :, :], w_in_dram[:, :, j, bass.ds(ct, 1), :]
                             .rearrange("p k a m -> p (k a) m")).then_inc(w_raw_loaded[slot], 16)

            load_unit(0, 0, 0)
            load_unit(0, 1, 1)
            for j in range(3):
                sp.dma_start(taps[:, :, j], ins["conv_k"][0, j].rearrange("(k p) -> p k", p=P)).then_inc(small_loaded, 16)
            gain(1, "ffn_norm_w", 0)
            gain(2, "mla_norm_w", 0)
            gain(3, "ffn_norm_w", 1)
            for layer in range(2):
                for half in range(2):
                    sp.dma_start(c.xw[:, layer, :, half],
                                 ins["ffn_norm_w"][layer, half * BANK:(half + 1) * BANK]
                                 .rearrange("(p j) -> p j", j=4)).then_inc(small_loaded, 16)
            load_router(sp, c, 0, small_loaded)

            def load_units(pair, n):
                for v in range(n):
                    sp.wait_ge(w_low_ready, 6 * pair + v + 1)
                    load_unit(2 * pair + (v + 2) // 3, (v + 2) % 3, v % 2)

            with sp.Fori(0, KD // 2 - 1) as pair:
                load_units(pair, 6)
            load_units(KD // 2 - 1, 4)
            sp.wait_ge(products, HT * KD - 1)
            for h in range(2):
                sp.dma_start(w_out[:, h, :, :], ins["conv_w_out"][0].rearrange("(k p) (h d) -> h p k d", p=P, h=2)[h]
                             ).then_inc(w_out_loaded[h], 16)
            for t in range(NT):
                norm1.sp_store(sp, t)
            for t in range(4):
                sp.wait_ge(norm1.rows_stored[t], 16 * NT // 4)

        @block.gpsimd
        def _(pool):
            step = Chain(pool, consts)
            step.mark(pool.memset(c.ident[:, :], 0.0))
            step.mark(pool.memset(c.ones[:, :], 1.0))
            step.mark(pool.memset(c.before[:, :], 1.0))
            step.mark(pool.memset(c.minus_half[:, :], -0.5))
            step.mark(pool.memset(c.upper_half[:, :], -1.0))
            step.mark(pool.iota(c.rank_of_col[:, :, :], [[0, 2], [1, RANKS]], base=0, channel_multiplier=0,
                                allow_small_or_imprecise_dtypes=True))
            step.mark(pool.iota(c.code[:, :, :], [[S, 2], [P, NT]], base=1, channel_multiplier=1,
                                allow_small_or_imprecise_dtypes=True))
            step.mark(pool.iota(c.from_last[:, :], [[-1, EG]], base=EG, channel_multiplier=0,
                                allow_small_or_imprecise_dtypes=True))
            step.mark(pool.iota(c.round_start[:, :], [[RANKS, MAXR]], base=0, channel_multiplier=0,
                                allow_small_or_imprecise_dtypes=True))
            step.sync()
            step.mark(pool.affine_select(out=c.ident[:, :], in_=c.ident[:, :], compare_op=ALU.not_equal, fill=1.0,
                                         base=0, pattern=[[-1, P]], channel_multiplier=1))
            step.mark(pool.affine_select(out=c.before[:, :], in_=c.before[:, :], compare_op=ALU.is_gt, fill=0.0,
                                         base=0, pattern=[[1, P]], channel_multiplier=-1))
            step.mark(pool.affine_select(out=c.upper_half[:, :], in_=c.upper_half[:, :], compare_op=ALU.is_ge,
                                         fill=-2.0, base=-RANKS, pattern=[[0, 1]], channel_multiplier=1))

            def low_part(u, j, slot):
                pool.wait_ge(w_high_ready, u + 1)
                pool.tensor_tensor(w_split[:, j, LOW, :, :], w_raw[:, slot, :, :], w_split[:, j, HIGH, :, :],
                                   ALU.subtract).then_inc(w_low_ready, 1)

            for t in range(NT - 1):
                norm0.pool_rstd(pool, t)
            low_part(0, 0, 0)
            low_part(1, 1, 1)
            norm0.pool_rstd(pool, NT - 1)
            for u in range(2, 6):
                low_part(u, u % 3, u % 2)
            with pool.Fori(1, KD // 2) as pair:
                for v in range(6):
                    low_part(pair * 6 + v, v % 3, v % 2)
            low_w_out(pool, 1)

            def low_y(t):
                pool.wait_ge(y_high_ready, t)
                pool.tensor_tensor(y_split[:, t % 2, LOW], yT[:, :, t * P:(t + 1) * P], y_split[:, t % 2, HIGH],
                                   ALU.subtract).then_inc(y_low_ready, 1)

            low_y(1)
            for t in range(NT):
                if t + 2 < NT:
                    low_y(t + 2)
                norm1.pool_rstd(pool, t)

        N_CONST = 12

        @block.scalar
        def _(act):
            def high_part(pair, v):
                j, ct = v % 3, 2 * pair + v // 3
                act.wait_ge(w_raw_loaded[v % 2], 48 * pair + 16 * (v // 2 + 1))
                if j < 2:
                    wait(act, unit_used[j], ct)
                else:
                    wait(act, products, HT * ct)
                act.activation(w_split[:, j, HIGH, :, :], w_raw[:, v % 2, :, :], ACT.Copy).then_inc(w_high_ready, 1)

            for t in range(NT + 2):
                if t < NT:
                    act.wait_ge(x_loaded[t], 16)
                    norm0.act_squares(act, t)
                if t >= 2:
                    norm0.act_rows(act, t - 2)
                if t == NT - 2:
                    high_part(0, 0)
                    high_part(0, 1)

            def copies(pair, i, ends=False):
                ct = 2 * pair + i
                for h in range(HT):
                    n = HT * ct + h
                    act.wait_ge(products, n + 1)
                    wait(act, z_half, n - 1)
                    act.activation(gc[:, h, :], c.ps[:, 3 * h + 1, :], ACT.Copy).then_inc(g_copied, 1)
                    wait(act, y_ready, ct)
                    act.activation(gb[:, h * BANK:(h + 1) * BANK], c.ps[:, 3 * h, :], ACT.Copy).then_inc(g_copied, 1)
                    if not ends:
                        for j in ((0, 1), (2,))[h]:
                            high_part(pair + i, 3 * (1 - i) + j)

            high_part(0, 2)
            act.wait_ge(norm0.turns, 2 * NT)
            copies(0, 0)
            copies(0, 1)
            with act.Fori(1, KD // 2 - 1) as pair:
                for i in range(2):
                    copies(pair, i)
            copies(KD // 2 - 1, 0)
            copies(KD // 2 - 1, 1, ends=True)
            for h in range(2):
                act.wait_ge(w_out_loaded[h], 16)
                for q in range(2):
                    ks = slice(4 * q, 4 * q + 4)
                    act.activation(w_out_high[:, h, ks, :], w_out[:, h, ks, :], ACT.Copy).then_inc(w_out_high_ready, 1)

            def high_y(t):
                act.wait_ge(out_products, max(1, 2 * t - 2))
                act.activation(y_split[:, t % 2, HIGH], yT[:, :, t * P:(t + 1) * P], ACT.Copy).then_inc(y_high_ready, 1)

            act.wait_ge(w_out_low_ready[0], 2)
            high_y(1)
            for t in range(NT + 2):
                if t + 2 < NT:
                    high_y(t + 2)
                if t < NT:
                    act.wait_ge(x_added, 2 * t + 2)
                    norm1.act_squares(act, t)
                    norm1.act_rows(act, t)
                if t >= 2:
                    norm1.act_logits(act, t - 2)

        @block.vector
        def _(dve):
            dve.wait_ge(gain_loaded, 16)
            for t in range(NT + 3):
                if t < NT:
                    norm0.dve_var(dve, t)
                if t >= 3:
                    norm0.dve_evacuate(dve, t - 3)
            dve.memset(z[:, 0:1], 0.0).then_inc(z_edges, 1)
            dve.memset(z[:, S + 1:S + 2], 0.0).then_inc(z_edges, 1)
            dve.wait_ge(z_edges, 2)
            dve.wait_ge(small_loaded, 16 * 14)
            step = Chain(dve, conv_step)

            def conv_tile(ct, i):
                step.at((ct + i) * 3)
                for h in range(HT):
                    n = HT * (ct + i) + h
                    dve.wait_ge(g_copied, 2 * n + 1)
                    dve.tensor_tensor(z[:, 1 + h * BANK:1 + (h + 1) * BANK], gc[:, h, :],
                                      c.ps[:, 3 * h + 2, :], ALU.mult).then_inc(z_half, 1)
                dve.wait_ge(z_half, HT * (ct + i) + HT)
                tap = taps[:, bass.ds(ct + i, 1), :].rearrange("p a j -> p (a j)")
                step.sync(dve.tensor_scalar(acc, z[:, 0:S], tap[:, 0:1], None, ALU.mult))
                step.sync(dve.scalar_tensor_tensor(out=acc, in0=z[:, 1:S + 1], scalar=tap[:, 1:2], in1=acc,
                                                   op0=ALU.mult, op1=ALU.add))
                step.sync(dve.scalar_tensor_tensor(out=acc, in0=z[:, 2:S + 2], scalar=tap[:, 2:3], in1=acc,
                                                   op0=ALU.mult, op1=ALU.add))
                dve.wait_ge(g_copied, 2 * HT * (ct + i + 1))
                dve.tensor_tensor(yT[:, bass.ds(ct + i, 1), :].rearrange("p a s -> p (a s)"), acc, gb,
                                  ALU.mult).then_inc(y_ready, 1)
                dve.wait_ge(y_ready, ct + i + 1)

            with dve.Fori(0, KD // 2) as pair:
                ct = pair * 2
                for i in range(2):
                    conv_tile(ct, i)

            def add(t):
                for h in range(2):
                    n = 2 * t + h
                    dve.wait_ge(out_products, n + 1)
                    xt = c.x[:, t, h * BANK:(h + 1) * BANK]
                    dve.tensor_tensor(xt, xt, c.ps[:, n % 4, :], ALU.add).then_inc(x_added, 1)

            low_w_out(dve, 0)
            dve.wait_ge(out_products, 1)
            dve.memset(c.earlier[:, 0, :], 0.0).then_inc(earlier_cleared, 1)
            dve.wait_ge(earlier_cleared, 1)
            for t in range(NT + 2):
                if t < NT:
                    add(t)
                if 1 <= t <= NT:
                    norm1.dve_evacuate(dve, t - 1)
                if t < NT:
                    norm1.dve_var(dve, t)
                if t >= 2:
                    norm1.dve_route(dve, t - 2)

        @block.tensor
        def _(pe):
            pe.wait_ge(consts, N_CONST)
            for t in range(NT // 2):
                norm0.pe_turn(pe, t)

            turn_before = {(0, 4): 4, (1, 2): 5, (1, 7): 6, (2, 4): 7}

            def multiply(ct):
                for h in range(HT):
                    n = HT * ct + h
                    wait(pe, z_half, n - 1)
                    wait(pe, g_copied, 2 * (n - 1))
                    if isinstance(n, int) and n < HT:
                        pe.wait_ge(norm0.evacuated, 2 * NT // HT * (n + 1))
                    for j in range(3):
                        if h == 0:
                            pe.wait_ge(w_low_ready, 3 * ct + j + 1)
                        for k in range(KD):
                            if isinstance(n, int) and n == 0 and (j, k) in turn_before:
                                norm0.pe_turn(pe, turn_before[j, k])
                            for a, b in PARTS:
                                last = pe.matmul(c.ps[:, 3 * h + j, :], w_split[:, j, a, k, :],
                                                 hT_split[:, b, k, h * BANK:(h + 1) * BANK],
                                                 start=(k == 0 and a == b), stop=(k == KD - 1 and a == LOW))
                        if h == 1 and j < 2:
                            last.then_inc(unit_used[j], 1)
                    last.then_inc(products, 1)

            multiply(0)
            multiply(1)
            with pe.Fori(1, KD // 2) as pair:
                for i in range(2):
                    multiply(pair * 2 + i)
            def out_product(t, h):
                n = 2 * t + h
                wait(pe, x_added, n - 3)
                if t == 0:
                    pe.wait_ge(w_out_loaded[h], 16)
                    for k in range(KD):
                        if n == 0 and k == KD - 1:
                            pe.wait_ge(y_ready, KD)
                        last = pe.matmul(c.ps[:, n % 4, :], yT[:, k, t * P:(t + 1) * P], w_out[:, h, k, :],
                                         start=(k == 0), stop=(k == KD - 1))
                else:
                    pe.wait_ge(y_low_ready, t)
                    pe.wait_ge(w_out_low_ready[h], 2)
                    for k in range(KD):
                        for a, b in PARTS:
                            w = (w_out_high, w_out_low)[b]
                            last = pe.matmul(c.ps[:, n % 4, :], y_split[:, t % 2, a, k, :], w[:, h, k, :],
                                             start=(k == 0 and a == b), stop=(k == KD - 1 and a == LOW))
                last.then_inc(out_products, 1)

            pe.wait_ge(z_half, HT * KD - 1)
            pe.wait_ge(g_copied, 2 * (HT * KD - 1))
            pe.wait_ge(y_ready, KD - 1)
            pe.wait_ge(small_loaded, 16 * 14)
            for t in range(NT + 2):
                if t < NT:
                    for h in range(2):
                        out_product(t, h)
                if 1 <= t <= NT:
                    norm1.pe_turn(pe, t - 1)
                if t >= 2:
                    norm1.pe_route(pe, t - 2)

    sems.clear()


def moe_phase(c, layer, last):
    nc, ins = c.nc, c.ins
    sems = Sems(nc, f"moe{layer}")
    piece = c.carve()
    w_gate = piece(2, 2, 4 * FF)
    w_up = piece(2, 2, 4 * FF)
    w_down = piece(2, KF, D)
    assert 3 * 2 * D <= piece.at[0]
    gathered = piece(2, BANK)
    xT = piece(2, 4, 2, RANKS)
    gate_up = piece(2, FF)
    silu = piece(2, KF, RANKS)
    hidden = piece(2, KF, RANKS)
    y = piece(2, BANK)
    rank = piece(2, NT)
    gates = piece(2, NT)
    idx_f = piece(4, NE)
    tiny = piece(16, NT)
    piece = c.carve(c.hT[:, :, :].rearrange("p k s -> p (k s)"))
    onehot = piece(2 * NT, P)
    by_rank = piece(NT * NE)
    by_pick = piece(2, NT, EG)
    chosen, coded, earlier = c.chosen, c.coded, c.earlier
    y_pair = c.arena[:, 0:3 * 2 * D].rearrange("p (r k d) -> p r k d", r=3, k=2)

    gather_idx, scatter_idx, col_idx, n_rounds = c.gather_idx, c.scatter_idx, c.col_idx, c.n_rounds
    cleared = sems("cleared")
    w_gate_up_loaded = [sems(f"w_gate_up_loaded{i}") for i in range(2)]
    w_down_loaded = [sems(f"w_down_loaded{i}") for i in range(2)]
    route_step = sems("route_step")
    exp_out = sems("exp_out")
    counted = sems("counted")
    rounds_ready = sems("rounds_ready")
    onehot_ready = sems("onehot_ready")
    idx_products = sems("idx_products")
    idx_ready = sems("idx_ready")
    round_step = sems("round_step")
    pool_step = sems("pool_step")
    rounds_begun = sems("rounds_begun")
    gathers_begun = sems("gathers_begun")
    scatters_begun = sems("scatters_begun")
    gather_done = [sems(f"gather_done{i}") for i in range(2)]
    y_stored = sems("y_stored")
    scatter_done = [sems(f"scatter_done{i}") for i in range(2)]
    x_turned = sems("x_turned")
    xT_ready = sems("xT_ready")
    gate_up_products = sems("gate_up_products")
    gate_up_copied = sems("gate_up_copied")
    h_turned = sems("h_turned")
    silu_ready = sems("silu_ready")
    hidden_ready = sems("hidden_ready")
    y_products = sems("y_products")
    y_copied = sems("y_copied")
    y_pair_loaded = [sems(f"y_pair_loaded{i}") for i in range(3)]
    gates_ready = sems("gates_ready")
    first_scaled = sems("first_scaled")
    summed = sems("summed")
    x_added = sems("x_added")
    stored = sems("stored")
    norm = None if last else Norm(c, sems, 2, False, (0, 1))

    def done(g):
        return g + 1 + AHEAD

    def free(g):
        return g + 1

    gate_dram = ins["exp_w_gate"][layer].rearrange("e (h p j) f -> p e h (j f)", h=2, p=P)
    up_dram = ins["exp_w_up"][layer].rearrange("e (h p j) f -> p e h (j f)", h=2, p=P)
    down_dram = ins["exp_w_down"][layer].rearrange("e (j p) d -> p e j d", p=P)
    h_halves = c.h_rows.rearrange("t (h d) -> (t h) d", h=2)
    y_halves = c.y_rows.rearrange("t (h d) -> (t h) d", h=2)

    def rounds(eng):
        eng.wait_ge(rounds_ready, 1)
        return eng.value_load(n_rounds[0:1, 0:1], min_val=1, max_val=MAXR)

    with nc.Block() as block:

        @block.sync
        def _(sp):
            def load_gate_up(slot, e):
                for w, dram in ((w_gate, gate_dram), (w_up, up_dram)):
                    src = dram[:, bass.ds(e, 1), :, :].rearrange("p a h f -> p (a h) f")
                    sp.dma_start(w[:, slot, :, :], src).then_inc(w_gate_up_loaded[slot], 16)

            def load_down(slot, e):
                src = down_dram[:, bass.ds(e, 1), :, :].rearrange("p a j d -> p (a j) d")
                sp.dma_start(w_down[:, slot, :, :], src).then_inc(w_down_loaded[slot], 16)

            for slot in range(2):
                load_gate_up(slot, slot)
                load_down(slot, slot)
            count = rounds(sp)
            with sp.Fori(1, count * (NE // 2)) as pair:
                g = pair * 2
                for slot in range(2):
                    e = (g + slot) % NE
                    sp.wait_ge(gate_up_products, g + slot + free(0))
                    load_gate_up(slot, e)
                    sp.wait_ge(y_products, g + slot + free(0))
                    load_down(slot, e)
            sp.wait_ge(y_stored, count * NE + AHEAD)
            for t in range(NT):
                if t >= 3:
                    sp.wait_ge(x_added, t - 2)
                src = c.y_rows.rearrange("(k t p) d -> t p k d", k=2, p=P)[t]
                sp.dma_start(y_pair[:, t % 3, :, :], src).then_inc(y_pair_loaded[t % 3], 16)
            if last:
                for t in range(NT):
                    sp.wait_ge(x_added, t + 1)
                    sp.dma_start(c.out[0, t * P:(t + 1) * P, :], c.x[:, t, :]).then_inc(stored, 16)
                sp.wait_ge(stored, 16 * NT)

        @block.gpsimd
        def _(pool):
            pool.memset(gathered, 0.0).then_inc(cleared, 1)
            pool.sem_inc(y_stored, AHEAD)
            pool.wait_ge(cleared, 1)
            count = rounds(pool)
            step = Chain(pool, pool_step)

            def gather(g, e, slot, n):
                pool.wait_ge(x_turned, g + free(0))
                pool.sem_inc(gathers_begun, 1)
                pool.tensor_copy(col_idx[:, slot, :], gather_idx[:, bass.ds(e, 1)]).then_inc(pool_step, 1)
                pool.wait_ge(pool_step, n + 1)
                pool.sem_inc(gathers_begun, 1)
                pool.indirect_dma_start(gathered[:, slot, :], None, h_halves,
                                        bass.IndirectOffsetOnAxis(ap=col_idx[:, slot, :], axis=0),
                                        bounds_check=2 * S - 1, oob_is_err=False).then_inc(gather_done[slot], 16)

            def scatter(g, e, slot, n):
                pool.wait_ge(y_copied, g + done(0))
                pool.sem_inc(scatters_begun, 1)
                pool.tensor_copy(col_idx[:, 2 + slot, :], scatter_idx[:, bass.ds(e, 1)]).then_inc(pool_step, 1)
                pool.wait_ge(pool_step, n + 1)
                pool.sem_inc(scatters_begun, 1)
                pool.indirect_dma_start(y_halves, bass.IndirectOffsetOnAxis(ap=col_idx[:, 2 + slot, :], axis=0),
                                        y[:, slot, :], None,
                                        bounds_check=4 * S - 1, oob_is_err=False).then_inc(scatter_done[slot], 16)

            def complete(g, slot):
                pool.wait_ge(scatter_done[slot], g * 8 + (16 - 8 * slot))
                pool.sem_inc(y_stored, 1)

            with pool.Fori(0, count) as r:
                pool.wait_ge(idx_ready, 2 * r + 2)
                pool.sem_inc(rounds_begun, 1)
                g0, n0 = r * NE, r * (2 * NE)
                for slot in range(2):
                    gather(g0 + slot, slot, slot, n0 + slot)
                with pool.Fori(1, NE // 2) as pair:
                    e = pair * 2
                    for slot in range(2):
                        gather(g0 + e + slot, e + slot, slot, n0 + 2 * e + (2 * slot - 2))
                        if slot:
                            complete(g0 + e + (slot - 3), 1 - slot)
                        scatter(g0 + e + (slot - 2), e + (slot - 2), slot, n0 + 2 * e + (2 * slot - 1))
                    complete(g0 + e - 1, 1)
                for slot in range(2):
                    scatter(g0 + (NE - 2 + slot), NE - 2 + slot, slot, n0 + (2 * NE - 2 + slot))
                    complete(g0 + (NE - 2 + slot), slot)
            if norm:
                for t in range(NT):
                    norm.pool_rstd(pool, t)

        @block.scalar
        def _(act):
            act.activation(c.exps[:, :, :, :], c.exps[:, :, :, :], ACT.Exp).then_inc(exp_out, 1)
            for s in (gate_up_copied, silu_ready, y_copied):
                act.sem_inc(s, AHEAD)
            count = rounds(act)

            def expert(g, slot):
                act.wait_ge(gate_up_products, g + done(0))
                act.wait_ge(h_turned, g + free(0))
                act.activation(gate_up[:, slot, :], c.ps[:, 2 + slot, 0:FF], ACT.Copy).then_inc(gate_up_copied, 1)
                act.wait_ge(h_turned, g + done(0))
                act.wait_ge(hidden_ready, g + free(0))
                turned = c.ps[:, 4 + slot, 0:FF].rearrange("p (j m) -> p j m", m=P)
                act.activation(silu[:, slot, :, :], turned[:, :, 0:RANKS], ACT.Silu).then_inc(silu_ready, 1)
                act.wait_ge(y_products, g + done(0))
                act.wait_ge(y_stored, g + free(0))
                act.activation(y[:, slot, :], c.ps[:, 6 + slot, :], ACT.Copy).then_inc(y_copied, 1)

            with act.Fori(0, count) as r:
                with act.Fori(0, NE // 2) as pair:
                    e = pair * 2
                    for slot in range(2):
                        expert(r * NE + e + slot, slot)

            act.wait_ge(gates_ready, 1)
            for t in range(NT + (2 if norm else 0)):
                if t < NT:
                    act.wait_ge(y_pair_loaded[t % 3], 16 * (t // 3 + 1))
                    first = y_pair[:, t % 3, 0, :]
                    act.activation(first, first, ACT.Copy, scale=gates[:, 0, t:t + 1]).then_inc(first_scaled, 1)
                if norm and 1 <= t < NT + 1:
                    act.wait_ge(x_added, t)
                    norm.act_squares(act, t - 1)
                if norm and t >= 2:
                    norm.act_rows(act, t - 2)

        @block.vector
        def _(dve):
            for s in (xT_ready, hidden_ready):
                dve.sem_inc(s, AHEAD)
            step = Chain(dve, route_step)
            t_ = [tiny[:, i, :] for i in range(16)]

            def tt(out, a, b, op):
                step.sync(dve.tensor_tensor(out, a, b, op))

            def red(out, a, op):
                step.sync(dve.tensor_reduce(out, a, X, op))

            tok_counts = c.ps[:, 0, :].rearrange("p (t e) -> p t e", e=NE)
            chosen_counts = by_rank.rearrange("p (t e) -> p t e", e=NE)
            dve.wait_ge(counted, 1)
            for k in range(2):
                tt(chosen_counts, chosen[:, k, :, :], tok_counts, ALU.mult)
                red(rank[:, k, :], chosen_counts, ALU.add)
            dve.wait_ge(counted, 2)
            red(t_[0][:, 0:1], c.ps[:, 1, 0:NE], ALU.max)
            step.sync(dve.tensor_scalar(idx_f[:, 0, 0:MAXR], c.round_start[:, :], t_[0][:, 0:1], None, ALU.is_lt))
            red(t_[0][:, 1:2], idx_f[:, 0, 0:MAXR], ALU.add)
            dve.tensor_copy(n_rounds[:, :], t_[0][:, 1:2]).then_inc(rounds_ready, 1)

            def make_gates():
                group, first, second = (c.picked[:, i, :, :] for i in range(3))
                of_group, of_expert = c.exps[:, 0, :, :], c.exps[:, 1, :, :]
                dve.wait_ge(exp_out, 1)
                for i, (e, pick) in enumerate(((of_group, group), (of_expert, first), (of_expert, second))):
                    tt(by_pick[:, 0, :, :], e, pick, ALU.mult)
                    red(t_[1 + i], by_pick[:, 0, :, :], ALU.add)
                for i, e in enumerate((of_group, of_expert)):
                    red(t_[4], e, ALU.add)
                    step.sync(dve.reciprocal(t_[5 + i], t_[4]))
                for i, total in enumerate((5, 6, 6)):
                    tt(t_[7 + i], t_[1 + i], t_[total], ALU.mult)
                tt(t_[10], t_[8], t_[9], ALU.add)
                step.sync(dve.reciprocal(t_[11], t_[10]))
                for k in range(2):
                    tt(t_[12], t_[8 + k], t_[11], ALU.mult)
                    tt(gates[:, k, :], t_[12], t_[7], ALU.mult)

            count = rounds(dve)

            PER_ROUND = 7

            def expert_x(g, slot):
                dve.wait_ge(x_turned, g + done(0))
                dve.wait_ge(gate_up_products, g + free(0))
                dve.tensor_tensor(xT[:, slot, :, :, :].rearrange("p j h m -> p (j h) m"),
                                  c.ps[:, slot, :].rearrange("p (a m) -> p a m", m=RANKS),
                                  bc(c.xw[:, layer, :, :].rearrange("p j h -> p (j h)"), 2, RANKS),
                                  ALU.mult).then_inc(xT_ready, 1)

            def expert_h(g, slot):
                dve.wait_ge(silu_ready, g + done(0))
                dve.wait_ge(y_products, g + free(0))
                turned = c.ps[:, 4 + slot, 0:FF].rearrange("p (j m) -> p j m", m=P)
                dve.tensor_tensor(hidden[:, slot, :, :], silu[:, slot, :, :], turned[:, :, RANKS:P],
                                  ALU.mult).then_inc(hidden_ready, 1)

            with dve.Fori(0, count) as r:
                in_round = Chain(dve, round_step)
                in_round.at(r * PER_ROUND)
                dve.wait_ge(idx_products, r + 1)
                rank_all = rank.rearrange("p k t -> p (k t)")
                dve.tensor_tensor(onehot, bc(rank_all, 2, P),
                                  bc(c.rank_of_col[:, :, :].rearrange("p a b -> p (a b)"), 1, 2 * NT),
                                  ALU.is_equal).then_inc(onehot_ready, 1)
                dve.wait_ge(onehot_ready, r + 1)
                in_round.mark(dve.tensor_scalar(rank_all, rank_all, -float(RANKS), None, ALU.add))
                dve.wait_ge(idx_products, r + 2)
                in_round.sync(dve.tensor_copy(idx_f[:, 0, :], c.ps[:, 0, 0:NE]))
                code = idx_f[:, 0, :]
                in_round.mark(dve.tensor_scalar(idx_f[:, 1, :], code, 2.0, c.upper_half[:, 0:1], ALU.mult, ALU.add))
                in_round.mark(dve.tensor_scalar(idx_f[:, 2, :], code, 0.5, 1e6, ALU.is_lt, ALU.mult))
                in_round.sync(dve.tensor_scalar(idx_f[:, 3, :], code, float(S) + 0.5, -2.0 * S, ALU.is_gt, ALU.mult))
                in_round.sync(dve.tensor_tensor(idx_f[:, 1, :], idx_f[:, 1, :], idx_f[:, 2, :], ALU.add))
                in_round.sync(dve.tensor_tensor(idx_f[:, 3, :], idx_f[:, 1, :], idx_f[:, 3, :], ALU.add))
                assert in_round.n == PER_ROUND
                dve.wait_ge(y_stored, r * NE + AHEAD)
                dve.tensor_copy(gather_idx[:, :], idx_f[:, 3, :]).then_inc(idx_ready, 1)
                dve.tensor_copy(scatter_idx[:, :], idx_f[:, 1, :]).then_inc(idx_ready, 1)
                g0 = r * NE
                expert_x(g0, 0)
                with dve.Fori(0, NE // 2 - 1) as pair:
                    e = pair * 2
                    for slot in range(2):
                        expert_x(g0 + e + slot + 1, 1 - slot)
                        expert_h(g0 + e + slot, slot)
                expert_x(g0 + NE - 1, 1)
                expert_h(g0 + NE - 2, 0)
                expert_h(g0 + NE - 1, 1)

            make_gates()
            dve.sem_inc(gates_ready, 1)

            def combine(t):
                dve.wait_ge(first_scaled, t + 1)
                y0, y1 = y_pair[:, t % 3, 0, :], y_pair[:, t % 3, 1, :]
                dve.scalar_tensor_tensor(out=y0, in0=y1, scalar=gates[:, 1, t:t + 1], in1=y0,
                                         op0=ALU.mult, op1=ALU.add).then_inc(summed, 1)
                dve.wait_ge(summed, t + 1)
                dve.tensor_tensor(c.x[:, t, :], c.x[:, t, :], y0, ALU.add).then_inc(x_added, 1)

            for t in range(NT + (3 if norm else 0)):
                if t < NT:
                    combine(t)
                if norm and 1 <= t < NT + 1:
                    norm.dve_var(dve, t - 1)
                if norm and t >= 3:
                    norm.dve_evacuate(dve, t - 3)

        @block.tensor
        def _(pe):
            for s in (x_turned, gate_up_products, h_turned, y_products):
                pe.sem_inc(s, AHEAD)
            pe.sem_inc(idx_products, 1)
            tok = c.ps[:, 0, :]
            for k in range(2):
                pe.matmul(tok, c.before[:, :], chosen[:, k, :, :].rearrange("p t e -> p (t e)"),
                          start=(k == 0), stop=False)
            pe.matmul(tok, c.ones[:, :], earlier[:, 0:NT, :].rearrange("p t e -> p (t e)"),
                      start=False, stop=True).then_inc(counted, 1)
            pe.matmul(c.ps[:, 1, 0:NE], c.ones[:, :], earlier[:, NT, :], start=True, stop=True).then_inc(counted, 1)
            count = rounds(pe)
            pe.wait_ge(cleared, 1)

            def turn_x(g, slot):
                pe.wait_ge(gather_done[slot], g * 8 + (16 - 8 * slot))
                pe.wait_ge(xT_ready, g + free(0))
                rows = gathered[:, slot, :].rearrange("p (m j) -> p j m", j=4)
                for j in range(4):
                    last_ = pe.transpose(c.ps[:, slot, j * P:(j + 1) * P], rows[:, j, :], c.ident[:, :])
                last_.then_inc(x_turned, 1)

            def gate_and_up(g, slot):
                pe.wait_ge(xT_ready, g + done(0))
                pe.wait_ge(w_gate_up_loaded[slot], g * 16 + (32 - 16 * slot))
                pe.wait_ge(gate_up_copied, g + free(0))
                for half in range(2):
                    for j in range(4):
                        for row, w in ((0, w_gate), (RANKS, w_up)):
                            last_ = pe.matmul(c.ps[row:row + RANKS, 2 + slot, 0:FF], xT[:, slot, j, half, :],
                                              w[:, slot, half, j * FF:(j + 1) * FF],
                                              start=(half + j == 0), stop=(half == 1 and j == 3))
                last_.then_inc(gate_up_products, 1)

            def turn_h(g, slot):
                pe.wait_ge(gate_up_copied, g + done(0))
                pe.wait_ge(hidden_ready, g + free(0))
                for j in range(KF):
                    last_ = pe.transpose(c.ps[:, 4 + slot, j * P:(j + 1) * P],
                                         gate_up[:, slot, j * P:(j + 1) * P], c.ident[:, :])
                last_.then_inc(h_turned, 1)

            def down(g, slot):
                pe.wait_ge(hidden_ready, g + done(0))
                pe.wait_ge(w_down_loaded[slot], g * 8 + (16 - 8 * slot))
                pe.wait_ge(y_copied, g + free(0))
                for j in range(KF):
                    for half in range(2):
                        last_ = pe.matmul(c.ps[half * RANKS:(half + 1) * RANKS, 6 + slot, :], hidden[:, slot, j, :],
                                          w_down[:, slot, j, half * BANK:(half + 1) * BANK],
                                          start=(j == 0), stop=(j == KF - 1))
                last_.then_inc(y_products, 1)

            with pe.Fori(0, count) as r:
                pe.wait_ge(onehot_ready, r + 1)
                for n in range(2 * NT):
                    last_ = pe.matmul(c.ps[:, 0, 0:NE], onehot[:, n, :], coded[:, n // NT, n % NT, :],
                                      start=(n == 0), stop=(n == 2 * NT - 1))
                last_.then_inc(idx_products, 1)
                g0 = r * NE
                turn_x(g0, 0)
                with pe.Fori(0, NE // 2 - 1) as pair:
                    e = pair * 2
                    for slot in range(2):
                        gate_and_up(g0 + e + slot, slot)
                        turn_x(g0 + e + slot + 1, 1 - slot)
                        turn_h(g0 + e + slot, slot)
                        down(g0 + e + slot, slot)
                gate_and_up(g0 + NE - 2, 0)
                turn_x(g0 + NE - 1, 1)
                turn_h(g0 + NE - 2, 0)
                down(g0 + NE - 2, 0)
                gate_and_up(g0 + NE - 1, 1)
                turn_h(g0 + NE - 1, 1)
                down(g0 + NE - 1, 1)
            if norm:
                for t in range(NT):
                    norm.pe_turn(pe, t)

    sems.clear()


def attention_phase(c):
    nc, ins = c.nc, c.ins
    sems = Sems(nc, "mla")
    piece = c.carve(c.whole_arena)
    latT = piece(KQ + KKV, S)
    w_q = piece(KQ, NH * QD)
    w_kv = piece(KKV, NH * (NOPE + VD))
    heads_at = piece.at[0]
    qkT = piece(2, 2, S)
    ropeT = piece(2, 2, S)
    v = piece(2, NT, VD)
    probsT = piece(2, NT, 2 * P)
    piece_t = c.carve(c.turned[:, :, :, :].rearrange("p a k m -> p (a k m)"))
    piece_r = c.carve(c.rows[:, 2:4, :].rearrange("p a d -> p (a d)"))
    k_rope = piece_t(NT, ROPE)
    cos_q = piece_t(NT, ROPE)
    sin_q = piece_t(NT, ROPE)
    q_k_rows = piece_r(2, 2 * NOPE + 2 * ROPE)
    raw = piece_r(2, QD + NOPE + VD)
    junk = (piece_t(QD + NOPE), c.logits[:, :, :].rearrange("p t n -> p (t n)")[:, 0:QD + NOPE])
    rot = piece_r(2, ROPE)
    head_sumsq = piece_t(2, 2)
    head_sum2 = piece_t(2, 2)
    head_var = piece_t(2, 2)
    head_rstd = piece_t(2, 2)
    k_rope_sumsq = piece_t(NT, 2)
    row_max = piece_t(2, 1)
    minus_max = piece_t(2, 1)
    row_sum = piece_t(2, 1)
    row_rec = piece_t(2, 1)
    lat_gain = piece_t(KQ + KKV)
    nope_gain = piece_t(2)
    lat_sumsq = piece_t(NT, 2)
    lat_var = piece_t(NT, 2)
    lat_rstd = piece_t(NT, 2)
    early = [heads_at]

    def early_piece(*shape):
        n = int(np.prod(shape))
        a = c.arena[:, early[0]:early[0] + n]
        early[0] += n
        assert early[0] <= heads_at + 10240 + 4096
        if len(shape) == 2:
            a = a.rearrange("p (a b) -> p a b", b=shape[1])
        return a

    w_lat = early_piece(KD, LAT)
    lat_rows = early_piece(2, QL + KVL)
    k_raw = early_piece(NT, ROPE)
    lat_junk = early_piece(2, QL + KVL)
    pos_f = early_piece(NT)
    inv_freq = early_piece(ROPE // 2)
    angle = early_piece(NT, ROPE // 2)
    turns_ = early_piece(NT, ROPE // 2)
    sine = early_piece(NT, ROPE // 2)
    cosine = early_piece(NT, ROPE // 2)
    k_tmp = early_piece(NT, ROPE)
    k_tmp2 = early_piece(NT, ROPE)
    rope_gain = early_piece(2, ROPE)
    w_out = c.arena[:, 0:KD * D].rearrange("p (k d) -> p k d", k=KD)
    assert KD * D <= heads_at
    probs = c.rows
    oT = c.hT
    HR = ROPE // 2
    SCALE = float(QD) ** -0.5

    lat_w_loaded = sems("lat_w_loaded")
    up_w_loaded = sems("up_w_loaded")
    small_loaded = sems("small_loaded")
    out_w_loaded = sems("out_w_loaded")
    freq_set = sems("freq_set")
    trig_step = sems("trig_step")
    sin_in = sems("sin_in")
    sin_out = sems("sin_out")
    lat_products = sems("lat_products")
    lat_squares = sems("lat_squares")
    lat_step = sems("lat_step")
    lat_var_ready = sems("lat_var_ready")
    lat_rstd_ready = sems("lat_rstd_ready")
    lat_scaled = sems("lat_scaled")
    lat_turned = sems("lat_turned")
    latT_ready = sems("latT_ready")
    k_rope_ready = sems("k_rope_ready")
    up_products = sems("up_products")
    raw_copied = sems("raw_copied")
    head_squares = sems("head_squares")
    head_step = sems("head_step")
    head_var_ready = sems("head_var_ready")
    head_rstd_ready = sems("head_rstd_ready")
    rows_normed = sems("rows_normed")
    rot_step = sems("rot_step")
    rows_ready = sems("rows_ready")
    v_copied = sems("v_copied")
    heads_begun = sems("heads_begun")
    qk_turned = sems("qk_turned")
    qkT_ready = sems("qkT_ready")
    ropeT_ready = sems("ropeT_ready")
    scores = sems("scores")
    max_found = sems("max_found")
    bias_ready = sems("bias_ready")
    exps = sems("exps")
    rec_ready = sems("rec_ready")
    probs_ready = sems("probs_ready")
    probs_turned = [sems(f"probs_turned{g}") for g in range(2)]
    probsT_ready = [sems(f"probsT_ready{g}") for g in range(2)]
    pair_products = sems("pair_products")
    pair_copied = sems("pair_copied")
    out_products = sems("out_products")
    x_added = sems("x_added")
    earlier_cleared = sems("earlier_cleared")
    norm = Norm(c, sems, 3, True, (5, 6), logit_bank=7)

    freqs = (10000.0 ** (-np.arange(0, ROPE, 2) / ROPE)).astype(np.float32)
    TWO_PI = 2 * np.pi
    PI_A = float(np.float32(6.28125))
    PI_B = float(np.float32(np.round((TWO_PI - PI_A) * 2**22) / 2**22))
    PI_C = float(np.float32(TWO_PI - PI_A - PI_B))
    ROUND = 1.5 * 2.0**23
    PI_MAX = float(np.nextafter(np.float32(np.pi), np.float32(0)))

    LAST = NH - 1
    PROB_BANKS = ((5, 6), (6, 5))

    with nc.Block() as block:

        @block.sync
        def _(sp):
            sp.dma_start(w_lat, ins["mla_w_down"][0].rearrange("(k p) m -> p k m", p=P)).then_inc(lat_w_loaded, 16)
            sp.dma_start(c.pos_i[:, :], ins["positions"][0].rearrange("(t p) -> p t", p=P)).then_inc(small_loaded, 16)
            sp.dma_start(lat_gain[:, 0:KQ], ins["mla_q_lat_norm"][0].rearrange("(k p) -> p k", p=P)).then_inc(small_loaded, 16)
            sp.dma_start(lat_gain[:, KQ:KQ + KKV], ins["mla_kv_lat_norm"][0].rearrange("(k p) -> p k", p=P)).then_inc(small_loaded, 16)
            for i, name in enumerate(("mla_q_head_norm", "mla_k_head_norm")):
                sp.dma_start(nope_gain[:, i:i + 1], ins[name][0, 0:NOPE].rearrange("(p a) -> p a", a=1)).then_inc(small_loaded, 16)
                sp.dma_start(rope_gain[:, i, :], ins[name][0, NOPE:QD].partition_broadcast(P)).then_inc(small_loaded, 16)
            load_router(sp, c, 1, small_loaded)
            sp.dma_start(w_q, ins["mla_w_q_up"][0].rearrange("(k p) m -> p k m", p=P)).then_inc(up_w_loaded, 16)
            sp.dma_start(w_kv, ins["mla_w_kv_up"][0].rearrange("(k p) m -> p k m", p=P)).then_inc(up_w_loaded, 16)
            sp.wait_ge(up_products, NH * NT)
            sp.dma_start(w_out, ins["mla_w_out"][0].rearrange("(k p) d -> p k d", p=P)).then_inc(out_w_loaded, 16)
            for t in range(NT):
                norm.sp_store(sp, t)
            for t in range(4):
                sp.wait_ge(norm.rows_stored[t], 16 * NT // 4)

        @block.gpsimd
        def _(pool):
            for i in range(HR):
                pool.memset(inv_freq[:, i:i + 1], float(freqs[i])).then_inc(freq_set, 1)
            pool.memset(k_rope_sumsq[:, :, 0:1], 0.0).then_inc(freq_set, 1)
            for t in range(NT):
                pool.wait_ge(lat_var_ready, t + 1)
                pool.tensor_tensor(lat_rstd[:, t, :], lat_var[:, t, :], c.minus_half[:, :], ALU.pow).then_inc(lat_rstd_ready, 1)

            def head_tile(p, h, par, i):
                pool.wait_ge(head_var_ready, p + 1)
                pool.tensor_tensor(head_rstd[:, i % 2, :], head_var[:, i % 2, :], c.minus_half[:, :],
                                   ALU.pow).then_inc(head_rstd_ready, 1)
                if i == 0:
                    wait(pool, pair_products, 4 * (h - 1))
                    pool.sem_inc(heads_begun, 1)
                pool.tensor_copy(v[:, par, i, :], raw[:, i % 2, QD + NOPE:]).then_inc(v_copied, 1)

            for i in range(NT):
                head_tile(i, 0, 0, i)
            for i in range(NT):
                head_tile(NT + i, 1, 1, i)
            with pool.Fori(1, NH // 2) as pair:
                for par in range(2):
                    for i in range(NT):
                        h = pair * 2 + par
                        head_tile(h * NT + i, h, par, i)
            for t in range(NT):
                norm.pool_rstd(pool, t)

        @block.scalar
        def _(act):
            for i, (src, dst) in enumerate(((angle, sine), (turns_, cosine))):
                act.wait_ge(sin_in, i + 1)
                act.activation(dst, src, ACT.Sin).then_inc(sin_out, 1)
            for t in range(NT + 1):
                if t < NT:
                    act.wait_ge(lat_products, 2 * t + 2)
                    wait(act, lat_var_ready, t - 1)
                    a, b = 2 * (t % 2), 2 * (t % 2) + 1
                    act.activation(lat_junk[:, t % 2, 0:QL], c.ps[:, a, 0:QL], ACT.Square,
                                   accum_out=lat_sumsq[:, t, 0:1]).then_inc(lat_squares, 1)
                    act.activation(lat_junk[:, t % 2, QL:], c.ps[:, b, 0:KVL], ACT.Square,
                                   accum_out=lat_sumsq[:, t, 1:2]).then_inc(lat_squares, 1)
                    act.activation(k_raw[:, t, :], c.ps[:, b, KVL:KVL + ROPE], ACT.Copy).then_inc(lat_scaled, 1)
                if t >= 1:
                    u = t - 1
                    a, b = 2 * (u % 2), 2 * (u % 2) + 1
                    act.wait_ge(lat_rstd_ready, u + 1)
                    wait(act, lat_turned, 2 * (u - 1))
                    act.activation(lat_rows[:, u % 2, 0:QL], c.ps[:, a, 0:QL], ACT.Copy,
                                   scale=lat_rstd[:, u, 0:1]).then_inc(lat_scaled, 1)
                    act.activation(lat_rows[:, u % 2, QL:], c.ps[:, b, 0:KVL], ACT.Copy,
                                   scale=lat_rstd[:, u, 1:2]).then_inc(lat_scaled, 1)

            def squares(p, slot):
                act.wait_ge(up_products, p + 1)
                wait(act, rows_ready, p - 1)
                wait(act, v_copied, p - 1)
                act.activation(raw[:, slot, :], c.ps[:, 4, 0:QD + NOPE + VD], ACT.Copy).then_inc(raw_copied, 1)
                act.wait_ge(raw_copied, p + 1)
                act.activation(junk[slot][:, 0:QD], raw[:, slot, 0:QD], ACT.Square,
                               accum_out=head_sumsq[:, slot, 0:1]).then_inc(head_squares, 1)
                act.activation(junk[slot][:, QD:], raw[:, slot, QD:QD + NOPE], ACT.Square,
                               accum_out=head_sumsq[:, slot, 1:2]).then_inc(head_squares, 1)

            def exp(s, slot):
                act.wait_ge(bias_ready, s + 1)
                wait(act, probs_turned[1], s - 1)
                act.activation(probs[:, slot, :], c.ps[:, 2 * slot:2 * slot + 2, :].rearrange("p a b -> p (a b)"),
                               ACT.Exp, bias=minus_max[:, slot, :], scale=SCALE,
                               accum_out=row_sum[:, slot, :]).then_inc(exps, 1)

            def copy_probs(s, i, q):
                act.wait_ge(probs_turned[1], s + 1)
                wait(act, pair_products, q - 1)
                act.activation(probsT[:, (i // 2) % 2, 4:8, (i % 2) * P:(i % 2 + 1) * P],
                               c.ps[:, PROB_BANKS[i % 2][1], :].rearrange("p (a m) -> p a m", m=P),
                               ACT.Copy).then_inc(probsT_ready[1], 1)

            def copy_out(q, h, j):
                act.wait_ge(pair_products, q + 1)
                act.activation(oT[:, bass.ds(h, 1), j * 2 * P:(j + 1) * 2 * P].rearrange("p a m -> p (a m)"),
                               c.ps[:, 7, 0:2 * P], ACT.Copy).then_inc(pair_copied, 1)

            def step(h, i, par, first=False, ends=False):
                s = h * NT + i
                if i > 0:
                    exp(s, i % 2)
                if not ends:
                    squares(s + NT, i % 2)
                if not (first and i == 0):
                    copy_probs(s - 1, (i - 1) % NT, 4 * h + (i - 1) // 2)
                if i == 0:
                    exp(s, i % 2)
                if i % 2 == 1 and not (first and i == 1):
                    copy_out(4 * h + (i - 3) // 2, h if i > 1 else h - 1, ((i - 3) // 2) % 4)

            for p in range(NT):
                squares(p, p % 2)
            for i in range(NT):
                step(0, i, 0, first=True)
            with act.Fori(0, (LAST - 1) // 2) as pair:
                h = pair * 2 + 1
                for par in (1, 0):
                    for i in range(NT):
                        step(h + (1 - par), i, par)
            for i in range(NT):
                step(LAST, i, 1, ends=True)
            n = NH * NT
            copy_probs(n - 1, NT - 1, 4 * NH - 1)
            copy_out(4 * NH - 1, LAST, 3)
            for t in range(NT + 2):
                if t < NT:
                    act.wait_ge(x_added, 2 * t + 2)
                    norm.act_squares(act, t)
                    norm.act_rows(act, t)
                if t >= 2:
                    norm.act_logits(act, t - 2)

        @block.vector
        def _(dve):
            trig = Chain(dve, trig_step)
            dve.wait_ge(freq_set, HR + 1)
            dve.wait_ge(small_loaded, 16 * 11)
            trig.sync(dve.tensor_copy(pos_f, c.pos_i[:, :]))
            trig.sync(dve.tensor_tensor(angle, bc(pos_f, 2, HR), bc(inv_freq, 1, NT), ALU.mult))
            trig.sync(dve.tensor_scalar(turns_, angle, 1.0 / TWO_PI, ROUND, ALU.mult, ALU.add))
            trig.sync(dve.tensor_scalar(turns_, turns_, -ROUND, None, ALU.add))
            for part in (PI_A, PI_B, PI_C):
                trig.sync(dve.scalar_tensor_tensor(out=angle, in0=turns_, scalar=-part, in1=angle,
                                                   op0=ALU.mult, op1=ALU.add))
            trig.sync(dve.tensor_scalar(turns_, angle, PI_MAX / 2, -TWO_PI, ALU.is_gt, ALU.mult))
            trig.sync(dve.scalar_tensor_tensor(out=turns_, in0=angle, scalar=TWO_PI / 4, in1=turns_,
                                               op0=ALU.add, op1=ALU.add))
            dve.tensor_scalar(angle, angle, PI_MAX, -PI_MAX, ALU.min, ALU.max).then_inc(sin_in, 1)
            dve.tensor_scalar(turns_, turns_, PI_MAX, -PI_MAX, ALU.min, ALU.max).then_inc(sin_in, 1)

            lat = Chain(dve, lat_step)
            for t in range(NT + 2):
                if t < NT:
                    dve.wait_ge(lat_squares, 2 * t + 2)
                    lat.mark(dve.tensor_scalar(lat_var[:, t, 0:1], lat_sumsq[:, t, 0:1], 1.0 / QL, EPS, ALU.mult, ALU.add))
                    dve.tensor_scalar(lat_var[:, t, 1:2], lat_sumsq[:, t, 1:2], 1.0 / KVL, EPS,
                                      ALU.mult, ALU.add).then_inc(lat_var_ready, 1)
                if t >= 2:
                    u = t - 2
                    for g, (k0, n) in enumerate(((0, KQ), (KQ, KKV))):
                        dve.wait_ge(lat_turned, 2 * u + g + 1)
                        dve.tensor_tensor(latT[:, k0:k0 + n, u * P:(u + 1) * P],
                                          c.ps[:, 5 + g, 0:n * P].rearrange("p (a m) -> p a m", m=P),
                                          bc(lat_gain[:, k0:k0 + n], 2, P), ALU.mult).then_inc(latT_ready, 1)

            dve.wait_ge(sin_out, 2)
            dve.wait_ge(lat_scaled, 3 * NT)

            def tables(cos_w, sin_w, gain):
                g = rope_gain[:, gain, :]
                for half in range(2):
                    a, b = half * HR, (half + 1) * HR
                    o = (1 - half) * HR
                    trig.mark(dve.tensor_tensor(cos_w[:, :, a:b], cosine, bc(g[:, a:b], 1, NT), ALU.mult))
                    trig.mark(dve.scalar_tensor_tensor(out=sin_w[:, :, a:b], in0=sine, scalar=(-1.0, 1.0)[half],
                                                       in1=bc(g[:, o:o + HR], 1, NT), op0=ALU.mult, op1=ALU.mult))

            tables(cos_q, sin_q, 0)
            tables(k_tmp, k_tmp2, 1)
            trig.sync()
            trig.mark(dve.tensor_tensor(k_tmp, k_tmp, k_raw, ALU.mult))
            trig.mark(dve.tensor_tensor(k_tmp2[:, :, 0:HR], k_tmp2[:, :, 0:HR], k_raw[:, :, HR:], ALU.mult))
            trig.sync(dve.tensor_tensor(k_tmp2[:, :, HR:], k_tmp2[:, :, HR:], k_raw[:, :, 0:HR], ALU.mult))
            trig.sync(dve.tensor_tensor(k_rope, k_tmp, k_tmp2, ALU.add))
            trig.sync(dve.tensor_tensor(k_tmp, k_raw, k_raw, ALU.mult))
            trig.sync(dve.tensor_reduce(k_rope_sumsq[:, :, 1], k_tmp, X, ALU.add))

            def norm_rows(p, slot, i):
                dve.wait_ge(head_squares, 2 * p + 2)
                wait(dve, head_rstd_ready, p - 1)
                dve.tensor_tensor(head_sum2[:, slot, :], head_sumsq[:, slot, :], k_rope_sumsq[:, i, :],
                                  ALU.add).then_inc(head_step, 1)
                dve.wait_ge(head_step, p + 1)
                dve.tensor_scalar(head_var[:, slot, :], head_sum2[:, slot, :], 1.0 / QD, EPS,
                                  ALU.mult, ALU.add).then_inc(head_var_ready, 1)
                dve.wait_ge(head_rstd_ready, p + 1)
                wait(dve, qk_turned, p - 1)
                rows = q_k_rows[:, slot, :]
                rope_in = rot[:, 0, :]
                dve.tensor_scalar(rope_in, raw[:, slot, NOPE:QD], head_rstd[:, slot, 0:1], None,
                                  ALU.mult).then_inc(rows_normed, 1)
                dve.tensor_scalar(rows[:, 0:NOPE], raw[:, slot, 0:NOPE], head_rstd[:, slot, 0:1], None,
                                  ALU.mult).then_inc(rows_normed, 1)
                dve.tensor_scalar(rows[:, NOPE:2 * NOPE], raw[:, slot, QD:QD + NOPE], head_rstd[:, slot, 1:2], None,
                                  ALU.mult).then_inc(rows_normed, 1)
                dve.tensor_scalar(rows[:, 2 * NOPE + ROPE:], k_rope[:, i, :], head_rstd[:, slot, 1:2], None,
                                  ALU.mult).then_inc(rows_normed, 1)
                dve.wait_ge(rows_normed, 4 * p + 4)
                q_rot = rows[:, 2 * NOPE:2 * NOPE + ROPE]
                dve.tensor_tensor(rot[:, 1, 0:HR], rope_in[:, HR:], sin_q[:, i, 0:HR], ALU.mult).then_inc(rot_step, 1)
                dve.tensor_tensor(rot[:, 1, HR:], rope_in[:, 0:HR], sin_q[:, i, HR:], ALU.mult).then_inc(rot_step, 1)
                dve.tensor_tensor(q_rot, rope_in, cos_q[:, i, :], ALU.mult).then_inc(rot_step, 1)
                dve.wait_ge(rot_step, 3 * p + 3)
                dve.tensor_tensor(q_rot, q_rot, rot[:, 1, :], ALU.add).then_inc(rows_ready, 1)
                dve.wait_ge(rows_ready, p + 1)

            def gain_qk(p, h, i, bank):
                dve.wait_ge(qk_turned, p + 1)
                dve.tensor_tensor(qkT[:, h % 2, :, i * P:(i + 1) * P],
                                  c.ps[:, bank, 0:2 * P].rearrange("p (a m) -> p a m", m=P),
                                  bc(nope_gain, 2, P), ALU.mult).then_inc(qkT_ready, 1)
                dve.tensor_copy(ropeT[0:ROPE, h % 2, :, i * P:(i + 1) * P],
                                c.ps[0:ROPE, bank, 2 * P:4 * P].rearrange("p (a m) -> p a m", m=P)
                                ).then_inc(ropeT_ready, 1)

            def find_max(s, slot):
                dve.wait_ge(scores, s + 1)
                dve.tensor_reduce(row_max[:, slot, :], c.ps[:, 2 * slot:2 * slot + 2, :].rearrange("p a b -> p (a b)"),
                                  X, ALU.max).then_inc(max_found, 1)
                dve.wait_ge(max_found, s + 1)
                dve.tensor_scalar(minus_max[:, slot, :], row_max[:, slot, :], -SCALE, None,
                                  ALU.mult).then_inc(bias_ready, 1)

            def copy_probs(s, i, q):
                dve.wait_ge(probs_turned[0], s + 1)
                wait(dve, pair_products, q - 1)
                dve.tensor_copy(probsT[:, (i // 2) % 2, 0:4, (i % 2) * P:(i % 2 + 1) * P],
                                c.ps[:, PROB_BANKS[i % 2][0], :].rearrange("p (a m) -> p a m", m=P)
                                ).then_inc(probsT_ready[0], 1)

            def divide(s, slot):
                dve.wait_ge(exps, s + 1)
                dve.reciprocal(row_rec[:, slot, :], row_sum[:, slot, :]).then_inc(rec_ready, 1)
                dve.wait_ge(rec_ready, s + 1)
                dve.tensor_scalar(probs[:, slot, :], probs[:, slot, :], row_rec[:, slot, :], None,
                                  ALU.mult).then_inc(probs_ready, 1)

            def step(h, i, par, first=False, ends=False):
                s = h * NT + i
                if i == 0:
                    if not first:
                        copy_probs(s - 1, NT - 1, 4 * h - 1)
                    gain_qk(s + NT - 1, par, NT - 1, 5)
                    if not ends:
                        norm_rows(s + NT, 0, 0)
                    find_max(s, 0)
                    divide(s, 0)
                    return
                find_max(s, i % 2)
                if not ends:
                    gain_qk(s + NT - 1, par + 1, i - 1, 5 + i % 2)
                if i < NT - 1:
                    copy_probs(s - 1, i - 1, 4 * h + (i - 1) // 2)
                divide(s, i % 2)
                if not ends:
                    norm_rows(s + NT, i % 2, i)
                if i == NT - 1:
                    copy_probs(s - 1, i - 1, 4 * h + (i - 1) // 2)

            for p in range(NT):
                norm_rows(p, p % 2, p)
                if p >= 1:
                    gain_qk(p - 1, 0, p - 1, 5 + (p - 1) % 2)
            for i in range(NT):
                step(0, i, 0, first=True)
            with dve.Fori(0, (LAST - 1) // 2) as pair:
                h = pair * 2 + 1
                for par in (1, 0):
                    for i in range(NT):
                        step(h + (1 - par), i, par)
            for i in range(NT):
                step(LAST, i, 1, ends=True)
            copy_probs(NH * NT - 1, NT - 1, 4 * NH - 1)

            def add(t):
                for h in range(2):
                    n = 2 * t + h
                    dve.wait_ge(out_products, n + 1)
                    xt = c.x[:, t, h * BANK:(h + 1) * BANK]
                    dve.tensor_tensor(xt, xt, c.ps[:, n % 4, :], ALU.add).then_inc(x_added, 1)

            dve.wait_ge(out_products, 1)
            dve.memset(c.earlier[:, 0, :], 0.0).then_inc(earlier_cleared, 1)
            dve.wait_ge(earlier_cleared, 1)
            for t in range(NT + 2):
                if t < NT:
                    add(t)
                if 1 <= t <= NT:
                    norm.dve_evacuate(dve, t - 1)
                if t < NT:
                    norm.dve_var(dve, t)
                if t >= 2:
                    norm.dve_route(dve, t - 2)

        @block.tensor
        def _(pe):
            def turn_latents(t):
                pe.wait_ge(lat_scaled, min(3 * t + 4, 3 * NT))
                for g, (k0, n) in enumerate(((0, KQ), (KQ, KKV))):
                    wait(pe, latT_ready, 2 * t + g - 1)
                    for j in range(n):
                        last = pe.transpose(c.ps[:, 5 + g, j * P:(j + 1) * P],
                                            lat_rows[:, t % 2, (k0 + j) * P:(k0 + j + 1) * P], c.ident[:, :])
                    last.then_inc(lat_turned, 1)

            pe.wait_ge(lat_w_loaded, 16)
            for t in range(NT + 1):
                if t < NT:
                    wait(pe, lat_scaled, 3 * t - 2 if t >= 2 else 0)
                    a, b = 2 * (t % 2), 2 * (t % 2) + 1
                    for bank, m0, m1 in ((a, 0, QL), (b, QL, LAT)):
                        for k in range(KD):
                            last = pe.matmul(c.ps[:, bank, 0:m1 - m0], c.hT[:, k, t * P:(t + 1) * P],
                                             w_lat[:, k, m0:m1], start=(k == 0), stop=(k == KD - 1))
                        last.then_inc(lat_products, 1)
                if t >= 1:
                    turn_latents(t - 1)

            def up(p, h, i):
                wait(pe, raw_copied, p)
                lat_cols = slice(i * P, (i + 1) * P)
                wq = w_q.rearrange("p k (h m) -> p k h m", h=NH)
                wkv = w_kv.rearrange("p k (h m) -> p k h m", h=NH)
                for k in range(KQ):
                    pe.matmul(c.ps[:, 4, 0:QD], latT[:, k, lat_cols],
                              wq[:, k, bass.ds(h, 1), :].rearrange("p a m -> p (a m)"),
                              start=(k == 0), stop=(k == KQ - 1))
                for k in range(KKV):
                    last = pe.matmul(c.ps[:, 4, QD:QD + NOPE + VD], latT[:, KQ + k, lat_cols],
                                     wkv[:, k, bass.ds(h, 1), :].rearrange("p a m -> p (a m)"),
                                     start=(k == 0), stop=(k == KKV - 1))
                last.then_inc(up_products, 1)

            def turn_qk(p, slot, bank):
                pe.wait_ge(rows_ready, p + 1)
                rows = q_k_rows[:, slot, :]
                for j in range(2):
                    pe.transpose(c.ps[:, bank, j * P:(j + 1) * P], rows[:, j * NOPE:(j + 1) * NOPE], c.ident[:, :])
                for j in range(2):
                    at = 2 * NOPE + j * ROPE
                    last = pe.transpose(c.ps[0:ROPE, bank, (2 + j) * P:(3 + j) * P], rows[:, at:at + ROPE], c.ident[:, :])
                last.then_inc(qk_turned, 1)

            def score(s, h, par, i, slot):
                wait(pe, exps, s - 1)
                if i == 0:
                    pe.wait_ge(qkT_ready, s + NT)
                    pe.wait_ge(ropeT_ready, s + NT)
                q = slice(i * P, (i + 1) * P)
                for half in range(2):
                    keys = slice(half * BANK, (half + 1) * BANK)
                    pe.matmul(c.ps[:, 2 * slot + half, :], qkT[:, par, 0, q], qkT[:, par, 1, keys],
                              start=True, stop=False)
                    last = pe.matmul(c.ps[:, 2 * slot + half, :], ropeT[0:ROPE, par, 0, q], ropeT[0:ROPE, par, 1, keys],
                                     start=False, stop=True)
                last.then_inc(scores, 1)

            def turn_probs(s, i):
                pe.wait_ge(probs_ready, s + 1)
                for g in range(2):
                    wait(pe, probsT_ready[1 - g], s)
                    for j in range(4):
                        kt = 4 * g + j
                        last = pe.transpose(c.ps[:, PROB_BANKS[i % 2][g], j * P:(j + 1) * P],
                                            probs[:, i % 2, kt * P:(kt + 1) * P], c.ident[:, :])
                    last.then_inc(probs_turned[g], 1)

            def weigh(q, h, par, j):
                pe.wait_ge(v_copied, NT * h + NT)
                for g in range(2):
                    pe.wait_ge(probsT_ready[g], 2 * q + 2)
                wait(pe, pair_copied, q)
                for kt in range(NT):
                    last = pe.matmul(c.ps[:, 7, 0:2 * P], v[:, par, kt, :], probsT[:, j % 2, kt, :],
                                     start=(kt == 0), stop=(kt == NT - 1))
                last.then_inc(pair_products, 1)

            def step(h, i, par, first=False, ends=False):
                s = h * NT + i

                def turn_last():
                    p = s + NT - 1
                    if first and i == 0:
                        pe.wait_ge(qkT_ready, p)
                        pe.wait_ge(ropeT_ready, p)
                    elif i == 0:
                        pe.wait_ge(probsT_ready[1], s)
                    else:
                        wait(pe, probsT_ready[0], s - 1)
                    turn_qk(p, (i + 1) % 2, 5 + i % 2)

                def turn_previous(n):
                    pe.wait_ge(qkT_ready, n)
                    pe.wait_ge(ropeT_ready, n)
                    turn_probs(s - 1, (i - 1) % NT)

                def weigh_pair():
                    weigh(4 * h + (i - 3) // 2, h if i > 1 else h - 1, par if i > 1 else 1 - par, ((i - 3) // 2) % 4)

                if i == 0:
                    if not ends:
                        up(s + NT, h + 1, i)
                    if not first:
                        turn_previous(s + NT - 1)
                    turn_last()
                    score(s, h, par, i, i % 2)
                    return
                score(s, h, par, i, i % 2)
                if i % 2 == 1 and i < NT - 1 and not (first and i == 1):
                    weigh_pair()
                if not ends:
                    turn_last()
                    up(s + NT, h + 1, i)
                if i == NT - 1:
                    weigh_pair()
                turn_previous(NH * NT if ends else s + NT)

            pe.wait_ge(up_w_loaded, 32)
            pe.wait_ge(latT_ready, 2 * NT)
            for p in range(NT):
                up(p, 0, p)
                if p >= 1:
                    wait(pe, qkT_ready, p - 2)
                    wait(pe, ropeT_ready, p - 2)
                    turn_qk(p - 1, (p - 1) % 2, 5 + (p - 1) % 2)
            for i in range(NT):
                step(0, i, 0, first=True)
            with pe.Fori(0, (LAST - 1) // 2) as pair:
                h = pair * 2 + 1
                for par in (1, 0):
                    for i in range(NT):
                        step(h + (1 - par), i, par)
            for i in range(NT):
                step(LAST, i, 1, ends=True)
            turn_probs(NH * NT - 1, NT - 1)
            weigh(4 * NH - 1, LAST, 1, 3)
            pe.wait_ge(out_w_loaded, 16)
            pe.wait_ge(pair_copied, 4 * NH)
            for t in range(NT + 2):
                if t < NT:
                    for h in range(2):
                        n = 2 * t + h
                        wait(pe, x_added, n - 3)
                        for k in range(KD):
                            last = pe.matmul(c.ps[:, n % 4, :], oT[:, k, t * P:(t + 1) * P],
                                             w_out[:, k, h * BANK:(h + 1) * BANK],
                                             start=(k == 0), stop=(k == KD - 1))
                        last.then_inc(out_products, 1)
                if 1 <= t <= NT:
                    norm.pe_turn(pe, t - 1)
                if t >= 2:
                    norm.pe_route(pe, t - 2)

    sems.clear()


def build_trunk(nc, ins, out):
    with ExitStack() as ctx:
        ctx.enter_context(nc.allow_non_contiguous_dma(reason="gains of a few KiB, one to a partition"))
        c = Core(nc, ins, out, ctx)
        conv_phase(c)
        moe_phase(c, 0, last=False)
        attention_phase(c)
        moe_phase(c, 1, last=True)


NAMES = ["x", "positions", "conv_norm_w", "conv_w_in", "conv_k", "conv_w_out", "mla_norm_w", "mla_w_down",
         "mla_q_lat_norm", "mla_kv_lat_norm", "mla_w_q_up", "mla_w_kv_up", "mla_q_head_norm", "mla_k_head_norm",
         "mla_w_out", "ffn_norm_w", "router_w_group", "router_b_group", "router_w_expert", "router_b_expert",
         "exp_w_gate", "exp_w_up", "exp_w_down"]


def kernel(**inputs):
    import concourse.bacc as bacc
    from concourse.bass_utils import run_bass_kernel_spmd

    nc = bacc.Bacc("TRN2", target_bir_lowering=False, num_devices=1)
    arrays, aps = {}, {}
    for name in NAMES:
        a = np.ascontiguousarray(inputs[name])
        arrays[f"in_{name}"] = a
        aps[name] = nc.dram_tensor(f"in_{name}", a.shape, mybir.dt.from_np(a.dtype), kind="ExternalInput").ap()
    out = nc.dram_tensor("out", inputs["x"].shape, F32, kind="ExternalOutput").ap()
    build_trunk(nc, aps, out)
    result = run_bass_kernel_spmd(nc, [arrays], core_ids=[0])
    return result.results[0]["out"]
```

```python
from contextlib import ExitStack

import numpy as np

import concourse.bass as bass
from concourse import mybir

F32 = mybir.dt.float32
I32 = mybir.dt.int32
BF16 = mybir.dt.bfloat16
F32R = mybir.dt.float32r
ALU = mybir.AluOpType
ACT = mybir.ActivationFunctionType
X = mybir.AxisListType.X

P = 128
D, S = 1024, 1024
KD = D // P
NT = S // P
EPS = 1e-6
BANK = 512
NE, NG, EG = 64, 8, 8
NL = NG + NE
FF = 384
KF = FF // P
RANKS = 64
MAXR = 2 * S // RANKS
NH, NOPE, ROPE, VD = 8, 128, 64, 128
QD = NOPE + ROPE
QL, KVL = 384, 256
LAT = QL + KVL + ROPE
KQ, KKV = QL // P, KVL // P
HIGH, LOW = 0, 1
PARTS = ((HIGH, HIGH), (HIGH, LOW), (LOW, HIGH))
LATENT_AT = 12 * D
AHEAD = 2


def wait(eng, sem, value):
    if isinstance(value, int) and value <= 0:
        return
    eng.wait_ge(sem, value)


class Chain:

    def __init__(self, eng, sem):
        self.eng, self.sem, self.base, self.n = eng, sem, 0, 0

    def at(self, base):
        self.base, self.n = base, 0

    def mark(self, ins):
        ins.then_inc(self.sem, 1)
        self.n += 1

    def sync(self, ins=None):
        if ins is not None:
            self.mark(ins)
        self.eng.wait_ge(self.sem, self.base + self.n)


class Core:

    def __init__(self, nc, ins, out, ctx):
        self.nc, self.ins, self.out = nc, ins, out

        def sb(name, shape, dt=F32):
            return ctx.enter_context(nc.sbuf_tensor(name, shape, dt))

        self.x = sb("x", [P, NT, D])
        self.hT_at = -(-nc.sbuf_base // 32) * 32
        self.hT = sb("hT", [P, KD, S])
        self.rows = sb("rows", [P, 4, D])
        self.turned = sb("turned", [P, 2, KD, P])
        self.logits = sb("logits", [P, NT, NL])
        self.w_router = sb("w_router", [P, KD, NL])
        self.ident = sb("ident", [P, P])
        self.before = sb("before", [P, P], BF16)
        self.ones = sb("ones", [P, P], BF16)
        self.rank_of_col = sb("rank_of_col", [P, 2, RANKS])
        self.row_plus_1 = sb("row_plus_1", [P, 1])
        self.from_last = sb("from_last", [P, EG])
        self.round_start = sb("round_start", [P, MAXR])
        self.upper_half = sb("upper_half", [P, 1])
        self.minus_half = sb("minus_half", [P, 2])
        self.sumsq = sb("sumsq", [P, NT])
        self.var = sb("var", [P, NT])
        self.rstd = sb("rstd", [P, NT])
        self.norm_w = sb("norm_w", [P, 4, KD])
        self.xw = sb("xw", [P, 2, 4, 2])
        self.gather_idx = sb("gather_idx", [P, NE], I32)
        self.scatter_idx = sb("scatter_idx", [P, NE], I32)
        self.col_idx = sb("col_idx", [P, 4, 1], I32)
        self.n_rounds = sb("n_rounds", [P, 1], I32)
        self.pos_i = sb("pos_i", [P, NT], I32)
        self.arena_words = 28300
        self.arena_at = -(-nc.sbuf_base // 32) * 32
        self.arena = sb("arena", [P, self.arena_words])
        self.route_words = 2900
        piece = self.carve(self.arena[:, self.arena_words - self.route_words:])
        self.chosen = piece(2, NT, NE)
        at = self.arena_words - self.route_words + 2 * NT * NE
        self.coded = self.typed("coded", at, [P, 2, NT, 2, NE], BF16)
        self.both = self.typed("both", at + 2 * NT * NE, [P, NT, NE], BF16)
        self.earlier = self.typed("earlier", at + 2 * NT * NE + NT * NE // 2, [P, NT + 1, NE], BF16)
        piece(2 * NT * NE + NT * NE // 2 + (NT + 1) * NE // 2)
        self.route_big = piece(3, NE)
        self.route_small = piece(8, EG)
        self.route_tiny = piece(8)
        self.whole_arena = self.arena[:, :]
        self.arena_words -= self.route_words
        self.exps = sb("exps", [P, 2, NT, EG])
        self.picked = sb("picked", [P, 3, NT, EG])
        self.bias = sb("bias", [P, NL])
        self.ps = ctx.enter_context(nc.psum_tensor("ps", [P, 8, BANK], F32))
        self.h_rows = nc.dram_tensor("h_rows", [S, D], F32, kind="Internal").ap()
        self.y_rows = nc.dram_tensor("y_rows", [2 * S, D], F32, kind="Internal").ap()

    def typed(self, name, at, shape, dt, place=None):
        place = self.arena_at if place is None else place
        t = self.nc.alloc_sbuf_tensor_at(name, shape, dt, offset=place + 4 * at)
        return t[tuple(slice(None) for _ in shape)]

    def carve(self, place=None):
        at = [0]
        place = self.arena[:, 0:self.arena_words] if place is None else place
        words = place.shape[1]

        def piece(*shape):
            n = int(np.prod(shape))
            a = place[:, at[0]:at[0] + n]
            at[0] += n
            assert at[0] <= words, (at[0], words)
            if len(shape) == 2:
                a = a.rearrange("p (a b) -> p a b", b=shape[1])
            elif len(shape) == 3:
                a = a.rearrange("p (a b c) -> p a b c", b=shape[1], c=shape[2])
            elif len(shape) == 4:
                a = a.rearrange("p (a b c d) -> p a b c d", b=shape[1], c=shape[2], d=shape[3])
            return a

        piece.at = at
        return piece


def bc(ap, axis, n):
    a = ap.unsqueeze(axis)
    shape = list(a.shape)
    shape[axis] = n
    return a.broadcast_to(shape)


class Sems:

    def __init__(self, nc, tag):
        self.nc, self.tag, self.all = nc, tag, []

    def __call__(self, name):
        s = self.nc.alloc_semaphore(f"{self.tag}_{name}")
        self.all.append(s)
        return s

    def clear(self):
        self.nc.clear_and_free_semaphores(self.all)
        self.nc.all_engine_barrier()


class Norm:

    def __init__(self, c, sems, which, route, banks, logit_bank=None, split=None):
        self.split = split
        self.c, self.w, self.route, self.banks, self.logit_bank = c, which, route, banks, logit_bank
        named = sems

        def sems(name):
            return named(f"{name}_{which}")

        self.squares = sems("norm_squares")
        self.var_ready = sems("norm_var_ready")
        self.rstd_ready = sems("norm_rstd_ready")
        self.rows_ready = sems("norm_rows_ready")
        self.turns = sems("norm_turns")
        self.evacuated = sems("norm_evacuated")
        self.high_ready = sems("norm_high_ready")
        if route:
            self.logits_ready = sems("norm_logits_ready")
            self.logits_copied = sems("norm_logits_copied")
            self.route_step = sems("norm_route_step")
            self.rows_stored = [sems(f"norm_rows_stored{i}") for i in range(4)]

    def act_squares(self, act, t):
        c = self.c
        if t >= 4:
            act.wait_ge(self.turns, 2 * (t - 3))
            if self.route:
                act.wait_ge(self.rows_stored[t % 4], 16 * (t // 4))
        act.activation(c.rows[:, t % 4, :], c.x[:, t, :], ACT.Square,
                       accum_out=c.sumsq[:, t:t + 1]).then_inc(self.squares, 1)

    def dve_var(self, dve, t):
        c = self.c
        dve.wait_ge(self.squares, t + 1)
        dve.tensor_scalar(c.var[:, t:t + 1], c.sumsq[:, t:t + 1], 1.0 / D, EPS,
                          ALU.mult, ALU.add).then_inc(self.var_ready, 1)

    def pool_rstd(self, pool, t):
        c = self.c
        pool.wait_ge(self.var_ready, t + 1)
        pool.tensor_tensor(c.rstd[:, t:t + 1], c.var[:, t:t + 1], c.minus_half[:, 0:1],
                           ALU.pow).then_inc(self.rstd_ready, 1)

    def act_rows(self, act, t):
        c = self.c
        act.wait_ge(self.rstd_ready, t + 1)
        act.activation(c.rows[:, t % 4, :], c.x[:, t, :], ACT.Copy,
                       scale=c.rstd[:, t:t + 1]).then_inc(self.rows_ready, 1)

    def sp_store(self, sp, t):
        c = self.c
        sp.wait_ge(self.rows_ready, t + 1)
        sp.dma_start(c.h_rows[t * P:(t + 1) * P, :], c.rows[:, t % 4, :]).then_inc(self.rows_stored[t % 4], 16)

    def pe_turn(self, pe, t):
        c = self.c
        pe.wait_ge(self.rows_ready, t + 1)
        for g in range(2):
            n = 2 * t + g
            wait(pe, self.evacuated, n - 1)
            for j in range(4):
                k = 4 * g + j
                ins = pe.transpose(c.ps[:, self.banks[g], j * P:(j + 1) * P],
                                   c.rows[:, t % 4, k * P:(k + 1) * P], c.ident[:, :])
            ins.then_inc(self.turns, 1)

    def dve_evacuate(self, dve, t):
        if self.split is not None:
            return self.dve_evacuate_split(dve, t)
        c = self.c
        for g in range(2):
            dve.wait_ge(self.turns, 2 * t + g + 1)
            if self.route:
                if g == 0:
                    wait(dve, self.logits_ready, t - 1)
                out = c.turned[:, t % 2, 4 * g:4 * g + 4, :]
            else:
                out = c.hT[:, 4 * g:4 * g + 4, t * P:(t + 1) * P]
            dve.tensor_tensor(out, c.ps[:, self.banks[g], :].rearrange("p (a b) -> p a b", b=P),
                              bc(c.norm_w[:, self.w, 4 * g:4 * g + 4], 2, P),
                              ALU.mult).then_inc(self.evacuated, 1)

    def dve_evacuate_split(self, dve, t):
        c = self.c
        cols = slice(t * P, (t + 1) * P)
        for g in range(2):
            dve.wait_ge(self.turns, 2 * t + g + 1)
            dve.tensor_tensor(self.split[:, 0, 4 * g:4 * g + 4, cols],
                              c.ps[:, self.banks[g], :].rearrange("p (a b) -> p a b", b=P),
                              bc(c.norm_w[:, self.w, 4 * g:4 * g + 4], 2, P), ALU.mult).then_inc(self.high_ready, 1)
        for g in range(2):
            dve.wait_ge(self.high_ready, 2 * t + g + 1)
            for j in range(4):
                k = 4 * g + j
                ins = dve.scalar_tensor_tensor(out=self.split[:, 1, k, cols], in0=c.ps[:, self.banks[g], j * P:(j + 1) * P],
                                               scalar=c.norm_w[:, self.w, k:k + 1], in1=self.split[:, 0, k, cols],
                                               op0=ALU.mult, op1=ALU.subtract)
            ins.then_inc(self.evacuated, 1)

    def pe_route(self, pe, t):
        c = self.c
        pe.wait_ge(self.evacuated, 2 * t + 2)
        wait(pe, self.logits_copied, t)
        at = (t % 2) * P
        for k in range(KD):
            ins = pe.matmul(c.ps[:, self.logit_bank, at:at + NL], c.turned[:, t % 2, k, :],
                            c.w_router[:, k, :], start=(k == 0), stop=(k == KD - 1))
        ins.then_inc(self.logits_ready, 1)

    def act_logits(self, act, t):
        c = self.c
        act.wait_ge(self.logits_ready, t + 1)
        at = (t % 2) * P
        act.activation(c.logits[:, t, :], c.ps[:, self.logit_bank, at:at + NL],
                       ACT.Copy).then_inc(self.logits_copied, 1)

    def dve_route(self, dve, t, part=None):
        c = self.c
        step = Chain(dve, self.route_step)
        step.at(t * self.ROUTE_STEPS)
        lg = c.logits[:, t, 0:NG]
        le = c.logits[:, t, NG:NL].rearrange("p (g j) -> p g j", j=EG)
        big = [c.route_big[:, i, :].rearrange("p (g j) -> p g j", j=EG) for i in range(3)]
        small = [c.route_small[:, i, :] for i in range(8)]
        tiny = [c.route_tiny[:, i:i + 1] for i in range(8)]
        group, first, second = (c.picked[:, i, t, :] for i in range(3))

        def tt(out, a, b, op, wait_=True):
            step.mark(dve.tensor_tensor(out, a, b, op))
            if wait_:
                step.sync()

        def reduce(out, a, op, wait_=True):
            step.mark(dve.tensor_reduce(out, a, X, op))
            if wait_:
                step.sync()

        def first_largest(out, values, s, m):
            reduce(m, values, ALU.max)
            step.sync(dve.scalar_tensor_tensor(out=s, in0=values, scalar=m, in1=c.from_last[:, :],
                                               op0=ALU.is_equal, op1=ALU.mult))
            reduce(m, s, ALU.max)
            step.sync(dve.tensor_scalar(out, s, m, None, ALU.is_equal))

        if part != 1:
            dve.wait_ge(self.logits_copied, t + 1)
            wait(dve, self.route_step, t * self.ROUTE_STEPS)
            reduce(tiny[0], lg, ALU.max, False)
            tt(small[0], lg, c.bias[:, 0:NG], ALU.add)
            first_largest(group, small[0], small[1], tiny[1])
            tt(big[0], le, bc(group, 2, EG), ALU.mult, False)
            tt(big[1], bc(group, 2, EG), c.bias[:, NG:NL].rearrange("p (g j) -> p g j", j=EG), ALU.mult)
            reduce(small[2], big[0].rearrange("p g j -> p j g"), ALU.add, False)
            reduce(small[3], big[1].rearrange("p g j -> p j g"), ALU.add, False)
            step.mark(dve.tensor_scalar(c.exps[:, 0, t, :], lg, tiny[0], None, ALU.subtract))
            step.sync()
            tt(small[4], small[2], small[3], ALU.add, False)
            reduce(tiny[2], small[2], ALU.max)
            step.mark(dve.tensor_scalar(c.exps[:, 1, t, :], small[2], tiny[2], None, ALU.subtract))
            first_largest(first, small[4], small[5], tiny[3])
            assert step.n == self.FIRST_STEPS, step.n
            if part == 0:
                return
        step.n = self.FIRST_STEPS
        step.sync(dve.scalar_tensor_tensor(out=small[6], in0=first, scalar=-1e30, in1=small[4],
                                           op0=ALU.mult, op1=ALU.add))
        first_largest(second, small[6], small[7], tiny[4])
        for k, pick in enumerate((first, second)):
            tt(c.chosen[:, k, t, :].rearrange("p (g j) -> p g j", j=EG), bc(group, 2, EG), bc(pick, 1, NG),
               ALU.mult, False)
        step.sync()
        tt(c.both[:, t, :], c.chosen[:, 0, t, :], c.chosen[:, 1, t, :], ALU.add, False)
        for k in range(2):
            step.mark(dve.tensor_scalar(c.coded[:, k, t, 0, :], c.chosen[:, k, t, :], float(k * NT + t), None, ALU.mult))
            step.mark(dve.tensor_scalar(c.coded[:, k, t, 1, :], c.chosen[:, k, t, :], c.row_plus_1[:, 0:1], None,
                                        ALU.mult))
        step.sync()
        tt(c.earlier[:, t + 1, :], c.earlier[:, t, :], c.both[:, t, :], ALU.add)
        assert step.n == self.ROUTE_STEPS, step.n

    ROUTE_STEPS, FIRST_STEPS = 31, 18


class ExpertWeights:

    def __init__(self, c, layer):
        self.sems = Sems(c.nc, f"weights{layer}")
        self.gate_up_loaded = [self.sems(f"gate_up_loaded{i}") for i in range(2)]
        self.down_loaded = [self.sems(f"down_loaded{i}") for i in range(2)]
        self.piece = c.carve()
        self.gate = self.piece(2, 2, 4 * FF)
        self.up = self.piece(2, 2, 4 * FF)
        self.down = self.piece(2, KF, D)
        self.gate_dram = c.ins["exp_w_gate"][layer].rearrange("e (h p j) f -> p e h (j f)", h=2, p=P)
        self.up_dram = c.ins["exp_w_up"][layer].rearrange("e (h p j) f -> p e h (j f)", h=2, p=P)
        self.down_dram = c.ins["exp_w_down"][layer].rearrange("e (j p) d -> p e j d", p=P)

    def load_gate_up(self, sp, slot, e):
        for w, dram in ((self.gate, self.gate_dram), (self.up, self.up_dram)):
            src = dram[:, bass.ds(e, 1), :, :].rearrange("p a h f -> p (a h) f")
            sp.dma_start(w[:, slot, :, :], src).then_inc(self.gate_up_loaded[slot], 16)

    def load_down(self, sp, slot, e):
        src = self.down_dram[:, bass.ds(e, 1), :, :].rearrange("p a j d -> p (a j) d")
        sp.dma_start(self.down[:, slot, :, :], src).then_inc(self.down_loaded[slot], 16)


class OutProjection:

    def __init__(self, c, sems, norm, dram, yT, w_out, w_high, w_low, y_split, experts):
        self.experts = experts
        self.c, self.norm, self.dram, self.yT, self.y_split = c, norm, dram, yT, y_split
        self.w_out, self.w_high, self.w_low = w_out, w_high, w_low
        self.w_loaded = [sems(f"w_out_loaded{h}") for h in range(2)]
        self.w_high_ready = sems("w_out_high_ready")
        self.w_low_ready = [sems(f"w_out_low_ready{h}") for h in range(2)]
        self.y_high_ready = sems("y_high_ready")
        self.y_low_ready = sems("y_low_ready")
        self.products = sems("out_products")
        self.x_added = sems("x_added")
        self.earlier_cleared = sems("earlier_cleared")

    def sp_load(self, sp):
        for h in range(2):
            sp.dma_start(self.w_out[:, h, :, :], self.dram.rearrange("(k p) (h d) -> h p k d", p=P, h=2)[h]
                         ).then_inc(self.w_loaded[h], 16)

    def sp_store_rows(self, sp):
        for t in range(NT - 1):
            self.norm.sp_store(sp, t)
        sp.wait_ge(self.products, 2 * NT)
        self.experts.load_gate_up(sp, 0, 0)
        self.norm.sp_store(sp, NT - 1)
        self.experts.load_down(sp, 0, 0)
        self.experts.load_gate_up(sp, 1, 1)
        self.experts.load_down(sp, 1, 1)
        for t in range(4):
            sp.wait_ge(self.norm.rows_stored[t], 16 * NT // 4)

    def low_w(self, eng, h):
        for q in range(2):
            eng.wait_ge(self.w_high_ready, 2 * h + q + 1)
            ks = slice(4 * q, 4 * q + 4)
            eng.tensor_tensor(self.w_low[:, h, ks, :], self.w_out[:, h, ks, :], self.w_high[:, h, ks, :],
                              ALU.subtract).then_inc(self.w_low_ready[h], 1)

    def act_program(self, act):
        for h in range(2):
            act.wait_ge(self.w_loaded[h], 16)
            for q in range(2):
                ks = slice(4 * q, 4 * q + 4)
                act.activation(self.w_high[:, h, ks, :], self.w_out[:, h, ks, :], ACT.Copy
                               ).then_inc(self.w_high_ready, 1)

        def high_y(t):
            act.wait_ge(self.products, max(1, 2 * t - 2))
            act.activation(self.y_split[:, t % 2, HIGH], self.yT[:, :, t * P:(t + 1) * P], ACT.Copy
                           ).then_inc(self.y_high_ready, 1)

        act.wait_ge(self.w_low_ready[0], 2)
        high_y(1)
        for t in range(NT + 1):
            if t + 2 < NT:
                high_y(t + 2)
            if t >= 1:
                self.norm.act_logits(act, t - 1)
            if t < NT:
                act.wait_ge(self.x_added, 2 * t + 2)
                self.norm.act_squares(act, t)
                self.norm.act_rows(act, t)

    def pool_program(self, pool):
        def low_y(t):
            pool.wait_ge(self.y_high_ready, t)
            pool.tensor_tensor(self.y_split[:, t % 2, LOW], self.yT[:, :, t * P:(t + 1) * P],
                               self.y_split[:, t % 2, HIGH], ALU.subtract).then_inc(self.y_low_ready, 1)

        self.low_w(pool, 1)
        low_y(1)
        for t in range(NT):
            if t + 2 < NT:
                low_y(t + 2)
            self.norm.pool_rstd(pool, t)

    def dve_program(self, dve):
        c = self.c

        def add(t, h):
            n = 2 * t + h
            dve.wait_ge(self.products, n + 1)
            xt = c.x[:, t, h * BANK:(h + 1) * BANK]
            dve.tensor_tensor(xt, xt, c.ps[:, n % 4, :], ALU.add).then_inc(self.x_added, 1)

        self.low_w(dve, 0)
        dve.wait_ge(self.products, 1)
        dve.memset(c.earlier[:, 0, :], 0.0).then_inc(self.earlier_cleared, 1)
        dve.wait_ge(self.earlier_cleared, 1)
        for t in range(NT + 1):
            if t < NT:
                add(t, 0)
            if t >= 1:
                self.norm.dve_evacuate(dve, t - 1)
            if t < NT:
                add(t, 1)
                self.norm.dve_var(dve, t)
            if t == NT:
                self.norm.dve_route(dve, t - 2, 1)
            if t >= 1:
                self.norm.dve_route(dve, t - 1, 0 if t == NT - 1 else None)

    def pe_program(self, pe, y_ready):
        c = self.c

        def product(t, h):
            n = 2 * t + h
            wait(pe, self.x_added, n - 3)
            bank = c.ps[:, n % 4, :]
            if t == 0:
                pe.wait_ge(self.w_loaded[h], 16)
                for k in range(KD):
                    if n == 0 and k == KD - 1:
                        y_ready()
                    last = pe.matmul(bank, self.yT[:, k, 0:P], self.w_out[:, h, k, :],
                                     start=(k == 0), stop=(k == KD - 1))
            else:
                pe.wait_ge(self.y_low_ready, t)
                pe.wait_ge(self.w_low_ready[h], 2)
                for k in range(KD):
                    for a, b in PARTS:
                        w = (self.w_high, self.w_low)[b]
                        last = pe.matmul(bank, self.y_split[:, t % 2, a, k, :], w[:, h, k, :],
                                         start=(k == 0 and a == b), stop=(k == KD - 1 and a == LOW))
            last.then_inc(self.products, 1)

        for t in range(NT + 1):
            if t < NT:
                product(t, 0)
            if t >= 1:
                self.norm.pe_turn(pe, t - 1)
            if t < NT:
                product(t, 1)
            if t >= 1:
                self.norm.pe_route(pe, t - 1)


def load_router(eng, c, layer, sem):
    eng.dma_start(c.bias[:, 0:NG], c.ins["router_b_group"][layer].partition_broadcast(P)).then_inc(sem, 16)
    eng.dma_start(c.bias[:, NG:NL], c.ins["router_b_expert"][layer].partition_broadcast(P)).then_inc(sem, 16)
    eng.dma_start(c.w_router[:, :, 0:NG],
                  c.ins["router_w_group"][layer].rearrange("(k p) g -> p k g", p=P)).then_inc(sem, 16)
    eng.dma_start(c.w_router[:, :, NG:NL],
                  c.ins["router_w_expert"][layer].rearrange("(k p) e -> p k e", p=P)).then_inc(sem, 16)


def conv_phase(c, experts):
    nc, ins = c.nc, c.ins
    sems = Sems(nc, "conv")
    hT_split = c.typed("hT_split", 0, [P, 2, KD, S], F32R)
    w_split = c.typed("w_split", 2 * KD * S, [P, 3, 2, KD, P], F32R)
    piece = c.carve(c.whole_arena[:, 2 * KD * S + 6 * KD * P:])
    w_raw = piece(2, KD, P)
    taps = piece(KD, 3)
    w_out_high = hT_split[:, :, :, BANK:]
    w_out_low = c.typed("w_out_low", 2 * KD * S, [P, 2, KD, BANK], F32R)
    y_split = hT_split[:, HIGH, :, 0:BANK].rearrange("p k (i a m) -> p i a k m", i=2, a=2)
    w_out = c.arena[:, 0:2 * KD * S].rearrange("p (h k s) -> p h k s", h=2, s=S)[:, :, :, 0:BANK]
    yT = c.hT
    piece = c.carve(c.rows[:, :, :].rearrange("p a d -> p (a d)"))
    z = piece(S + 2)
    acc = piece(S)
    gb = piece(S)
    gc = c.turned[:, 0, :, :].rearrange("p k m -> p (k m)").rearrange("p (h m) -> p h m", h=2)
    HT = S // BANK
    UNITS = 3 * KD

    x_loaded = [sems(f"x_loaded{t}") for t in range(NT)]
    w_raw_loaded = [sems(f"w_raw_loaded{i}") for i in range(2)]
    w_high_ready = sems("w_high_ready")
    w_low_ready = sems("w_low_ready")
    unit_used = [sems(f"unit_used{j}") for j in range(2)]
    gain_loaded = sems("gain_loaded")
    small_loaded = sems("small_loaded")
    consts = sems("consts")
    z_edges = sems("z_edges")
    products = sems("products")
    g_copied = sems("g_copied")
    z_half = sems("z_half")
    conv_step = sems("conv_step")
    y_ready = sems("y_ready")
    norm0 = Norm(c, sems, 0, False, (6, 7), split=hT_split)
    norm1 = Norm(c, sems, 1, True, (6, 7), logit_bank=5)
    out_projection = OutProjection(c, sems, norm1, ins["conv_w_out"][0], yT, w_out, w_out_high, w_out_low, y_split,
                                   experts)
    w_in_dram = ins["conv_w_in"][0].rearrange("(k p) (j c m) -> p k j c m", p=P, j=3, m=P)

    with nc.Block() as block:

        @block.sync
        def _(sp):
            def gain(i, name, row):
                sp.dma_start(c.norm_w[:, i, :], ins[name][row].rearrange("(k p) -> p k", p=P)).then_inc(
                    gain_loaded if i == 0 else small_loaded, 16)

            gain(0, "conv_norm_w", 0)
            for t in range(NT):
                sp.dma_start(c.x[:, t, :], ins["x"][0, t * P:(t + 1) * P, :]).then_inc(x_loaded[t], 16)

            def load_unit(ct, j, slot):
                sp.dma_start(w_raw[:, slot, :, :], w_in_dram[:, :, j, bass.ds(ct, 1), :]
                             .rearrange("p k a m -> p (k a) m")).then_inc(w_raw_loaded[slot], 16)

            load_unit(0, 0, 0)
            load_unit(0, 1, 1)
            for j in range(3):
                sp.dma_start(taps[:, :, j], ins["conv_k"][0, j].rearrange("(k p) -> p k", p=P)).then_inc(small_loaded, 16)
            gain(1, "ffn_norm_w", 0)
            gain(2, "mla_norm_w", 0)
            gain(3, "ffn_norm_w", 1)
            for layer in range(2):
                for half in range(2):
                    sp.dma_start(c.xw[:, layer, :, half],
                                 ins["ffn_norm_w"][layer, half * BANK:(half + 1) * BANK]
                                 .rearrange("(p j) -> p j", j=4)).then_inc(small_loaded, 16)
            load_router(sp, c, 0, small_loaded)

            def load_units(pair, n):
                for v in range(n):
                    sp.wait_ge(w_low_ready, 6 * pair + v + 1)
                    load_unit(2 * pair + (v + 2) // 3, (v + 2) % 3, v % 2)

            with sp.Fori(0, KD // 2 - 1) as pair:
                load_units(pair, 6)
            load_units(KD // 2 - 1, 4)
            sp.wait_ge(products, HT * KD - 1)
            out_projection.sp_load(sp)
            out_projection.sp_store_rows(sp)

        @block.gpsimd
        def _(pool):
            step = Chain(pool, consts)
            step.mark(pool.memset(c.ident[:, :], 0.0))
            step.mark(pool.memset(c.ones[:, :], 1.0))
            step.mark(pool.memset(c.before[:, :], 1.0))
            step.mark(pool.memset(c.minus_half[:, :], -0.5))
            step.mark(pool.memset(c.upper_half[:, :], -1.0))
            step.mark(pool.iota(c.rank_of_col[:, :, :], [[0, 2], [1, RANKS]], base=0, channel_multiplier=0,
                                allow_small_or_imprecise_dtypes=True))
            step.mark(pool.iota(c.row_plus_1[:, :], [[0, 1]], base=1, channel_multiplier=1,
                                allow_small_or_imprecise_dtypes=True))
            step.mark(pool.iota(c.from_last[:, :], [[-1, EG]], base=EG, channel_multiplier=0,
                                allow_small_or_imprecise_dtypes=True))
            step.mark(pool.iota(c.round_start[:, :], [[RANKS, MAXR]], base=0, channel_multiplier=0,
                                allow_small_or_imprecise_dtypes=True))
            step.sync()
            step.mark(pool.affine_select(out=c.ident[:, :], in_=c.ident[:, :], compare_op=ALU.not_equal, fill=1.0,
                                         base=0, pattern=[[-1, P]], channel_multiplier=1))
            step.mark(pool.affine_select(out=c.before[:, :], in_=c.before[:, :], compare_op=ALU.is_gt, fill=0.0,
                                         base=0, pattern=[[1, P]], channel_multiplier=-1))
            step.mark(pool.affine_select(out=c.upper_half[:, :], in_=c.upper_half[:, :], compare_op=ALU.is_ge,
                                         fill=-2.0, base=-RANKS, pattern=[[0, 1]], channel_multiplier=1))

            def low_part(u, j, slot):
                pool.wait_ge(w_high_ready, u + 1)
                pool.tensor_tensor(w_split[:, j, LOW, :, :], w_raw[:, slot, :, :], w_split[:, j, HIGH, :, :],
                                   ALU.subtract).then_inc(w_low_ready, 1)

            for t in range(NT - 1):
                norm0.pool_rstd(pool, t)
            low_part(0, 0, 0)
            low_part(1, 1, 1)
            norm0.pool_rstd(pool, NT - 1)
            for u in range(2, 6):
                low_part(u, u % 3, u % 2)
            with pool.Fori(1, KD // 2) as pair:
                for v in range(6):
                    low_part(pair * 6 + v, v % 3, v % 2)
            out_projection.pool_program(pool)

        N_CONST = 12

        @block.scalar
        def _(act):
            def high_part(pair, v):
                j, ct = v % 3, 2 * pair + v // 3
                act.wait_ge(w_raw_loaded[v % 2], 48 * pair + 16 * (v // 2 + 1))
                if j < 2:
                    wait(act, unit_used[j], ct)
                else:
                    wait(act, products, HT * ct)
                act.activation(w_split[:, j, HIGH, :, :], w_raw[:, v % 2, :, :], ACT.Copy).then_inc(w_high_ready, 1)

            for t in range(NT + 2):
                if t < NT:
                    act.wait_ge(x_loaded[t], 16)
                    norm0.act_squares(act, t)
                if t >= 2:
                    norm0.act_rows(act, t - 2)
                if t == NT - 2:
                    high_part(0, 0)
                    high_part(0, 1)

            def copies(pair, i, ends=False):
                ct = 2 * pair + i
                for h in range(HT):
                    n = HT * ct + h
                    act.wait_ge(products, n + 1)
                    wait(act, z_half, n - 1)
                    act.activation(gc[:, h, :], c.ps[:, 3 * h + 1, :], ACT.Copy).then_inc(g_copied, 1)
                    wait(act, y_ready, ct)
                    act.activation(gb[:, h * BANK:(h + 1) * BANK], c.ps[:, 3 * h, :], ACT.Copy).then_inc(g_copied, 1)
                    if not ends:
                        for j in ((0, 1), (2,))[h]:
                            high_part(pair + i, 3 * (1 - i) + j)

            high_part(0, 2)
            act.wait_ge(norm0.turns, 2 * NT)
            copies(0, 0)
            copies(0, 1)
            with act.Fori(1, KD // 2 - 1) as pair:
                for i in range(2):
                    copies(pair, i)
            copies(KD // 2 - 1, 0)
            copies(KD // 2 - 1, 1, ends=True)
            out_projection.act_program(act)

        @block.vector
        def _(dve):
            dve.wait_ge(gain_loaded, 16)
            for t in range(NT + 3):
                if t < NT:
                    norm0.dve_var(dve, t)
                if t >= 3:
                    norm0.dve_evacuate(dve, t - 3)
            dve.memset(z[:, 0:1], 0.0).then_inc(z_edges, 1)
            dve.memset(z[:, S + 1:S + 2], 0.0).then_inc(z_edges, 1)
            dve.wait_ge(z_edges, 2)
            dve.wait_ge(small_loaded, 16 * 14)
            step = Chain(dve, conv_step)

            def conv_tile(ct, i):
                step.at((ct + i) * 3)
                for h in range(HT):
                    n = HT * (ct + i) + h
                    dve.wait_ge(g_copied, 2 * n + 1)
                    dve.tensor_tensor(z[:, 1 + h * BANK:1 + (h + 1) * BANK], gc[:, h, :],
                                      c.ps[:, 3 * h + 2, :], ALU.mult).then_inc(z_half, 1)
                dve.wait_ge(z_half, HT * (ct + i) + HT)
                tap = taps[:, bass.ds(ct + i, 1), :].rearrange("p a j -> p (a j)")
                step.sync(dve.tensor_scalar(acc, z[:, 0:S], tap[:, 0:1], None, ALU.mult))
                step.sync(dve.scalar_tensor_tensor(out=acc, in0=z[:, 1:S + 1], scalar=tap[:, 1:2], in1=acc,
                                                   op0=ALU.mult, op1=ALU.add))
                step.sync(dve.scalar_tensor_tensor(out=acc, in0=z[:, 2:S + 2], scalar=tap[:, 2:3], in1=acc,
                                                   op0=ALU.mult, op1=ALU.add))
                dve.wait_ge(g_copied, 2 * HT * (ct + i + 1))
                dve.tensor_tensor(yT[:, bass.ds(ct + i, 1), :].rearrange("p a s -> p (a s)"), acc, gb,
                                  ALU.mult).then_inc(y_ready, 1)
                dve.wait_ge(y_ready, ct + i + 1)

            with dve.Fori(0, KD // 2) as pair:
                ct = pair * 2
                for i in range(2):
                    conv_tile(ct, i)

            out_projection.dve_program(dve)

        @block.tensor
        def _(pe):
            pe.wait_ge(consts, N_CONST)
            for t in range(NT // 2):
                norm0.pe_turn(pe, t)

            turn_before = {(0, 4): 4, (1, 2): 5, (1, 7): 6, (2, 4): 7}

            def multiply(ct):
                for h in range(HT):
                    n = HT * ct + h
                    wait(pe, z_half, n - 1)
                    wait(pe, g_copied, 2 * (n - 1))
                    if isinstance(n, int) and n < HT:
                        pe.wait_ge(norm0.evacuated, 2 * NT // HT * (n + 1))
                    for j in range(3):
                        if h == 0:
                            pe.wait_ge(w_low_ready, 3 * ct + j + 1)
                        for k in range(KD):
                            if isinstance(n, int) and n == 0 and (j, k) in turn_before:
                                norm0.pe_turn(pe, turn_before[j, k])
                            for a, b in PARTS:
                                last = pe.matmul(c.ps[:, 3 * h + j, :], w_split[:, j, a, k, :],
                                                 hT_split[:, b, k, h * BANK:(h + 1) * BANK],
                                                 start=(k == 0 and a == b), stop=(k == KD - 1 and a == LOW))
                        if h == 1 and j < 2:
                            last.then_inc(unit_used[j], 1)
                    last.then_inc(products, 1)

            multiply(0)
            multiply(1)
            with pe.Fori(1, KD // 2) as pair:
                for i in range(2):
                    multiply(pair * 2 + i)
            pe.wait_ge(z_half, HT * KD - 1)
            pe.wait_ge(g_copied, 2 * (HT * KD - 1))
            pe.wait_ge(y_ready, KD - 1)
            pe.wait_ge(small_loaded, 16 * 14)
            out_projection.pe_program(pe, lambda: pe.wait_ge(y_ready, KD))

    sems.clear()


class LatentPlaces:

    def __init__(self, c):
        piece = c.carve(c.arena[:, LATENT_AT:c.arena_words])
        self.w_lat = piece(KD, LAT)
        self.rope_gain = piece(2, ROPE)
        self.piece = piece
        piece = c.carve(c.turned[:, :, :, :].rearrange("p a k m -> p (a k m)"))
        self.lat_gain = piece(KQ + KKV)
        self.qk_gain = piece(4)
        self.piece_t = piece

    def load(self, sp, c, loaded):
        ins = c.ins
        sp.dma_start(self.w_lat, ins["mla_w_down"][0].rearrange("(k p) m -> p k m", p=P)).then_inc(loaded, 16)
        sp.dma_start(c.pos_i[:, :], ins["positions"][0].rearrange("(t p) -> p t", p=P)).then_inc(loaded, 16)
        sp.dma_start(self.lat_gain[:, 0:KQ], ins["mla_q_lat_norm"][0].rearrange("(k p) -> p k", p=P)).then_inc(loaded, 16)
        sp.dma_start(self.lat_gain[:, KQ:KQ + KKV],
                     ins["mla_kv_lat_norm"][0].rearrange("(k p) -> p k", p=P)).then_inc(loaded, 16)
        for i, name in enumerate(("mla_q_head_norm", "mla_k_head_norm")):
            sp.dma_start(self.qk_gain[:, 2 * i:2 * i + 1], ins[name][0, 0:NOPE].rearrange("(p a) -> p a", a=1)).then_inc(loaded, 16)
            sp.dma_start(self.rope_gain[:, i, :], ins[name][0, NOPE:QD].partition_broadcast(P)).then_inc(loaded, 16)
        load_router(sp, c, 1, loaded)
        sp.wait_ge(loaded, 16 * 12)


def moe_phase(c, layer, last, experts):
    nc, ins = c.nc, c.ins
    sems = Sems(nc, f"moe{layer}")
    piece, w_gate, w_up, w_down = experts.piece, experts.gate, experts.up, experts.down
    assert LATENT_AT + KD * LAT <= piece.at[0]
    gathered = piece(2, BANK)
    xT = piece(2, 4, 2, RANKS)
    gate_up = piece(2, FF)
    silu = piece(2, KF, RANKS)
    hidden = piece(2, KF, RANKS)
    y = piece(2, BANK)
    rank = piece(2, NT)
    gates = piece(2, NT)
    idx_f = piece(4, NE)
    tiny = piece(16, NT)
    piece = c.carve(c.hT[:, :, :].rearrange("p k s -> p (k s)"))
    onehot = c.typed(f"onehot{layer}", 0, [P, 2 * NT, P], BF16, c.hT_at)
    piece(NT * P)
    by_rank = piece(2 * NT * NE)
    by_pick = piece(2, NT, EG)
    chosen, coded, earlier = c.chosen, c.coded, c.earlier
    Y_RING = 6
    y_pair = c.arena[:, 0:Y_RING * 2 * D].rearrange("p (r k d) -> p r k d", r=Y_RING, k=2)

    gather_idx, scatter_idx, col_idx, n_rounds = c.gather_idx, c.scatter_idx, c.col_idx, c.n_rounds
    cleared = sems("cleared")
    w_gate_up_loaded, w_down_loaded = experts.gate_up_loaded, experts.down_loaded
    route_step = sems("route_step")
    exp_out = sems("exp_out")
    counted = sems("counted")
    rounds_ready = sems("rounds_ready")
    onehot_ready = sems("onehot_ready")
    idx_products = sems("idx_products")
    idx_ready = sems("idx_ready")
    round_step = sems("round_step")
    pool_step = sems("pool_step")
    rounds_begun = sems("rounds_begun")
    gathers_begun = sems("gathers_begun")
    scatters_begun = sems("scatters_begun")
    gather_done = [sems(f"gather_done{i}") for i in range(2)]
    y_stored = sems("y_stored")
    scatter_done = [sems(f"scatter_done{i}") for i in range(2)]
    x_turned = sems("x_turned")
    xT_ready = sems("xT_ready")
    gate_up_products = sems("gate_up_products")
    gate_up_copied = sems("gate_up_copied")
    h_turned = sems("h_turned")
    silu_ready = sems("silu_ready")
    hidden_ready = sems("hidden_ready")
    y_products = sems("y_products")
    y_copied = sems("y_copied")
    y_pair_loaded = [sems(f"y_pair_loaded{i}") for i in range(Y_RING)]
    gates_ready = sems("gates_ready")
    latents_loaded = sems("latents_loaded")
    first_scaled = sems("first_scaled")
    summed = sems("summed")
    x_added = sems("x_added")
    stored = sems("stored")
    norm = None if last else Norm(c, sems, 2, False, (0, 1))

    def done(g):
        return g + 1 + AHEAD

    def free(g):
        return g + 1

    h_halves = c.h_rows.rearrange("t (h d) -> (t h) d", h=2)
    y_halves = c.y_rows.rearrange("t (h d) -> (t h) d", h=2)

    def rounds(eng):
        eng.wait_ge(rounds_ready, 1)
        return eng.value_load(n_rounds[0:1, 0:1], min_val=1, max_val=MAXR)

    with nc.Block() as block:

        @block.sync
        def _(sp):
            count = rounds(sp)
            with sp.Fori(1, count * (NE // 2)) as pair:
                g = pair * 2
                for slot in range(2):
                    e = (g + slot) % NE
                    sp.wait_ge(gate_up_products, g + slot + free(0))
                    experts.load_gate_up(sp, slot, e)
                    sp.wait_ge(y_products, g + slot + free(0))
                    experts.load_down(sp, slot, e)
            sp.wait_ge(y_stored, count * NE + AHEAD)
            for t in range(NT):
                if t >= Y_RING:
                    sp.wait_ge(x_added, t - Y_RING + 1)
                src = c.y_rows.rearrange("(k t p) d -> t p k d", k=2, p=P)[t]
                sp.dma_start(y_pair[:, t % Y_RING, :, :], src).then_inc(y_pair_loaded[t % Y_RING], 16)
            if not last:
                LatentPlaces(c).load(sp, c, latents_loaded)
            if last:
                for t in range(NT):
                    sp.wait_ge(x_added, t + 1)
                    sp.dma_start(c.out[0, t * P:(t + 1) * P, :], c.x[:, t, :]).then_inc(stored, 16)
                sp.wait_ge(stored, 16 * NT)

        @block.gpsimd
        def _(pool):
            pool.memset(gathered, 0.0).then_inc(cleared, 1)
            pool.sem_inc(y_stored, AHEAD)
            pool.wait_ge(cleared, 1)
            count = rounds(pool)
            step = Chain(pool, pool_step)

            def gather(g, e, slot, n):
                pool.wait_ge(x_turned, g + free(0))
                pool.sem_inc(gathers_begun, 1)
                pool.tensor_copy(col_idx[:, slot, :], gather_idx[:, bass.ds(e, 1)]).then_inc(pool_step, 1)
                pool.wait_ge(pool_step, n + 1)
                pool.sem_inc(gathers_begun, 1)
                pool.indirect_dma_start(gathered[:, slot, :], None, h_halves,
                                        bass.IndirectOffsetOnAxis(ap=col_idx[:, slot, :], axis=0),
                                        bounds_check=2 * S - 1, oob_is_err=False).then_inc(gather_done[slot], 16)

            def scatter(g, e, slot, n):
                pool.wait_ge(y_copied, g + done(0))
                pool.sem_inc(scatters_begun, 1)
                pool.tensor_copy(col_idx[:, 2 + slot, :], scatter_idx[:, bass.ds(e, 1)]).then_inc(pool_step, 1)
                pool.wait_ge(pool_step, n + 1)
                pool.sem_inc(scatters_begun, 1)
                pool.indirect_dma_start(y_halves, bass.IndirectOffsetOnAxis(ap=col_idx[:, 2 + slot, :], axis=0),
                                        y[:, slot, :], None,
                                        bounds_check=4 * S - 1, oob_is_err=False).then_inc(scatter_done[slot], 16)

            def complete(g, slot):
                pool.wait_ge(scatter_done[slot], g * 8 + (16 - 8 * slot))
                pool.sem_inc(y_stored, 1)

            with pool.Fori(0, count) as r:
                pool.wait_ge(idx_ready, 2 * r + 2)
                pool.sem_inc(rounds_begun, 1)
                g0, n0 = r * NE, r * (2 * NE)
                for e in range(4):
                    gather(g0 + e, e, e % 2, n0 + e)
                scatter(g0, 0, 0, n0 + 4)
                with pool.Fori(2, NE // 2) as pair:
                    for slot in range(2):
                        e = pair * 2 + slot
                        gather(g0 + e, e, slot, n0 + 2 * e - 3)
                        complete(g0 + e - 4, slot)
                        scatter(g0 + e - 3, e - 3, 1 - slot, n0 + 2 * e - 2)
                for e in range(NE - 3, NE):
                    complete(g0 + e - 1, (e - 1) % 2)
                    scatter(g0 + e, e, e % 2, n0 + e + NE)
                complete(g0 + NE - 1, 1)
            if norm:
                for t in range(NT):
                    norm.pool_rstd(pool, t)

        @block.scalar
        def _(act):
            act.activation(c.exps[:, :, :, :], c.exps[:, :, :, :], ACT.Exp).then_inc(exp_out, 1)
            for s in (gate_up_copied, silu_ready, y_copied):
                act.sem_inc(s, AHEAD)
            count = rounds(act)

            def copy_gate_up(g, slot):
                act.wait_ge(gate_up_products, g + done(0))
                act.wait_ge(h_turned, g + free(0))
                act.activation(gate_up[:, slot, :], c.ps[:, 2 + slot, 0:FF], ACT.Copy).then_inc(gate_up_copied, 1)

            def make_silu(g, slot):
                act.wait_ge(h_turned, g + done(0))
                act.wait_ge(hidden_ready, g + free(0))
                turned = c.ps[:, 4 + slot, 0:FF].rearrange("p (j m) -> p j m", m=P)
                act.activation(silu[:, slot, :, :], turned[:, :, 0:RANKS], ACT.Silu).then_inc(silu_ready, 1)

            def copy_y(g, slot):
                act.wait_ge(y_products, g + done(0))
                act.wait_ge(y_stored, g + free(0))
                act.activation(y[:, slot, :], c.ps[:, 6 + slot, :], ACT.Copy).then_inc(y_copied, 1)

            def expert(g, slot):
                copy_gate_up(g, slot)
                copy_y(g - 1, 1 - slot)
                make_silu(g, slot)

            with act.Fori(0, count) as r:
                g0 = r * NE
                copy_gate_up(g0, 0)
                make_silu(g0, 0)
                with act.Fori(0, NE // 2 - 1) as pair:
                    for n in (1, 2):
                        expert(g0 + pair * 2 + n, n % 2)
                expert(g0 + NE - 1, 1)
                copy_y(g0 + NE - 1, 1)

            act.wait_ge(gates_ready, 1)
            for t in range(NT + (2 if norm else 0)):
                if t < NT:
                    act.wait_ge(y_pair_loaded[t % Y_RING], 16 * (t // Y_RING + 1))
                    first = y_pair[:, t % Y_RING, 0, :]
                    act.activation(first, first, ACT.Copy, scale=gates[:, 0, t:t + 1]).then_inc(first_scaled, 1)
                if norm and 1 <= t < NT + 1:
                    act.wait_ge(x_added, t)
                    norm.act_squares(act, t - 1)
                if norm and t >= 2:
                    norm.act_rows(act, t - 2)

        @block.vector
        def _(dve):
            for s in (xT_ready, hidden_ready):
                dve.sem_inc(s, AHEAD)
            step = Chain(dve, route_step)
            t_ = [tiny[:, i, :] for i in range(16)]

            def tt(out, a, b, op):
                step.sync(dve.tensor_tensor(out, a, b, op))

            def red(out, a, op):
                step.sync(dve.tensor_reduce(out, a, X, op))

            tok_counts = c.ps[:, 0, :].rearrange("p (t e) -> p t e", e=NE)
            chosen_counts = by_rank.rearrange("p (k t e) -> p k t e", k=2, e=NE)
            dve.wait_ge(counted, 1)
            tt(chosen_counts, chosen, bc(tok_counts, 1, 2), ALU.mult)
            red(rank, chosen_counts, ALU.add)
            dve.wait_ge(counted, 2)
            red(t_[0][:, 0:1], c.ps[:, 1, 0:NE], ALU.max)
            step.sync(dve.tensor_scalar(idx_f[:, 0, 0:MAXR], c.round_start[:, :], t_[0][:, 0:1], None, ALU.is_lt))
            red(t_[0][:, 1:2], idx_f[:, 0, 0:MAXR], ALU.add)
            dve.tensor_copy(n_rounds[:, :], t_[0][:, 1:2]).then_inc(rounds_ready, 1)

            def make_gates():
                group, first, second = (c.picked[:, i, :, :] for i in range(3))
                of_group, of_expert = c.exps[:, 0, :, :], c.exps[:, 1, :, :]
                dve.wait_ge(exp_out, 1)
                for i, (e, pick) in enumerate(((of_group, group), (of_expert, first), (of_expert, second))):
                    tt(by_pick[:, 0, :, :], e, pick, ALU.mult)
                    red(t_[1 + i], by_pick[:, 0, :, :], ALU.add)
                for i, e in enumerate((of_group, of_expert)):
                    red(t_[4], e, ALU.add)
                    step.sync(dve.reciprocal(t_[5 + i], t_[4]))
                for i, total in enumerate((5, 6, 6)):
                    tt(t_[7 + i], t_[1 + i], t_[total], ALU.mult)
                tt(t_[10], t_[8], t_[9], ALU.add)
                step.sync(dve.reciprocal(t_[11], t_[10]))
                for k in range(2):
                    tt(t_[12], t_[8 + k], t_[11], ALU.mult)
                    tt(gates[:, k, :], t_[12], t_[7], ALU.mult)

            count = rounds(dve)

            PER_ROUND = 8

            def expert_x(g, slot):
                dve.wait_ge(x_turned, g + done(0))
                dve.wait_ge(gate_up_products, g + free(0))
                dve.tensor_tensor(xT[:, slot, :, :, :].rearrange("p j h m -> p (j h) m"),
                                  c.ps[:, slot, :].rearrange("p (a m) -> p a m", m=RANKS),
                                  bc(c.xw[:, layer, :, :].rearrange("p j h -> p (j h)"), 2, RANKS),
                                  ALU.mult).then_inc(xT_ready, 1)

            def expert_h(g, slot):
                dve.wait_ge(silu_ready, g + done(0))
                dve.wait_ge(y_products, g + free(0))
                turned = c.ps[:, 4 + slot, 0:FF].rearrange("p (j m) -> p j m", m=P)
                dve.tensor_tensor(hidden[:, slot, :, :], silu[:, slot, :, :], turned[:, :, RANKS:P],
                                  ALU.mult).then_inc(hidden_ready, 1)

            with dve.Fori(0, count) as r:
                in_round = Chain(dve, round_step)
                in_round.at(r * PER_ROUND)
                dve.wait_ge(idx_products, r + 1)
                rank_all = rank.rearrange("p k t -> p (k t)")
                dve.tensor_tensor(onehot, bc(rank_all, 2, P),
                                  bc(c.rank_of_col[:, :, :].rearrange("p a b -> p (a b)"), 1, 2 * NT),
                                  ALU.is_equal).then_inc(onehot_ready, 1)
                dve.wait_ge(onehot_ready, r + 1)
                in_round.mark(dve.tensor_scalar(rank_all, rank_all, -float(RANKS), None, ALU.add))
                dve.wait_ge(idx_products, r + 2)
                in_round.sync(dve.tensor_copy(idx_f[:, 1, :], c.ps[:, 0, NE:2 * NE]))
                in_round.sync(dve.scalar_tensor_tensor(out=idx_f[:, 0, :], in0=c.ps[:, 0, 0:NE], scalar=float(P),
                                                       in1=idx_f[:, 1, :], op0=ALU.mult, op1=ALU.add))
                code = idx_f[:, 0, :]
                in_round.mark(dve.tensor_scalar(idx_f[:, 1, :], code, 2.0, c.upper_half[:, 0:1], ALU.mult, ALU.add))
                in_round.mark(dve.tensor_scalar(idx_f[:, 2, :], code, 0.5, 1e6, ALU.is_lt, ALU.mult))
                in_round.sync(dve.tensor_scalar(idx_f[:, 3, :], code, float(S) + 0.5, -2.0 * S, ALU.is_gt, ALU.mult))
                in_round.sync(dve.tensor_tensor(idx_f[:, 1, :], idx_f[:, 1, :], idx_f[:, 2, :], ALU.add))
                in_round.sync(dve.tensor_tensor(idx_f[:, 3, :], idx_f[:, 1, :], idx_f[:, 3, :], ALU.add))
                assert in_round.n == PER_ROUND
                dve.wait_ge(y_stored, r * NE + AHEAD)
                dve.tensor_copy(gather_idx[:, :], idx_f[:, 3, :]).then_inc(idx_ready, 1)
                dve.tensor_copy(scatter_idx[:, :], idx_f[:, 1, :]).then_inc(idx_ready, 1)
                g0 = r * NE
                expert_x(g0, 0)
                with dve.Fori(0, NE // 2 - 1) as pair:
                    e = pair * 2
                    for slot in range(2):
                        expert_x(g0 + e + slot + 1, 1 - slot)
                        expert_h(g0 + e + slot, slot)
                expert_x(g0 + NE - 1, 1)
                expert_h(g0 + NE - 2, 0)
                expert_h(g0 + NE - 1, 1)

            make_gates()
            dve.sem_inc(gates_ready, 1)

            def combine(t):
                dve.wait_ge(first_scaled, t + 1)
                y0, y1 = y_pair[:, t % Y_RING, 0, :], y_pair[:, t % Y_RING, 1, :]
                dve.scalar_tensor_tensor(out=y0, in0=y1, scalar=gates[:, 1, t:t + 1], in1=y0,
                                         op0=ALU.mult, op1=ALU.add).then_inc(summed, 1)
                dve.wait_ge(summed, t + 1)
                dve.tensor_tensor(c.x[:, t, :], c.x[:, t, :], y0, ALU.add).then_inc(x_added, 1)

            for t in range(NT + (3 if norm else 0)):
                if t < NT:
                    combine(t)
                if norm and 1 <= t < NT + 1:
                    norm.dve_var(dve, t - 1)
                if norm and t >= 3:
                    norm.dve_evacuate(dve, t - 3)

        @block.tensor
        def _(pe):
            for s in (x_turned, gate_up_products, h_turned, y_products):
                pe.sem_inc(s, AHEAD)
            pe.sem_inc(idx_products, 1)
            tok = c.ps[:, 0, :]
            pe.matmul(tok, c.before[:, :], c.both[:, :, :].rearrange("p t e -> p (t e)"), start=True, stop=False)
            pe.matmul(tok, c.ones[:, :], earlier[:, 0:NT, :].rearrange("p t e -> p (t e)"),
                      start=False, stop=True).then_inc(counted, 1)
            pe.matmul(c.ps[:, 1, 0:NE], c.ones[:, :], earlier[:, NT, :], start=True, stop=True).then_inc(counted, 1)
            count = rounds(pe)
            pe.wait_ge(cleared, 1)

            def turn_x(g, slot):
                pe.wait_ge(gather_done[slot], g * 8 + (16 - 8 * slot))
                pe.wait_ge(xT_ready, g + free(0))
                rows = gathered[:, slot, :].rearrange("p (m j) -> p j m", j=4)
                for j in range(4):
                    last_ = pe.transpose(c.ps[:, slot, j * P:(j + 1) * P], rows[:, j, :], c.ident[:, :])
                last_.then_inc(x_turned, 1)

            def gate_and_up(g, slot):
                pe.wait_ge(xT_ready, g + done(0))
                pe.wait_ge(w_gate_up_loaded[slot], g * 16 + (32 - 16 * slot))
                pe.wait_ge(gate_up_copied, g + free(0))
                for half in range(2):
                    for j in range(4):
                        for row, w in ((0, w_gate), (RANKS, w_up)):
                            last_ = pe.matmul(c.ps[row:row + RANKS, 2 + slot, 0:FF], xT[:, slot, j, half, :],
                                              w[:, slot, half, j * FF:(j + 1) * FF],
                                              start=(half + j == 0), stop=(half == 1 and j == 3))
                last_.then_inc(gate_up_products, 1)

            def turn_h(g, slot):
                pe.wait_ge(gate_up_copied, g + done(0))
                pe.wait_ge(hidden_ready, g + free(0))
                for j in range(KF):
                    last_ = pe.transpose(c.ps[:, 4 + slot, j * P:(j + 1) * P],
                                         gate_up[:, slot, j * P:(j + 1) * P], c.ident[:, :])
                last_.then_inc(h_turned, 1)

            def down(g, slot):
                pe.wait_ge(hidden_ready, g + done(0))
                pe.wait_ge(w_down_loaded[slot], g * 8 + (16 - 8 * slot))
                pe.wait_ge(y_copied, g + free(0))
                for j in range(KF):
                    for half in range(2):
                        last_ = pe.matmul(c.ps[half * RANKS:(half + 1) * RANKS, 6 + slot, :], hidden[:, slot, j, :],
                                          w_down[:, slot, j, half * BANK:(half + 1) * BANK],
                                          start=(j == 0), stop=(j == KF - 1))
                last_.then_inc(y_products, 1)

            with pe.Fori(0, count) as r:
                pe.wait_ge(onehot_ready, r + 1)
                for n in range(2 * NT):
                    last_ = pe.matmul(c.ps[:, 0, 0:2 * NE], onehot[:, n, :],
                                      coded[:, n // NT, n % NT, :, :].rearrange("p a e -> p (a e)"),
                                      start=(n == 0), stop=(n == 2 * NT - 1))
                last_.then_inc(idx_products, 1)
                g0 = r * NE
                turn_x(g0, 0)
                gate_and_up(g0, 0)
                turn_x(g0 + 1, 1)
                turn_h(g0, 0)
                with pe.Fori(0, NE // 2 - 1) as pair:
                    for n in (1, 2):
                        g, slot = g0 + pair * 2 + n, n % 2
                        gate_and_up(g, slot)
                        turn_x(g + 1, 1 - slot)
                        down(g - 1, 1 - slot)
                        turn_h(g, slot)
                gate_and_up(g0 + NE - 1, 1)
                down(g0 + NE - 2, 0)
                turn_h(g0 + NE - 1, 1)
                down(g0 + NE - 1, 1)
            if norm:
                for t in range(NT):
                    norm.pe_turn(pe, t)

    sems.all += experts.sems.all
    sems.clear()


def attention_phase(c, experts):
    nc, ins = c.nc, c.ins
    sems = Sems(nc, "mla")
    piece = c.carve(c.whole_arena)
    latT = piece(KQ + KKV, S)
    w_q = piece(2, KQ, QD)
    w_kv = piece(2, KKV, NOPE + VD)
    heads_at = (KQ + KKV) * S + 2 * (KQ * QD + KKV * (NOPE + VD))
    K_SETS = 3
    k_split = c.typed("k_split", heads_at, [P, 2, K_SETS, S], F32R)
    q_split = c.typed("q_split", heads_at + 2 * K_SETS * S, [P, 2, 2, S], F32R)
    piece = c.carve(c.whole_arena[:, heads_at + (2 * K_SETS + 4) * S:])
    v = piece(2, NT, VD)
    probsT = piece(2, NT, 2 * P)
    places = LatentPlaces(c)
    piece_t, w_lat, rope_gain = places.piece_t, places.w_lat, places.rope_gain
    lat_gain, qk_gain = places.lat_gain, places.qk_gain
    piece_r = c.carve(c.rows[:, 2:4, :].rearrange("p a d -> p (a d)"))
    k_rope = piece_t(NT, ROPE)
    cos_q = piece_t(NT, ROPE)
    sin_q = piece_t(NT, ROPE)
    q_k_rows = piece_r(2, 4, P)
    raw = piece_r(2, QD + NOPE + VD)
    junk = (piece_t(QD + NOPE), c.logits[:, :, :].rearrange("p t n -> p (t n)")[:, 0:QD + NOPE])
    rot = piece(3, ROPE)
    head_sumsq = piece_t(2, 2)
    head_sum2 = piece_t(2, 2)
    head_var = piece_t(2, 2)
    head_rstd = piece_t(2, 2)
    k_rope_sumsq = piece_t(NT, 2)
    row_max = piece_t(2, 1)
    minus_max = piece_t(2, 1)
    row_sum = piece_t(2, 1)
    row_rec = piece_t(2, 1)
    lat_sumsq = piece_t(NT, 2)
    lat_var = piece_t(NT, 2)
    lat_rstd = piece_t(NT, 2)
    early_piece = places.piece
    lat_rows = early_piece(2, QL + KVL)
    k_raw = early_piece(NT, ROPE)
    lat_junk = early_piece(2, QL + KVL)
    pos_f = early_piece(NT)
    inv_freq = early_piece(ROPE // 2)
    angle = early_piece(NT, ROPE // 2)
    turns_ = early_piece(NT, ROPE // 2)
    sine = early_piece(NT, ROPE // 2)
    cosine = early_piece(NT, ROPE // 2)
    k_tmp = early_piece(NT, ROPE)
    k_tmp2 = early_piece(NT, ROPE)
    w_out = c.arena[:, 0:KD * D].rearrange("p (h k d) -> p h k d", h=2, k=KD)
    w_out_high = c.typed("mla_w_out_high", KD * D, [P, 2, KD, BANK], F32R)
    w_out_low = c.typed("mla_w_out_low", 2 * KD * D, [P, 2, KD, BANK], F32R)
    y_split = c.typed("mla_y_split", 0, [P, 2, 2, KD, P], F32R)
    probs = c.rows
    oT = c.hT
    HR = ROPE // 2
    SCALE = float(QD) ** -0.5

    head_w_loaded = [sems(f"head_w_loaded{i}") for i in range(2)]
    freq_set = sems("freq_set")
    trig_step = sems("trig_step")
    sin_in = sems("sin_in")
    sin_out = sems("sin_out")
    lat_products = sems("lat_products")
    lat_squares = sems("lat_squares")
    lat_step = sems("lat_step")
    lat_var_ready = sems("lat_var_ready")
    lat_rstd_ready = sems("lat_rstd_ready")
    lat_scaled = sems("lat_scaled")
    lat_turned = sems("lat_turned")
    latT_ready = sems("latT_ready")
    k_rope_ready = sems("k_rope_ready")
    up_products = sems("up_products")
    raw_copied = sems("raw_copied")
    head_squares = sems("head_squares")
    head_step = sems("head_step")
    head_var_ready = sems("head_var_ready")
    head_rstd_ready = sems("head_rstd_ready")
    rows_normed = sems("rows_normed")
    rot_step = sems("rot_step")
    rows_ready = sems("rows_ready")
    v_copied = sems("v_copied")
    heads_begun = sems("heads_begun")
    qk_turned = sems("qk_turned")
    qkT_ready = sems("qkT_ready")
    qk_high_ready = sems("qk_high_ready")
    scores = sems("scores")
    max_found = sems("max_found")
    bias_ready = sems("bias_ready")
    exps = sems("exps")
    rec_ready = sems("rec_ready")
    probs_ready = sems("probs_ready")
    probs_turned = [sems(f"probs_turned{g}") for g in range(2)]
    probsT_ready = [sems(f"probsT_ready{g}") for g in range(2)]
    pair_products = sems("pair_products")
    pair_copied = sems("pair_copied")
    norm = Norm(c, sems, 3, True, (5, 6), logit_bank=7)
    out_projection = OutProjection(c, sems, norm, ins["mla_w_out"][0], oT, w_out, w_out_high, w_out_low, y_split,
                                   experts)

    freqs = (10000.0 ** (-np.arange(0, ROPE, 2) / ROPE)).astype(np.float32)
    TWO_PI = 2 * np.pi
    PI_A = float(np.float32(6.28125))
    PI_B = float(np.float32(np.round((TWO_PI - PI_A) * 2**22) / 2**22))
    PI_C = float(np.float32(TWO_PI - PI_A - PI_B))
    ROUND = 1.5 * 2.0**23
    PI_MAX = float(np.nextafter(np.float32(np.pi), np.float32(0)))

    LAST = NH - 1
    PROB_BANKS = ((5, 6), (6, 5))

    with nc.Block() as block:

        @block.sync
        def _(sp):

            def load_head(h, slot):
                w = ins["mla_w_q_up"][0].rearrange("(k p) (h m) -> p k h m", p=P, h=NH)
                sp.dma_start(w_q[:, slot, :, :], w[:, :, bass.ds(h, 1), :].rearrange("p k a m -> p (k a) m")
                             ).then_inc(head_w_loaded[slot], 16)
                w = ins["mla_w_kv_up"][0].rearrange("(k p) (h m) -> p k h m", p=P, h=NH)
                sp.dma_start(w_kv[:, slot, :, :], w[:, :, bass.ds(h, 1), :].rearrange("p k a m -> p (k a) m")
                             ).then_inc(head_w_loaded[slot], 16)

            load_head(0, 0)
            load_head(1, 1)
            with sp.Fori(1, NH // 2) as pair:
                for slot in range(2):
                    sp.wait_ge(up_products, NT * (2 * pair + slot - 1))
                    load_head(2 * pair + slot, slot)
            sp.wait_ge(up_products, NH * NT)
            out_projection.sp_load(sp)
            out_projection.sp_store_rows(sp)

        @block.gpsimd
        def _(pool):
            for i in range(HR):
                pool.memset(inv_freq[:, i:i + 1], float(freqs[i])).then_inc(freq_set, 1)
            pool.memset(k_rope_sumsq[:, :, 0:1], 0.0).then_inc(freq_set, 1)
            for i in (1, 3):
                pool.memset(qk_gain[:, i:i + 1], 1.0).then_inc(freq_set, 1)
            for t in range(NT):
                pool.wait_ge(lat_var_ready, t + 1)
                pool.tensor_tensor(lat_rstd[:, t, :], lat_var[:, t, :], c.minus_half[:, :], ALU.pow).then_inc(lat_rstd_ready, 1)

            def head_tile(p, h, par, i):
                pool.wait_ge(head_var_ready, p + 1)
                pool.wait_ge(raw_copied, p + 1)
                pool.tensor_tensor(head_rstd[:, i % 2, :], head_var[:, i % 2, :], c.minus_half[:, :],
                                   ALU.pow).then_inc(head_rstd_ready, 1)
                if i == 0:
                    wait(pool, pair_products, 4 * (h - 1))
                    pool.sem_inc(heads_begun, 1)
                pool.tensor_copy(v[:, par, i, :], raw[:, i % 2, QD + NOPE:]).then_inc(v_copied, 1)

            for i in range(NT):
                head_tile(i, 0, 0, i)
            for i in range(NT):
                head_tile(NT + i, 1, 1, i)
            with pool.Fori(1, NH // 2) as pair:
                for par in range(2):
                    for i in range(NT):
                        h = pair * 2 + par
                        head_tile(h * NT + i, h, par, i)
            out_projection.pool_program(pool)

        @block.scalar
        def _(act):
            for i, (src, dst) in enumerate(((angle, sine), (turns_, cosine))):
                act.wait_ge(sin_in, i + 1)
                act.activation(dst, src, ACT.Sin).then_inc(sin_out, 1)
            for t in range(NT + 1):
                if t < NT:
                    act.wait_ge(lat_products, 2 * t + 2)
                    wait(act, lat_var_ready, t - 1)
                    a, b = 2 * (t % 2), 2 * (t % 2) + 1
                    act.activation(lat_junk[:, t % 2, 0:QL], c.ps[:, a, 0:QL], ACT.Square,
                                   accum_out=lat_sumsq[:, t, 0:1]).then_inc(lat_squares, 1)
                    act.activation(lat_junk[:, t % 2, QL:], c.ps[:, b, 0:KVL], ACT.Square,
                                   accum_out=lat_sumsq[:, t, 1:2]).then_inc(lat_squares, 1)
                    act.activation(k_raw[:, t, :], c.ps[:, b, KVL:KVL + ROPE], ACT.Copy).then_inc(lat_scaled, 1)
                if t >= 1:
                    u = t - 1
                    a, b = 2 * (u % 2), 2 * (u % 2) + 1
                    act.wait_ge(lat_rstd_ready, u + 1)
                    wait(act, lat_turned, 2 * (u - 1))
                    act.activation(lat_rows[:, u % 2, 0:QL], c.ps[:, a, 0:QL], ACT.Copy,
                                   scale=lat_rstd[:, u, 0:1]).then_inc(lat_scaled, 1)
                    act.activation(lat_rows[:, u % 2, QL:], c.ps[:, b, 0:KVL], ACT.Copy,
                                   scale=lat_rstd[:, u, 1:2]).then_inc(lat_scaled, 1)

            def squares(p, slot):
                act.wait_ge(up_products, p + 1)
                wait(act, rows_ready, p - 1)
                wait(act, v_copied, p - 1)
                act.activation(junk[slot][:, 0:QD], c.ps[:, 4, 0:QD], ACT.Square,
                               accum_out=head_sumsq[:, slot, 0:1]).then_inc(head_squares, 1)
                act.activation(junk[slot][:, QD:], c.ps[:, 4, QD:QD + NOPE], ACT.Square,
                               accum_out=head_sumsq[:, slot, 1:2]).then_inc(head_squares, 1)
                act.activation(raw[:, slot, :], c.ps[:, 4, 0:QD + NOPE + VD], ACT.Copy).then_inc(raw_copied, 1)

            def exp(s, slot):
                act.wait_ge(bias_ready, s + 1)
                wait(act, probs_turned[1], s - 1)
                act.activation(probs[:, slot, :], c.ps[:, 2 * slot:2 * slot + 2, :].rearrange("p a b -> p (a b)"),
                               ACT.Exp, bias=minus_max[:, slot, :], scale=SCALE,
                               accum_out=row_sum[:, slot, :]).then_inc(exps, 1)

            def divide(s, slot):
                act.wait_ge(rec_ready, s + 1)
                act.activation(probs[:, slot, :], probs[:, slot, :], ACT.Copy,
                               scale=row_rec[:, slot, :]).then_inc(probs_ready, 1)

            def copy_probs(s, i, q):
                for g in range(2):
                    act.wait_ge(probs_turned[g], s + 1)
                    wait(act, pair_products, q - 1)
                    act.activation(probsT[:, (i // 2) % 2, 4 * g:4 * g + 4, (i % 2) * P:(i % 2 + 1) * P],
                                   c.ps[:, PROB_BANKS[i % 2][g], :].rearrange("p (a m) -> p a m", m=P),
                                   ACT.Copy).then_inc(probsT_ready[g], 1)

            def copy_out(q, h, j):
                act.wait_ge(pair_products, q + 1)
                act.activation(oT[:, bass.ds(h, 1), j * 2 * P:(j + 1) * 2 * P].rearrange("p a m -> p (a m)"),
                               c.ps[:, 7, 0:2 * P], ACT.Copy).then_inc(pair_copied, 1)

            def step(h, i, par, first=False, ends=False):
                s = h * NT + i
                if i > 0:
                    exp(s, i % 2)
                if not ends:
                    squares(s + NT, i % 2)
                if i > 0:
                    divide(s, i % 2)
                if not (first and i == 0):
                    copy_probs(s - 1, (i - 1) % NT, 4 * h + (i - 1) // 2)
                if i == 0:
                    exp(s, i % 2)
                    divide(s, i % 2)
                if i % 2 == 1 and not (first and i == 1):
                    copy_out(4 * h + (i - 3) // 2, h if i > 1 else h - 1, ((i - 3) // 2) % 4)

            for p in range(NT):
                squares(p, p % 2)
            for i in range(NT):
                step(0, i, 0, first=True)
            with act.Fori(0, (LAST - 1) // 2) as pair:
                h = pair * 2 + 1
                for par in (1, 0):
                    for i in range(NT):
                        step(h + (1 - par), i, par)
            for i in range(NT):
                step(LAST, i, 1, ends=True)
            n = NH * NT
            copy_probs(n - 1, NT - 1, 4 * NH - 1)
            copy_out(4 * NH - 1, LAST, 3)
            act.wait_ge(pair_products, 4 * NH)
            out_projection.act_program(act)

        @block.vector
        def _(dve):
            trig = Chain(dve, trig_step)
            dve.wait_ge(freq_set, HR + 3)
            trig.sync(dve.tensor_copy(pos_f, c.pos_i[:, :]))
            trig.sync(dve.tensor_tensor(angle, bc(pos_f, 2, HR), bc(inv_freq, 1, NT), ALU.mult))
            trig.sync(dve.tensor_scalar(turns_, angle, 1.0 / TWO_PI, ROUND, ALU.mult, ALU.add))
            trig.sync(dve.tensor_scalar(turns_, turns_, -ROUND, None, ALU.add))
            for part in (PI_A, PI_B, PI_C):
                trig.sync(dve.scalar_tensor_tensor(out=angle, in0=turns_, scalar=-part, in1=angle,
                                                   op0=ALU.mult, op1=ALU.add))
            trig.sync(dve.tensor_scalar(turns_, angle, PI_MAX / 2, -TWO_PI, ALU.is_gt, ALU.mult))
            trig.sync(dve.scalar_tensor_tensor(out=turns_, in0=angle, scalar=TWO_PI / 4, in1=turns_,
                                               op0=ALU.add, op1=ALU.add))
            dve.tensor_scalar(angle, angle, PI_MAX, -PI_MAX, ALU.min, ALU.max).then_inc(sin_in, 1)
            dve.tensor_scalar(turns_, turns_, PI_MAX, -PI_MAX, ALU.min, ALU.max).then_inc(sin_in, 1)

            lat = Chain(dve, lat_step)
            for t in range(NT + 2):
                if t < NT:
                    dve.wait_ge(lat_squares, 2 * t + 2)
                    lat.mark(dve.tensor_scalar(lat_var[:, t, 0:1], lat_sumsq[:, t, 0:1], 1.0 / QL, EPS, ALU.mult, ALU.add))
                    dve.tensor_scalar(lat_var[:, t, 1:2], lat_sumsq[:, t, 1:2], 1.0 / KVL, EPS,
                                      ALU.mult, ALU.add).then_inc(lat_var_ready, 1)
                if t >= 2:
                    u = t - 2
                    for g, (k0, n) in enumerate(((0, KQ), (KQ, KKV))):
                        dve.wait_ge(lat_turned, 2 * u + g + 1)
                        dve.tensor_tensor(latT[:, k0:k0 + n, u * P:(u + 1) * P],
                                          c.ps[:, 5 + g, 0:n * P].rearrange("p (a m) -> p a m", m=P),
                                          bc(lat_gain[:, k0:k0 + n], 2, P), ALU.mult).then_inc(latT_ready, 1)

            dve.wait_ge(sin_out, 2)
            dve.wait_ge(lat_scaled, 3 * NT)

            def tables(cos_w, sin_w, gain):
                g = rope_gain[:, gain, :]
                for half in range(2):
                    a, b = half * HR, (half + 1) * HR
                    o = (1 - half) * HR
                    trig.mark(dve.tensor_tensor(cos_w[:, :, a:b], cosine, bc(g[:, a:b], 1, NT), ALU.mult))
                    trig.mark(dve.scalar_tensor_tensor(out=sin_w[:, :, a:b], in0=sine, scalar=(-1.0, 1.0)[half],
                                                       in1=bc(g[:, o:o + HR], 1, NT), op0=ALU.mult, op1=ALU.mult))

            tables(cos_q, sin_q, 0)
            tables(k_tmp, k_tmp2, 1)
            trig.sync()
            trig.mark(dve.tensor_tensor(k_tmp, k_tmp, k_raw, ALU.mult))
            trig.mark(dve.tensor_tensor(k_tmp2[:, :, 0:HR], k_tmp2[:, :, 0:HR], k_raw[:, :, HR:], ALU.mult))
            trig.sync(dve.tensor_tensor(k_tmp2[:, :, HR:], k_tmp2[:, :, HR:], k_raw[:, :, 0:HR], ALU.mult))
            trig.sync(dve.tensor_tensor(k_rope, k_tmp, k_tmp2, ALU.add))
            trig.sync(dve.tensor_tensor(k_tmp, k_raw, k_raw, ALU.mult))
            trig.sync(dve.tensor_reduce(k_rope_sumsq[:, :, 1], k_tmp, X, ALU.add))

            def find_var(p, slot, i):
                dve.wait_ge(head_squares, 2 * p + 2)
                wait(dve, head_rstd_ready, p - 1)
                dve.tensor_tensor(head_sum2[:, slot, :], head_sumsq[:, slot, :], k_rope_sumsq[:, i, :],
                                  ALU.add).then_inc(head_step, 1)
                dve.wait_ge(head_step, p + 1)
                dve.tensor_scalar(head_var[:, slot, :], head_sum2[:, slot, :], 1.0 / QD, EPS,
                                  ALU.mult, ALU.add).then_inc(head_var_ready, 1)

            def norm_rows(p, slot, i):
                dve.wait_ge(head_rstd_ready, p + 1)
                dve.wait_ge(raw_copied, p + 1)
                wait(dve, qk_turned, p - 1)
                q_row, q_rot, k_row, k_rot = (q_k_rows[:, slot, j, :] for j in range(4))
                rope_in = rot[:, 0, :]
                dve.tensor_scalar(rope_in, raw[:, slot, NOPE:QD], head_rstd[:, slot, 0:1], None,
                                  ALU.mult).then_inc(rows_normed, 1)
                dve.tensor_scalar(q_row, raw[:, slot, 0:NOPE], head_rstd[:, slot, 0:1], None,
                                  ALU.mult).then_inc(rows_normed, 1)
                dve.tensor_scalar(k_row, raw[:, slot, QD:QD + NOPE], head_rstd[:, slot, 1:2], None,
                                  ALU.mult).then_inc(rows_normed, 1)
                dve.tensor_scalar(k_rot.rearrange("p (a m) -> p a m", a=2), bc(k_rope[:, i, :], 1, 2),
                                  head_rstd[:, slot, 1:2], None, ALU.mult).then_inc(rows_normed, 1)
                dve.wait_ge(rows_normed, 4 * p + 4)
                dve.tensor_tensor(rot[:, 1, 0:HR], rope_in[:, HR:], sin_q[:, i, 0:HR], ALU.mult).then_inc(rot_step, 1)
                dve.tensor_tensor(rot[:, 1, HR:], rope_in[:, 0:HR], sin_q[:, i, HR:], ALU.mult).then_inc(rot_step, 1)
                dve.tensor_tensor(rot[:, 2, :], rope_in, cos_q[:, i, :], ALU.mult).then_inc(rot_step, 1)
                dve.wait_ge(rot_step, 3 * p + 3)
                dve.tensor_tensor(q_rot.rearrange("p (a m) -> p a m", a=2), bc(rot[:, 1, :], 1, 2), bc(rot[:, 2, :], 1, 2),
                                  ALU.add).then_inc(rows_ready, 1)
                dve.wait_ge(rows_ready, p + 1)

            def split_qk(p, h, i, bank):
                par, cols = h % 2, slice(i * P, (i + 1) * P)
                turned = c.ps[:, bank, :].rearrange("p (j m) -> p j m", m=P)
                dve.wait_ge(qk_turned, p + 1)
                q_high, k_high = q_split[:, HIGH, :, cols], k_split[:, par, 0:2, cols]
                dve.tensor_tensor(q_high, turned[:, 0:2, :], bc(qk_gain[:, 0:2], 2, P), ALU.mult).then_inc(qk_high_ready, 1)
                dve.tensor_tensor(k_high, turned[:, 2:4, :], bc(qk_gain[:, 2:4], 2, P), ALU.mult).then_inc(qk_high_ready, 1)
                dve.wait_ge(qk_high_ready, 2 * p + 1)
                for j in range(2):
                    dve.scalar_tensor_tensor(out=q_split[:, LOW, j, cols], in0=turned[:, j, :], scalar=qk_gain[:, j:j + 1],
                                             in1=q_high[:, j, :], op0=ALU.mult, op1=ALU.subtract)
                dve.wait_ge(qk_high_ready, 2 * p + 2)
                dve.scalar_tensor_tensor(out=k_split[:, par, 2, cols], in0=turned[:, 2, :], scalar=qk_gain[:, 2:3],
                                         in1=k_high[:, 0, :], op0=ALU.mult, op1=ALU.subtract)
                below = k_high[ROPE:P, 1, :]
                dve.tensor_tensor(below, turned[ROPE:P, 3, :], below, ALU.subtract).then_inc(qkT_ready, 1)

            def find_max(s, slot):
                dve.wait_ge(scores, s + 1)
                dve.tensor_reduce(row_max[:, slot, :], c.ps[:, 2 * slot:2 * slot + 2, :].rearrange("p a b -> p (a b)"),
                                  X, ALU.max).then_inc(max_found, 1)
                dve.wait_ge(max_found, s + 1)
                dve.tensor_scalar(minus_max[:, slot, :], row_max[:, slot, :], -SCALE, None,
                                  ALU.mult).then_inc(bias_ready, 1)

            def invert(s, slot):
                dve.wait_ge(exps, s + 1)
                dve.reciprocal(row_rec[:, slot, :], row_sum[:, slot, :]).then_inc(rec_ready, 1)

            def step(h, i, par, first=False, ends=False):
                s = h * NT + i
                if i == 0:
                    split_qk(s + NT - 1, par, NT - 1, 5)
                    if not ends:
                        find_var(s + NT, 0, 0)
                        norm_rows(s + NT, 0, 0)
                    find_max(s, 0)
                    invert(s, 0)
                    return
                find_max(s, i % 2)
                if not ends:
                    split_qk(s + NT - 1, par + 1, i - 1, 5 + i % 2)
                invert(s, i % 2)
                if not ends:
                    find_var(s + NT, i % 2, i)
                    norm_rows(s + NT, i % 2, i)

            for p in range(NT):
                find_var(p, p % 2, p)
                if p >= 1:
                    split_qk(p - 1, 0, p - 1, 5 + (p - 1) % 2)
                norm_rows(p, p % 2, p)
            for i in range(NT):
                step(0, i, 0, first=True)
            with dve.Fori(0, (LAST - 1) // 2) as pair:
                h = pair * 2 + 1
                for par in (1, 0):
                    for i in range(NT):
                        step(h + (1 - par), i, par)
            for i in range(NT):
                step(LAST, i, 1, ends=True)

            out_projection.dve_program(dve)

        @block.tensor
        def _(pe):
            def turn_latents(t):
                pe.wait_ge(lat_scaled, min(3 * t + 4, 3 * NT))
                for g, (k0, n) in enumerate(((0, KQ), (KQ, KKV))):
                    wait(pe, latT_ready, 2 * t + g - 1)
                    for j in range(n):
                        last = pe.transpose(c.ps[:, 5 + g, j * P:(j + 1) * P],
                                            lat_rows[:, t % 2, (k0 + j) * P:(k0 + j + 1) * P], c.ident[:, :])
                    last.then_inc(lat_turned, 1)

            for t in range(NT + 1):
                if t < NT:
                    wait(pe, lat_scaled, 3 * t - 2 if t >= 2 else 0)
                    a, b = 2 * (t % 2), 2 * (t % 2) + 1
                    for bank, m0, m1 in ((a, 0, QL), (b, QL, LAT)):
                        for k in range(KD):
                            last = pe.matmul(c.ps[:, bank, 0:m1 - m0], c.hT[:, k, t * P:(t + 1) * P],
                                             w_lat[:, k, m0:m1], start=(k == 0), stop=(k == KD - 1))
                        last.then_inc(lat_products, 1)
                if t >= 1:
                    turn_latents(t - 1)

            def up(p, h, i, slot):
                wait(pe, raw_copied, p)
                if i == 0:
                    pe.wait_ge(head_w_loaded[slot], 16 * h + (32 - 16 * slot))
                lat_cols = slice(i * P, (i + 1) * P)
                for k in range(KQ):
                    pe.matmul(c.ps[:, 4, 0:QD], latT[:, k, lat_cols], w_q[:, slot, k, :],
                              start=(k == 0), stop=(k == KQ - 1))
                for k in range(KKV):
                    last = pe.matmul(c.ps[:, 4, QD:QD + NOPE + VD], latT[:, KQ + k, lat_cols], w_kv[:, slot, k, :],
                                     start=(k == 0), stop=(k == KKV - 1))
                last.then_inc(up_products, 1)

            def turn_qk(p, slot, bank):
                pe.wait_ge(rows_ready, p + 1)
                for j in range(4):
                    last = pe.transpose(c.ps[:, bank, j * P:(j + 1) * P], q_k_rows[:, slot, j, :], c.ident[:, :])
                last.then_inc(qk_turned, 1)

            def score(s, h, par, i, slot):
                wait(pe, exps, s - 1)
                if i == 0:
                    pe.wait_ge(qkT_ready, s + NT)
                q = slice(i * P, (i + 1) * P)
                for half in range(2):
                    keys = slice(half * BANK, (half + 1) * BANK)
                    out = c.ps[:, 2 * slot + half, :]
                    for n, (a, b) in enumerate(PARTS):
                        pe.matmul(out, q_split[:, a, 0, q], k_split[:, par, 2 * b, keys], start=(n == 0), stop=False)
                    for a in (HIGH, LOW):
                        last = pe.matmul(out, q_split[:, a, 1, q], k_split[:, par, 1, keys],
                                         start=False, stop=(a == LOW))
                last.then_inc(scores, 1)

            def turn_probs(s, i, n=None):
                pe.wait_ge(probs_ready, s + 1)
                for g in range(2):
                    wait(pe, probsT_ready[1 - g], s)
                    if g == 1:
                        pe.wait_ge(qkT_ready, n)
                    for j in range(4):
                        kt = 4 * g + j
                        last = pe.transpose(c.ps[:, PROB_BANKS[i % 2][g], j * P:(j + 1) * P],
                                            probs[:, i % 2, kt * P:(kt + 1) * P], c.ident[:, :])
                    last.then_inc(probs_turned[g], 1)

            def weigh(q, h, par, j):
                pe.wait_ge(v_copied, NT * h + NT)
                for g in range(2):
                    pe.wait_ge(probsT_ready[g], 2 * q + 2)
                wait(pe, pair_copied, q)
                for kt in range(NT):
                    last = pe.matmul(c.ps[:, 7, 0:2 * P], v[:, par, kt, :], probsT[:, j % 2, kt, :],
                                     start=(kt == 0), stop=(kt == NT - 1))
                last.then_inc(pair_products, 1)

            def step(h, i, par, first=False, ends=False):
                s = h * NT + i

                def turn_last():
                    p = s + NT - 1
                    if first and i == 0:
                        pe.wait_ge(qkT_ready, p)
                    else:
                        wait(pe, probsT_ready[0], s - 1)
                    turn_qk(p, (i + 1) % 2, 5 + i % 2)

                def weigh_pair():
                    weigh(4 * h + (i - 3) // 2, h if i > 1 else h - 1, par if i > 1 else 1 - par, ((i - 3) // 2) % 4)

                if i == 0:
                    turn_last()
                    if not ends:
                        up(s + NT, h + 1, i, 1 - par)
                    if not first:
                        turn_probs(s - 1, NT - 1, s + NT)
                    score(s, h, par, i, i % 2)
                    return
                score(s, h, par, i, i % 2)
                if not ends:
                    turn_last()
                    up(s + NT, h + 1, i, 1 - par)
                if i % 2 == 1 and not (first and i == 1):
                    weigh_pair()
                turn_probs(s - 1, i - 1, NH * NT if ends else s + NT)

            pe.wait_ge(latT_ready, 2 * NT)
            for p in range(NT):
                up(p, 0, p, 0)
                if p >= 1:
                    wait(pe, qkT_ready, p - 2)
                    turn_qk(p - 1, (p - 1) % 2, 5 + (p - 1) % 2)
            for i in range(NT):
                step(0, i, 0, first=True)
            with pe.Fori(0, (LAST - 1) // 2) as pair:
                h = pair * 2 + 1
                for par in (1, 0):
                    for i in range(NT):
                        step(h + (1 - par), i, par)
            for i in range(NT):
                step(LAST, i, 1, ends=True)
            turn_probs(NH * NT - 1, NT - 1, NH * NT)
            weigh(4 * NH - 1, LAST, 1, 3)
            pe.wait_ge(pair_copied, 4 * NH)
            out_projection.pe_program(pe, lambda: None)

    sems.clear()


def build_trunk(nc, ins, out):
    with ExitStack() as ctx:
        ctx.enter_context(nc.allow_non_contiguous_dma(reason="gains of a few KiB, one to a partition"))
        c = Core(nc, ins, out, ctx)
        experts = [ExpertWeights(c, layer) for layer in range(2)]
        conv_phase(c, experts[0])
        moe_phase(c, 0, False, experts[0])
        attention_phase(c, experts[1])
        moe_phase(c, 1, True, experts[1])


NAMES = ["x", "positions", "conv_norm_w", "conv_w_in", "conv_k", "conv_w_out", "mla_norm_w", "mla_w_down",
         "mla_q_lat_norm", "mla_kv_lat_norm", "mla_w_q_up", "mla_w_kv_up", "mla_q_head_norm", "mla_k_head_norm",
         "mla_w_out", "ffn_norm_w", "router_w_group", "router_b_group", "router_w_expert", "router_b_expert",
         "exp_w_gate", "exp_w_up", "exp_w_down"]


def kernel(**inputs):
    import concourse.bacc as bacc
    from concourse.bass_utils import run_bass_kernel_spmd

    nc = bacc.Bacc("TRN2", target_bir_lowering=False, num_devices=1)
    arrays, aps = {}, {}
    for name in NAMES:
        a = np.ascontiguousarray(inputs[name])
        arrays[f"in_{name}"] = a
        aps[name] = nc.dram_tensor(f"in_{name}", a.shape, mybir.dt.from_np(a.dtype), kind="ExternalInput").ap()
    out = nc.dram_tensor("out", inputs["x"].shape, F32, kind="ExternalOutput").ap()
    build_trunk(nc, aps, out)
    result = run_bass_kernel_spmd(nc, [arrays], core_ids=[0])
    return result.results[0]["out"]
```
